# Optimizing a Trainium2 kernel written in Bass

```python
import jax, jax.numpy as jnp
from jax import lax
import numpy as np
import math

D_MODEL = 1024
BATCH = 1
SEQ = 256
DEPTH = 2

N_EVEN = (DEPTH + 1) // 2
N_ODD = DEPTH // 2
NORM_EPS = 1e-6
D_FF = 2816

CONV_WIDTH = D_MODEL // 2
CONV_GROUPS = 8
CONV_TAPS = 3
RWKV_WIDTH = D_MODEL - CONV_WIDTH
RWKV_HEAD = 64
RWKV_HEADS = RWKV_WIDTH // RWKV_HEAD
DECAY_RANK = 32
ICLR_RANK = 32
GATE_RANK = 96
RWKV_GN_EPS = 64e-5
RWKV_SHIFT_COLS = 3 * RWKV_WIDTH + DECAY_RANK + ICLR_RANK + GATE_RANK
EVEN_IN = 3 * CONV_WIDTH + RWKV_SHIFT_COLS
_RWKV_SPLITS = (RWKV_WIDTH, 2 * RWKV_WIDTH, 3 * RWKV_WIDTH,
                3 * RWKV_WIDTH + DECAY_RANK, 3 * RWKV_WIDTH + DECAY_RANK + ICLR_RANK)

MLA_HEADS = 8
Q_RANK = 384
KV_RANK = 256
NOPE_DIM = 128
ROPE_DIM = 64
V_DIM = 128
QK_DIM = NOPE_DIM + ROPE_DIM
ODD_IN = Q_RANK + KV_RANK + ROPE_DIM
ROPE_THETA = 10000.0
Q_BLOCK = 128
ATTN_SCALE = QK_DIM ** -0.5


def _rmsnorm(x, gain, eps=NORM_EPS):
    xf = x.astype(jnp.float32)
    y = xf * lax.rsqrt(jnp.mean(xf * xf, axis=-1, keepdims=True) + eps)
    return (y * gain.astype(jnp.float32)).astype(x.dtype)

def _swiglu(h, w_gate, w_up, w_down):
    return (jax.nn.silu(h @ w_gate) * (h @ w_up)) @ w_down

def _shift(u):
    return jnp.pad(u, ((0, 0), (1, 0), (0, 0)))[:, :-1]

def _short_conv(u, w):
    T = u.shape[1]
    up = jnp.pad(u, ((0, 0), (CONV_TAPS - 1, 0), (0, 0)))
    return sum(up[:, j:j + T] * w[j] for j in range(CONV_TAPS))

def _rwkv7_scan(r, decay, k, v, a_vec, b_vec):
    B, T, H, N = r.shape

    def step(S, inp):
        r_t, w_t, k_t, v_t, a_t, b_t = inp
        Sa = jnp.einsum('bhvk,bhk->bhv', S, a_t)
        S = S * w_t[:, :, None, :] + Sa[..., None] * b_t[:, :, None, :] + v_t[..., None] * k_t[:, :, None, :]
        return S, jnp.einsum('bhvk,bhk->bhv', S, r_t)

    xs = tuple(jnp.moveaxis(t, 1, 0) for t in (r, decay, k, v, a_vec, b_vec))
    S0 = jnp.zeros((B, H, N, N), jnp.float32)
    _, y = lax.scan(step, S0, xs)
    return jnp.moveaxis(y, 0, 1)

def _conv_rwkv_mixer(h, w_in, conv_w, mu_shift, w0, w_up, a0, a_up, g_up,
                     k_k, k_a, r_k, ln_w, ln_b, w_out):
    B, T, _ = h.shape
    f32 = jnp.float32
    p = h @ w_in
    p_conv, p_rwkv = p[..., :3 * CONV_WIDTH], p[..., 3 * CONV_WIDTH:]
    gate_b, gate_c, h_in = jnp.split(p_conv, 3, axis=-1)
    y_conv = gate_b * _short_conv(gate_c * h_in, conv_w)
    p_rwkv = p_rwkv + (_shift(p_rwkv) - p_rwkv) * mu_shift
    r, k, v, dw, da, dg = jnp.split(p_rwkv, _RWKV_SPLITS, axis=-1)
    log_w = -jax.nn.softplus(-(w0 + jnp.tanh(dw) @ w_up).astype(f32)) - 0.5
    decay = jnp.exp(-jnp.exp(log_w))
    a = jax.nn.sigmoid((a0 + da @ a_up).astype(f32))
    g = jax.nn.sigmoid(dg) @ g_up

    def heads(t):
        return t.astype(f32).reshape(B, T, RWKV_HEADS, RWKV_HEAD)

    r_h, v_h, a_h, decay_h = heads(r), heads(v), heads(a), heads(decay)
    kk = heads(k * k_k)
    kk = kk * lax.rsqrt(jnp.maximum(jnp.sum(kk * kk, axis=-1, keepdims=True), 1e-24))
    k_h = heads(k) * (1.0 + (a_h - 1.0) * k_a.astype(f32).reshape(RWKV_HEADS, RWKV_HEAD))
    y = _rwkv7_scan(r_h, decay_h, k_h, v_h, -kk, kk * a_h)
    mu = jnp.mean(y, axis=-1, keepdims=True)
    var = jnp.mean(jnp.square(y - mu), axis=-1, keepdims=True)
    y = (y - mu) * lax.rsqrt(var + RWKV_GN_EPS) * ln_w.astype(f32).reshape(RWKV_HEADS, RWKV_HEAD) \
        + ln_b.astype(f32).reshape(RWKV_HEADS, RWKV_HEAD)
    y = y + jnp.sum(r_h * k_h * r_k.astype(f32), axis=-1, keepdims=True) * v_h
    y_rwkv = y.reshape(B, T, RWKV_WIDTH).astype(h.dtype) * g
    return jnp.concatenate([y_conv, y_rwkv], axis=-1) @ w_out

def _rope(t, cos, sin):
    t1, t2 = t[..., :ROPE_DIM // 2], t[..., ROPE_DIM // 2:]
    return jnp.concatenate([t1 * cos - t2 * sin, t2 * cos + t1 * sin], axis=-1)

def _causal_attention(q, k, v):
    B, T, H, Dk = q.shape
    nb = T // Q_BLOCK
    qb = q.reshape(B, nb, Q_BLOCK, H, Dk).transpose(1, 0, 3, 2, 4)
    kpos = jnp.arange(T)

    def one_block(args):
        qi, i = args
        s = jnp.einsum('bhqd,bkhd->bhqk', qi, k, preferred_element_type=jnp.float32) * ATTN_SCALE
        qpos = i * Q_BLOCK + jnp.arange(Q_BLOCK)
        s = jnp.where(kpos[None, :] <= qpos[:, None], s, jnp.finfo(jnp.float32).min)
        p = jax.nn.softmax(s, axis=-1)
        return jnp.einsum('bhqk,bkhd->bqhd', p.astype(v.dtype), v)

    out = lax.map(one_block, (qb, jnp.arange(nb)))
    return out.transpose(1, 0, 2, 3, 4).reshape(B, T, H, v.shape[-1])

def _mla_mixer(h, cos, sin, w_in, q_a_norm, kv_a_norm, w_q_up, w_kv_up, q_norm, k_norm, w_out):
    B, T, _ = h.shape
    p = h @ w_in
    c_q, c_kv, k_pe = jnp.split(p, (Q_RANK, Q_RANK + KV_RANK), axis=-1)
    q = (_rmsnorm(c_q, q_a_norm) @ w_q_up).reshape(B, T, MLA_HEADS, QK_DIM)
    kv = (_rmsnorm(c_kv, kv_a_norm) @ w_kv_up).reshape(B, T, MLA_HEADS, NOPE_DIM + V_DIM)
    k_nope, v = kv[..., :NOPE_DIM], kv[..., NOPE_DIM:]
    k = jnp.concatenate([k_nope, jnp.broadcast_to(k_pe[:, :, None, :], (B, T, MLA_HEADS, ROPE_DIM))], axis=-1)
    q = _rmsnorm(q, q_norm)
    k = _rmsnorm(k, k_norm)
    q = jnp.concatenate([q[..., :NOPE_DIM], _rope(q[..., NOPE_DIM:], cos, sin)], axis=-1)
    k = jnp.concatenate([k[..., :NOPE_DIM], _rope(k[..., NOPE_DIM:], cos, sin)], axis=-1)
    o = _causal_attention(q, k, v)
    return o.reshape(B, T, MLA_HEADS * V_DIM) @ w_out

def first_inputs(seed: int = 0) -> dict:
    key = jax.random.key(seed)
    ks = iter(jax.random.split(key, 32))
    f32 = jnp.float32

    def nrm(shape, fan_in):
        return jax.random.normal(next(ks), shape, f32) * fan_in ** -0.5

    def gain(shape):
        return 1.0 + 0.02 * jax.random.normal(next(ks), shape, f32)

    def unif(shape, lo, hi):
        return jax.random.uniform(next(ks), shape, f32, lo, hi)

    x = jax.random.normal(next(ks), (BATCH, SEQ, D_MODEL), f32)
    offset = jax.random.randint(next(ks), (BATCH, 1), 0, 1024, jnp.int32)
    positions = (offset + jnp.arange(SEQ, dtype=jnp.int32)[None, :]).astype(jnp.int32)
    return {
        "x": x,
        "positions": positions,
        "norm_gains": gain((DEPTH, 3, D_MODEL)),
        "ffn_w_gate": nrm((DEPTH, 2, D_MODEL, D_FF), D_MODEL),
        "ffn_w_up": nrm((DEPTH, 2, D_MODEL, D_FF), D_MODEL),
        "ffn_w_down": nrm((DEPTH, 2, D_FF, D_MODEL), D_FF),
        "even_w_in": nrm((N_EVEN, D_MODEL, EVEN_IN), D_MODEL),
        "even_conv_w": nrm((N_EVEN, CONV_TAPS, CONV_WIDTH), CONV_TAPS),
        "even_mu_shift": unif((N_EVEN, RWKV_SHIFT_COLS), 0.0, 1.0),
        "rwkv_w0": unif((N_EVEN, RWKV_WIDTH), -6.0, 0.0),
        "rwkv_w_up": nrm((N_EVEN, DECAY_RANK, RWKV_WIDTH), DECAY_RANK),
        "rwkv_a0": 0.1 * jax.random.normal(next(ks), (N_EVEN, RWKV_WIDTH), f32),
        "rwkv_a_up": nrm((N_EVEN, ICLR_RANK, RWKV_WIDTH), ICLR_RANK),
        "rwkv_g_up": nrm((N_EVEN, GATE_RANK, RWKV_WIDTH), GATE_RANK),
        "rwkv_k_k": 0.85 + 0.05 * jax.random.normal(next(ks), (N_EVEN, RWKV_WIDTH), f32),
        "rwkv_k_a": gain((N_EVEN, RWKV_WIDTH)),
        "rwkv_r_k": 0.1 * jax.random.normal(next(ks), (N_EVEN, RWKV_HEADS, RWKV_HEAD), f32),
        "rwkv_ln_w": gain((N_EVEN, RWKV_WIDTH)),
        "rwkv_ln_b": 0.02 * jax.random.normal(next(ks), (N_EVEN, RWKV_WIDTH), f32),
        "even_w_out": nrm((N_EVEN, CONV_WIDTH + RWKV_WIDTH, D_MODEL), CONV_WIDTH + RWKV_WIDTH),
        "odd_w_in": nrm((N_ODD, D_MODEL, ODD_IN), D_MODEL),
        "mla_q_a_norm": gain((N_ODD, Q_RANK)),
        "mla_kv_a_norm": gain((N_ODD, KV_RANK)),
        "mla_w_q_up": nrm((N_ODD, Q_RANK, MLA_HEADS * QK_DIM), Q_RANK),
        "mla_w_kv_up": nrm((N_ODD, KV_RANK, MLA_HEADS * (NOPE_DIM + V_DIM)), KV_RANK),
        "mla_q_norm": gain((N_ODD, QK_DIM)),
        "mla_k_norm": gain((N_ODD, QK_DIM)),
        "odd_w_out": nrm((N_ODD, MLA_HEADS * V_DIM, D_MODEL), MLA_HEADS * V_DIM),
    }

def first_block(x, positions, norm_gains, ffn_w_gate, ffn_w_up, ffn_w_down,
              even_w_in, even_conv_w, even_mu_shift, rwkv_w0, rwkv_w_up, rwkv_a0, rwkv_a_up,
              rwkv_g_up, rwkv_k_k, rwkv_k_a, rwkv_r_k, rwkv_ln_w, rwkv_ln_b, even_w_out,
              odd_w_in, mla_q_a_norm, mla_kv_a_norm, mla_w_q_up, mla_w_kv_up,
              mla_q_norm, mla_k_norm, odd_w_out):
    inv_freq = ROPE_THETA ** (-jnp.arange(0, ROPE_DIM, 2, dtype=jnp.float32) / ROPE_DIM)
    ang = positions.astype(jnp.float32)[..., None] * inv_freq
    cos = jnp.cos(ang)[:, :, None, :].astype(x.dtype)
    sin = jnp.sin(ang)[:, :, None, :].astype(x.dtype)

    for layer in range(DEPTH):
        g = norm_gains[layer]
        x = x + 0.5 * _swiglu(_rmsnorm(x, g[0]), ffn_w_gate[layer, 0], ffn_w_up[layer, 0], ffn_w_down[layer, 0])
        h = _rmsnorm(x, g[1])
        if layer % 2 == 0:
            i = layer // 2
            mix = _conv_rwkv_mixer(h, even_w_in[i], even_conv_w[i], even_mu_shift[i], rwkv_w0[i],
                                   rwkv_w_up[i], rwkv_a0[i], rwkv_a_up[i], rwkv_g_up[i], rwkv_k_k[i],
                                   rwkv_k_a[i], rwkv_r_k[i], rwkv_ln_w[i], rwkv_ln_b[i], even_w_out[i])
        else:
            j = layer // 2
            mix = _mla_mixer(h, cos, sin, odd_w_in[j], mla_q_a_norm[j], mla_kv_a_norm[j], mla_w_q_up[j],
                             mla_w_kv_up[j], mla_q_norm[j], mla_k_norm[j], odd_w_out[j])
        x = x + mix.astype(x.dtype)
        x = x + 0.5 * _swiglu(_rmsnorm(x, g[2]), ffn_w_gate[layer, 1], ffn_w_up[layer, 1], ffn_w_down[layer, 1])
    return x


N_MIXERS = 3
REL_BUCKETS = 32
REL_EXACT = REL_BUCKETS // 2
REL_MAX_DIST = 128
ATTN_HEADS = 16
HEAD_DIM = D_MODEL // ATTN_HEADS
NSA_KV_HEADS = 4
NSA_QPG = ATTN_HEADS // NSA_KV_HEADS
CMP_STRIDE = 16
CMP_LEN = 2 * CMP_STRIDE
CMP_HIDDEN = 2 * HEAD_DIM
SEL_BLOCK = 64
SEL_COUNT = 16
NSA_WINDOW = 512
NSA_QBLOCK = 64
NSA_IN = ATTN_HEADS * HEAD_DIM + 6 * NSA_KV_HEADS * HEAD_DIM + 3 * ATTN_HEADS
HGRN_HEADS = 8
HGRN_KDIM = D_MODEL // HGRN_HEADS
HGRN_VDIM = D_MODEL // HGRN_HEADS
HGRN_CHUNK = 64
SWA_KV_HEADS = 2
SWA_QPG = ATTN_HEADS // SWA_KV_HEADS
SWA_WINDOW = 128
SWA_BLOCK = SWA_WINDOW
SWA_IN = ATTN_HEADS * HEAD_DIM + 2 * SWA_KV_HEADS * HEAD_DIM
LN_EPS = 1e-5
RMS_EPS = 1e-6
NEG_INF = -1e30
N_NSA = len(range(0, DEPTH, N_MIXERS))
N_HGRN = len(range(1, DEPTH, N_MIXERS))
N_SWA = len(range(2, DEPTH, N_MIXERS))


F32 = jnp.float32

def _layer_norm(x, g, b):
    xf = x.astype(F32)
    mu = jnp.mean(xf, axis=-1, keepdims=True)
    xc = xf - mu
    var = jnp.mean(xc * xc, axis=-1, keepdims=True)
    return (xc * lax.rsqrt(var + LN_EPS) * g.astype(F32) + b.astype(F32)).astype(x.dtype)

def _swiglu_2(x, w_gate, w_up, w_down):
    return (jax.nn.silu(x @ w_gate) * (x @ w_up)) @ w_down

def _t5_bucket(dist):
    n = jnp.maximum(dist, 0)
    nf = jnp.maximum(n, 1).astype(F32)
    large = REL_EXACT + (jnp.log(nf / REL_EXACT) / math.log(REL_MAX_DIST / REL_EXACT)
                         * (REL_BUCKETS - REL_EXACT)).astype(jnp.int32)
    return jnp.where(n < REL_EXACT, n, jnp.minimum(large, REL_BUCKETS - 1))

def _rel_bias(table, dist):
    return jnp.moveaxis(table[_t5_bucket(dist)], -1, 0).astype(F32)

def _masked_softmax(logits, valid):
    p = jax.nn.softmax(jnp.where(valid, logits.astype(F32), NEG_INF), axis=-1)
    return jnp.where(valid, p, 0.0)

def _lower_bounds(lb_param):
    sm = jax.nn.softmax(lb_param.astype(F32), axis=0)
    return jnp.cumsum(sm, axis=0) - sm[0]

def _nsa(x, w_in, w_out, cmp_pos, cmp_w1, cmp_w2, rel_bias):
    B, T, _ = x.shape
    dt = x.dtype
    G, Q, Dh = NSA_KV_HEADS, NSA_QPG, HEAD_DIM
    n_cmp = T // CMP_STRIDE - 1
    n_blk = T // SEL_BLOCK
    n_sel = min(SEL_COUNT, n_blk)
    n_qb = T // NSA_QBLOCK
    scale = Dh ** -0.5
    kvw = G * Dh
    h = x @ w_in
    sizes = [ATTN_HEADS * Dh] + [kvw] * 6
    q, k_c, v_c, k_s, v_s, k_w, v_w, gate = jnp.split(h, np.cumsum(sizes).tolist(), axis=-1)

    def heads(z):
        return z.reshape(B, T, G, Dh)

    def compress(z, pos, w1, w2):
        ch = heads(z).reshape(B, T // CMP_STRIDE, CMP_STRIDE, G, Dh)
        blk = jnp.concatenate([ch[:, :-1], ch[:, 1:]], axis=2) + pos[:, None, :]
        hid = jax.nn.gelu(jnp.einsum('bnlgd,lde->bnge', blk, w1))
        return jnp.einsum('bnge,ed->bgnd', hid, w2)

    kc = compress(k_c, cmp_pos[0], cmp_w1[0], cmp_w2[0])
    vc = compress(v_c, cmp_pos[1], cmp_w1[1], cmp_w2[1])
    cmp_end = CMP_STRIDE * jnp.arange(n_cmp, dtype=jnp.int32) + CMP_LEN - 1
    ci = np.arange(n_cmp)[:, None]
    bj = np.arange(n_blk)[None, :]
    overlap = jnp.asarray(((CMP_STRIDE * ci < SEL_BLOCK * (bj + 1)) &
                           (CMP_STRIDE * ci + CMP_LEN > SEL_BLOCK * bj)).astype(np.float32))

    def sel_blocks(z):
        return heads(z).reshape(B, n_blk, SEL_BLOCK, G, Dh).transpose(0, 3, 1, 2, 4)

    ks, vs = sel_blocks(k_s), sel_blocks(v_s)

    def win_keys(z):
        return jnp.pad(heads(z).transpose(0, 2, 1, 3), ((0, 0), (0, 0), (NSA_WINDOW, 0), (0, 0)))

    kw, vw = win_keys(k_w), win_keys(v_w)
    q_blocks = q.reshape(B, n_qb, NSA_QBLOCK, G, Q, Dh).transpose(1, 0, 3, 4, 2, 5)
    g_blocks = jax.nn.sigmoid(gate.astype(F32)).reshape(B, n_qb, NSA_QBLOCK, G, Q, 3).transpose(1, 0, 3, 4, 2, 5)
    bi = jnp.arange(B)[:, None, None, None]
    gi = jnp.arange(G)[None, :, None, None]
    tab_g = rel_bias.reshape(REL_BUCKETS, G, Q).transpose(1, 0, 2)
    blk_ids = jnp.arange(n_blk, dtype=jnp.int32)
    tok_in_blk = jnp.arange(SEL_BLOCK, dtype=jnp.int32)
    win_off = jnp.arange(NSA_WINDOW + NSA_QBLOCK, dtype=jnp.int32)

    def block(args):
        qb, gb, qi = args
        t = qi * NSA_QBLOCK + jnp.arange(NSA_QBLOCK, dtype=jnp.int32)
        d_c = t[:, None] - cmp_end[None, :]
        l_c = (jnp.einsum('bgqtd,bgnd->bgqtn', qb, kc).astype(F32) * scale
               + _rel_bias(rel_bias, d_c).reshape(G, Q, NSA_QBLOCK, n_cmp))
        p_c = _masked_softmax(l_c, d_c >= 0)
        o_c = jnp.einsum('bgqtn,bgnd->bgqtd', p_c.astype(dt), vc)
        imp = jnp.einsum('bgqtn,nj->bgtj', p_c, overlap)
        cur = (t // SEL_BLOCK)[:, None]
        forced = (blk_ids == 0) | (blk_ids == cur) | (blk_ids == cur - 1)
        imp = jnp.where(blk_ids > cur, -1e9, jnp.where(forced, 1e9, imp))
        _, idx = lax.top_k(imp, n_sel)
        k_g = ks[bi, gi, idx].reshape(B, G, NSA_QBLOCK, n_sel * SEL_BLOCK, Dh)
        v_g = vs[bi, gi, idx].reshape(B, G, NSA_QBLOCK, n_sel * SEL_BLOCK, Dh)
        pos = (idx[..., None] * SEL_BLOCK + tok_in_blk).reshape(B, G, NSA_QBLOCK, n_sel * SEL_BLOCK)
        d_s = t[:, None] - pos
        b_s = tab_g[gi, _t5_bucket(d_s)].transpose(0, 1, 4, 2, 3).astype(F32)
        l_s = jnp.einsum('bgqtd,bgtsd->bgqts', qb, k_g).astype(F32) * scale + b_s
        p_s = _masked_softmax(l_s, (d_s >= 0)[:, :, None])
        o_s = jnp.einsum('bgqts,bgtsd->bgqtd', p_s.astype(dt), v_g)
        start = qi * NSA_QBLOCK
        k_wb = lax.dynamic_slice_in_dim(kw, start, NSA_WINDOW + NSA_QBLOCK, axis=2)
        v_wb = lax.dynamic_slice_in_dim(vw, start, NSA_WINDOW + NSA_QBLOCK, axis=2)
        s_abs = start - NSA_WINDOW + win_off
        d_w = t[:, None] - s_abs[None, :]
        valid_w = (d_w >= 0) & (d_w < NSA_WINDOW) & (s_abs >= 0)[None, :]
        l_w = (jnp.einsum('bgqtd,bgsd->bgqts', qb, k_wb).astype(F32) * scale
               + _rel_bias(rel_bias, d_w).reshape(G, Q, NSA_QBLOCK, NSA_WINDOW + NSA_QBLOCK))
        p_w = _masked_softmax(l_w, valid_w)
        o_w = jnp.einsum('bgqts,bgsd->bgqtd', p_w.astype(dt), v_wb)
        return (gb[..., 0:1] * o_c + gb[..., 1:2] * o_s + gb[..., 2:3] * o_w).astype(dt)

    o = lax.map(block, (q_blocks, g_blocks, jnp.arange(n_qb, dtype=jnp.int32)))
    o = o.transpose(1, 0, 4, 2, 3, 5).reshape(B, T, D_MODEL)
    return o @ w_out

def _hgrn2(x, w_in, w_out, norm_gain, lb):
    B, T, _ = x.shape
    H, K, V, C = HGRN_HEADS, HGRN_KDIM, HGRN_VDIM, HGRN_CHUNK
    n_ch = T // C
    h = (x @ w_in).astype(F32)
    zq, zf, zi, zg = jnp.split(h, 4, axis=-1)
    lbf = lb.astype(F32)
    q = jax.nn.silu(zq)
    log_f = jnp.logaddexp(jnp.log(lbf), jnp.log1p(-lbf) + jax.nn.log_sigmoid(zf))
    k = (1.0 - lbf) * jax.nn.sigmoid(-zf)

    def chunks(z, d):
        return z.reshape(B, n_ch, C, H, d).transpose(1, 0, 3, 2, 4)

    causal = jnp.tril(jnp.ones((C, C), dtype=bool))[None, None, :, :, None]

    def step(S, inp):
        qc, kc, vc, gc = inp
        bcum = jnp.cumsum(gc, axis=2)
        o_inter = jnp.einsum('bhck,bhkv->bhcv', qc * jnp.exp(bcum), S)
        diff = jnp.where(causal, bcum[:, :, :, None, :] - bcum[:, :, None, :, :], -jnp.inf)
        a = jnp.einsum('bhtk,bhsk,bhtsk->bhts', qc, kc, jnp.exp(diff))
        o_intra = jnp.einsum('bhts,bhsv->bhtv', a, vc)
        b_last = bcum[:, :, -1]
        S_new = (jnp.exp(b_last)[..., None] * S
                 + jnp.einsum('bhsk,bhsv->bhkv', kc * jnp.exp(b_last[:, :, None] - bcum), vc))
        return S_new, o_inter + o_intra

    S0 = jnp.zeros((B, H, K, V), F32)
    _, o = lax.scan(step, S0, (chunks(q, K), chunks(k, K), chunks(zi, V), chunks(log_f, K)))
    o = o.transpose(1, 0, 3, 2, 4).reshape(B, T, H, V)
    o = o * lax.rsqrt(jnp.mean(o * o, axis=-1, keepdims=True) + RMS_EPS) * norm_gain.astype(F32)
    o = o * jax.nn.silu(zg.reshape(B, T, H, V))
    return o.reshape(B, T, D_MODEL).astype(x.dtype) @ w_out

def _swa(x, w_in, w_out, sinks, rel_bias):
    B, T, _ = x.shape
    nb = T // SWA_BLOCK
    Kv, Q, Dh, L = SWA_KV_HEADS, SWA_QPG, HEAD_DIM, SWA_BLOCK
    scale = Dh ** -0.5
    h = x @ w_in
    q, k, v = jnp.split(h, [ATTN_HEADS * Dh, ATTN_HEADS * Dh + Kv * Dh], axis=-1)
    q = q.reshape(B, nb, L, Kv, Q, Dh)

    def band(z):
        z = jnp.pad(z.reshape(B, T, Kv, Dh), ((0, 0), (L, 0), (0, 0), (0, 0))).reshape(B, nb + 1, L, Kv, Dh)
        return jnp.concatenate([z[:, :-1], z[:, 1:]], axis=2)

    kb, vb = band(k), band(v)
    tl = jnp.arange(L, dtype=jnp.int32)
    sl = jnp.arange(2 * L, dtype=jnp.int32)
    dist = tl[:, None] + L - sl[None, :]
    bias = _rel_bias(rel_bias, dist).reshape(Kv, Q, L, 2 * L)
    abs_s = jnp.arange(nb, dtype=jnp.int32)[:, None] * L - L + sl[None, :]
    valid = ((dist >= 0) & (dist < SWA_WINDOW))[None] & (abs_s >= 0)[:, None, :]
    logits = jnp.einsum('bntgqd,bnsgd->bngqts', q, kb).astype(F32) * scale + bias
    logits = jnp.where(valid[None, :, None, None], logits, NEG_INF)
    sink = sinks.astype(F32).reshape(Kv, Q)[None, None, :, :, None, None]
    m = jnp.maximum(jnp.max(logits, axis=-1, keepdims=True), sink)
    e = jnp.exp(logits - m)
    p = e / (jnp.sum(e, axis=-1, keepdims=True) + jnp.exp(sink - m))
    o = jnp.einsum('bngqts,bnsgd->bntgqd', p.astype(x.dtype), vb).reshape(B, T, D_MODEL)
    return o @ w_out

def second_inputs(seed: int = 0) -> dict:
    key = jax.random.key(seed)
    ks = jax.random.split(key, 22)
    beta = (8.0 * DEPTH) ** -0.25
    D = D_MODEL

    def nrm(k, shape, scale):
        return jax.random.normal(k, shape, F32) * scale

    return {
        'x': nrm(ks[0], (BATCH, SEQ, D), 1.0),
        'rel_bias': nrm(ks[1], (REL_BUCKETS, ATTN_HEADS), 0.5),
        'ln_gain': 1.0 + nrm(ks[2], (DEPTH, 3, D), 0.02),
        'ln_bias': nrm(ks[3], (DEPTH, 3, D), 0.02),
        'ffn1_w_gate': nrm(ks[4], (DEPTH, D, D_FF), D ** -0.5),
        'ffn1_w_up': nrm(ks[5], (DEPTH, D, D_FF), D ** -0.5),
        'ffn1_w_down': nrm(ks[6], (DEPTH, D_FF, D), beta * D_FF ** -0.5),
        'ffn2_w_gate': nrm(ks[7], (DEPTH, D, D_FF), D ** -0.5),
        'ffn2_w_up': nrm(ks[8], (DEPTH, D, D_FF), D ** -0.5),
        'ffn2_w_down': nrm(ks[9], (DEPTH, D_FF, D), beta * D_FF ** -0.5),
        'nsa_w_in': nrm(ks[10], (N_NSA, D, NSA_IN), D ** -0.5),
        'nsa_w_out': nrm(ks[11], (N_NSA, D, D), beta * D ** -0.5),
        'nsa_cmp_pos': nrm(ks[12], (N_NSA, 2, CMP_LEN, HEAD_DIM), 0.1),
        'nsa_cmp_w1': nrm(ks[13], (N_NSA, 2, CMP_LEN, HEAD_DIM, CMP_HIDDEN), (CMP_LEN * HEAD_DIM) ** -0.5),
        'nsa_cmp_w2': nrm(ks[14], (N_NSA, 2, CMP_HIDDEN, HEAD_DIM), CMP_HIDDEN ** -0.5),
        'hgrn_w_in': nrm(ks[15], (N_HGRN, D, 4 * D), D ** -0.5),
        'hgrn_w_out': nrm(ks[16], (N_HGRN, D, D), beta * D ** -0.5),
        'hgrn_norm_gain': 1.0 + nrm(ks[17], (N_HGRN, HGRN_VDIM), 0.02),
        'hgrn_lb': nrm(ks[18], (DEPTH, D), 1.0),
        'swa_w_in': nrm(ks[19], (N_SWA, D, SWA_IN), D ** -0.5),
        'swa_w_out': nrm(ks[20], (N_SWA, D, D), beta * D ** -0.5),
        'swa_sinks': nrm(ks[21], (N_SWA, ATTN_HEADS), 0.5),
    }

def second_block(x, rel_bias, ln_gain, ln_bias, ffn1_w_gate, ffn1_w_up, ffn1_w_down,
              ffn2_w_gate, ffn2_w_up, ffn2_w_down, nsa_w_in, nsa_w_out, nsa_cmp_pos,
              nsa_cmp_w1, nsa_cmp_w2, hgrn_w_in, hgrn_w_out, hgrn_norm_gain, hgrn_lb,
              swa_w_in, swa_w_out, swa_sinks):
    alpha = (2.0 * DEPTH) ** 0.25
    lbs = _lower_bounds(hgrn_lb)
    for i in range(DEPTH):
        x = _layer_norm(alpha * x + 0.5 * _swiglu_2(x, ffn1_w_gate[i], ffn1_w_up[i], ffn1_w_down[i]),
                        ln_gain[i, 0], ln_bias[i, 0])
        kind, slot = i % N_MIXERS, i // N_MIXERS
        if kind == 0:
            y = _nsa(x, nsa_w_in[slot], nsa_w_out[slot], nsa_cmp_pos[slot], nsa_cmp_w1[slot],
                     nsa_cmp_w2[slot], rel_bias)
        elif kind == 1:
            y = _hgrn2(x, hgrn_w_in[slot], hgrn_w_out[slot], hgrn_norm_gain[slot], lbs[i])
        else:
            y = _swa(x, swa_w_in[slot], swa_w_out[slot], swa_sinks[slot], rel_bias)
        x = _layer_norm(alpha * x + y, ln_gain[i, 1], ln_bias[i, 1])
        x = _layer_norm(alpha * x + 0.5 * _swiglu_2(x, ffn2_w_gate[i], ffn2_w_up[i], ffn2_w_down[i]),
                        ln_gain[i, 2], ln_bias[i, 2])
    return x


def setup_inputs(seed=0):
    out = dict(first_inputs(seed))
    for name, value in second_inputs(seed + 1).items():
        if name != "x":
            out[name + "_2"] = value
    return out


def reference(
    x, positions, norm_gains, ffn_w_gate, ffn_w_up, ffn_w_down, even_w_in, even_conv_w,
    even_mu_shift, rwkv_w0, rwkv_w_up, rwkv_a0, rwkv_a_up, rwkv_g_up, rwkv_k_k, rwkv_k_a,
    rwkv_r_k, rwkv_ln_w, rwkv_ln_b, even_w_out, odd_w_in, mla_q_a_norm, mla_kv_a_norm,
    mla_w_q_up, mla_w_kv_up, mla_q_norm, mla_k_norm, odd_w_out, rel_bias_2, ln_gain_2,
    ln_bias_2, ffn1_w_gate_2, ffn1_w_up_2, ffn1_w_down_2, ffn2_w_gate_2, ffn2_w_up_2,
    ffn2_w_down_2, nsa_w_in_2, nsa_w_out_2, nsa_cmp_pos_2, nsa_cmp_w1_2, nsa_cmp_w2_2,
    hgrn_w_in_2, hgrn_w_out_2, hgrn_norm_gain_2, hgrn_lb_2, swa_w_in_2, swa_w_out_2,
    swa_sinks_2,
):
    x = first_block(
        x, positions, norm_gains, ffn_w_gate, ffn_w_up, ffn_w_down, even_w_in, even_conv_w,
        even_mu_shift, rwkv_w0, rwkv_w_up, rwkv_a0, rwkv_a_up, rwkv_g_up, rwkv_k_k, rwkv_k_a,
        rwkv_r_k, rwkv_ln_w, rwkv_ln_b, even_w_out, odd_w_in, mla_q_a_norm, mla_kv_a_norm,
        mla_w_q_up, mla_w_kv_up, mla_q_norm, mla_k_norm, odd_w_out,
    )
    return second_block(
        x, rel_bias_2, ln_gain_2, ln_bias_2, ffn1_w_gate_2, ffn1_w_up_2, ffn1_w_down_2,
        ffn2_w_gate_2, ffn2_w_up_2, ffn2_w_down_2, nsa_w_in_2, nsa_w_out_2, nsa_cmp_pos_2,
        nsa_cmp_w1_2, nsa_cmp_w2_2, hgrn_w_in_2, hgrn_w_out_2, hgrn_norm_gain_2, hgrn_lb_2,
        swa_w_in_2, swa_w_out_2, swa_sinks_2,
    )


_drawn_inputs = setup_inputs


def setup_inputs(seed=0):
    import zlib

    import numpy as np

    out = dict(_drawn_inputs(seed))
    spreads = {}
    factors = {'rwkv_w_up': 3.251,
     'rwkv_k_k': 5.017,
     'rwkv_k_a': 8.0,
     'rwkv_ln_w': 8.0,
     'rwkv_ln_b': 6.703,
     'mla_q_a_norm': 8.0,
     'mla_kv_a_norm': 8.0,
     'mla_q_norm': 8.0,
     'mla_k_norm': 8.0,
     'nsa_cmp_pos_2': 3.92,
     'hgrn_norm_gain_2': 8.0,
     'hgrn_lb_2': 2.912}
    for name, (base, spread) in spreads.items():
        noise = np.random.default_rng([zlib.crc32(name.encode()), seed]).standard_normal(out[name].shape)
        drawn = base * np.exp(spread * noise) if base else spread * noise
        out[name] = __import__('jax').numpy.asarray(drawn.astype(out[name].dtype))
    for name, factor in factors.items():
        out[name] = (out[name] * factor).astype(out[name].dtype)
    return out
```

```python
from contextlib import ExitStack
import math

import numpy as np
import concourse.bass as bass
from concourse import mybir

ALU = mybir.AluOpType
ACT = mybir.ActivationFunctionType
AX = mybir.AxisListType
F32 = mybir.dt.float32
F32R = mybir.dt.float32r
I32 = mybir.dt.int32
U32 = mybir.dt.uint32

P = 128
T = 256
NT = T // P
D = 1024
KC = D // P
FF = 2816
FT = FF // P
HALF = 512
RMS_EPS = 1e-6
LN_EPS = 1e-5
DEPTH = 2
ALPHA = (2.0 * DEPTH) ** 0.25
UNUSED = ("swa_w_in_2", "swa_w_out_2", "swa_sinks_2")
ARENA = 18484


def build_program(nc, a, out, stop=None, start=None):
    ctx = ExitStack()
    with ctx:
        def sb(name, shape, dt=F32):
            return ctx.enter_context(nc.sbuf_tensor(name, shape, dt))

        def sem(name):
            return ctx.enter_context(nc.semaphore(name))

        raw_a = sb("raw_a", [P, 2, 2, D])
        hi_a = sb("hi_a", [P, 2, 2, D], F32R)
        lo_a = sb("lo_a", [P, 2, 2, D], F32R)
        raw_b = sb("raw_b", [P, 2, D])
        hi_b = sb("hi_b", [P, 2, D], F32R)
        lo_b = sb("lo_b", [P, 2, D], F32R)
        x = sb("x_res", [P, NT, D])
        xn = sb("xn", [P, NT, D])
        act_hi = sb("act_hi", [P, KC, T], F32R)
        act_lo = sb("act_lo", [P, KC, T], F32R)
        sg = sb("sg", [P, 2, T])
        hf = sb("hf", [P, 2, T])
        h_hi = sb("h_hi", [P, 2, T], F32R)
        h_lo = sb("h_lo", [P, 2, T], F32R)
        ln_g = sb("ln_g", [P, D])
        ln_b = sb("ln_b", [P, D])
        ident = sb("ident", [P, P])
        prow = sb("prow", [P, 3, P])
        pcol = sb("pcol", [P, 3, P])
        stat = sb("stat", [P, NT, 2, 6])
        mv = sb("mv", [P, NT, 2])
        ssq = sb("ssq", [P, NT])
        rstd = sb("rstd", [P, NT])
        neg_half = sb("neg_half", [P, T])
        arena = sb("arena", [P, ARENA])
        block_ones = sb("block_ones", [P, P])
        level = sb("level", [P, 7, P])
        level0_t = sb("level0_t", [P, P])
        upper = sb("upper", [P, 2, P])
        small = sb("small", [P, 256])
        bank = [ctx.enter_context(nc.psum_tensor(f"bank{i}", [P, HALF], F32)) for i in range(8)]

        a_loaded = [sem("a_loaded0"), sem("a_loaded1")]
        b_loaded = [sem("b_loaded0"), sem("b_loaded1")]
        a_hi_done = sem("a_hi_done")
        b_hi_done = sem("b_hi_done")
        a_lo_done = sem("a_lo_done")
        b_lo_done = sem("b_lo_done")
        a_used = sem("a_used")
        b_used = sem("b_used")
        silu_done = sem("silu_done")
        h_done = sem("h_done")
        hs_hi = sem("hs_hi")
        hs_done = sem("hs_done")
        pe_done = sem("pe_done")
        act_done = sem("act_done")
        dve_done = sem("dve_done")
        pool_done = sem("pool_done")
        done_of = {"pe": pe_done, "act": act_done, "dve": dve_done, "pool": pool_done}
        pt_read = sem("pt_read")
        phase_done = sem("phase_done")
        p_loaded = sem("p_loaded")
        ln_loaded = sem("ln_loaded")
        out_stored = sem("out_stored")

        block = ctx.enter_context(nc.Block())

        na = [0]
        nb = [0]
        a_words = [0, 0]
        b_words = [0, 0]
        nffn = [0]
        nphase = [0]
        chain = {"pe": 0, "act": 0, "dve": 0, "pool": 0}
        npt = [0]

        def done(kind, ins):
            chain[kind] += 1
            ins.then_inc(done_of[kind], 1)
            return chain[kind]

        def V(dve, ins):
            dve.wait_ge(dve_done, done("dve", ins))

        def A(act, ins):
            act.wait_ge(act_done, done("act", ins))

        def G(pool, ins):
            pool.wait_ge(pool_done, done("pool", ins))

        def end_phase():
            nphase[0] += 1
            n = 4 * nphase[0]

            @block.tensor
            def _(pe):
                pe.drain().then_inc(phase_done, 1)
                pe.wait_ge(phase_done, n)

            @block.scalar
            def _(act):
                act.drain().then_inc(phase_done, 1)
                act.wait_ge(phase_done, n)

            @block.vector
            def _(dve):
                dve.drain().then_inc(phase_done, 1)
                dve.wait_ge(phase_done, n)

            @block.gpsimd
            def _(pool):
                pool.drain().then_inc(phase_done, 1)
                pool.wait_ge(phase_done, n)

        prime = sb("prime", [P, 1])

        @block.vector
        def _(dve):
            dve.memset(prime[:, :], 0.0).then_inc(a_lo_done, 2)
            dve.memset(neg_half[:, :], -0.5).then_inc(b_lo_done, 2)

        @block.gpsimd
        def _(pool):
            pool.nop().then_inc(a_used, 2)
            pool.nop().then_inc(b_used, 2)
            pool.nop().then_inc(h_done, 2)
            pool.nop().then_inc(pt_read, 2)

        rows = []
        col_of = {}
        fill = [0, 0, 0]

        def param(name, src, n, width=P, tile=0):
            rows.append((tile, fill[tile], n, src, width))
            col_of[name] = (tile, fill[tile])
            fill[tile] += n

        def as_rows(ap):
            return ap.rearrange("(r c) -> r c", c=P)

        param("norm", a["norm_gains"].rearrange("l s (r c) -> (l s r) c", c=P), 48)
        param("conv", a["even_conv_w"][0].rearrange("j (r c) -> (j r) c", c=P), 12)
        param("mu", as_rows(a["even_mu_shift"][0][0:1536]), 12)
        param("mu_wa", a["even_mu_shift"][0:1, 1536:1600], 1, 64)
        param("mu_g", a["even_mu_shift"][0:1, 1600:1696], 1, 96)
        for name in ("rwkv_w0", "rwkv_a0", "rwkv_k_k", "rwkv_k_a", "rwkv_ln_w", "rwkv_ln_b"):
            param(name, as_rows(a[name][0]), 4)
        param("rwkv_r_k", a["rwkv_r_k"][0].rearrange("(r q) c -> r (q c)", q=2), 4)
        param("q_a", as_rows(a["mla_q_a_norm"][0]), 3)
        param("kv_a", as_rows(a["mla_kv_a_norm"][0]), 2)
        param("qn", a["mla_q_norm"][0:1, 0:128], 1)
        param("kn", a["mla_k_norm"][0:1, 0:128], 1)
        param("cmp_pos", a["nsa_cmp_pos_2"][0].rearrange("a (r l) d -> (a r) (l d)", l=2), 32, tile=1)
        param("lb", a["hgrn_lb_2"].rearrange("l (r c) -> (l r) c", c=P), 16, tile=1)
        param("hg", a["hgrn_norm_gain_2"], 1, tile=1)
        param("ln_gain", a["ln_gain_2"].rearrange("l s (r c) -> (l s r) c", c=P), 48, tile=1)
        param("ln_bias", a["ln_bias_2"].rearrange("l s (r c) -> (l s r) c", c=P), 48, tile=2)
        assert max(fill) <= P

        def pc(name, i=0):
            tile, row = col_of[name]
            return pcol[:, tile, row + i:row + i + 1]

        tab = sb("tab", [33, 16])
        onehot = sb("onehot", [33, 384])
        bias_row = sb("bias_row", [16, 384])
        seen = sb("seen", [P, 1])
        scratch = nc.dram_tensor("bias_scratch", (16, P, 512), F32)
        bias_in = sem("bias_in")
        bias_done = sem("bias_done")
        bias_stored = sem("bias_stored")

        @block.vector
        def _(dve):
            dve.memset(tab[32:33, :], -1e30).then_inc(bias_in, 1)

        @block.scalar
        def _(act):
            act.dma_start(tab[0:32, :], a["rel_bias_2"]).then_inc(p_loaded, 16)
            act.dma_start(onehot[:, :], a["c_onehot"]).then_inc(p_loaded, 16)
            act.dma_start(seen[:, :], a["c_seen"]).then_inc(p_loaded, 16)

        prow_zero = sem("prow_zero")
        pcol_in = sem("pcol_in")
        pcol_done = sem("pcol_done")

        @block.gpsimd
        def _(pool):
            pool.memset(prow[:, :, :], 0.0).then_inc(prow_zero, 1)

        @block.scalar
        def _(act):
            act.dma_start(ident[:, :], a["c_ident"]).then_inc(p_loaded, 16)
            for dst, name in ((block_ones, "c_block_ones"), (level, "c_level"), (level0_t, "c_level0_t"),
                              (upper, "c_upper")):
                act.dma_start(dst[:], a[name]).then_inc(p_loaded, 16)
            act.wait_ge(prow_zero, 1)
            for tile, row, n, src, width in rows:
                act.dma_start(prow[row:row + n, tile, 0:width], src).then_inc(p_loaded, 16)

        @block.tensor
        def _(pe):
            pe.wait_ge(p_loaded, 16 * (len(rows) + 8))
            for tile in range(3):
                ins = pe.transpose(bank[0][:, tile * P:tile * P + P], prow[:, tile, :], ident[:, :])
            ins.then_inc(pcol_in, 1)
            pe.wait_ge(bias_in, 1)
            pe.matmul(bank[1][0:16, 0:384], tab[:, :], onehot[:, :], start=True, stop=True).then_inc(bias_done, 1)

        @block.vector
        def _(dve):
            dve.wait_ge(pcol_in, 1)
            dve.tensor_copy(pcol[:, :, :], bank[0][:, 0:3 * P].rearrange("p (a b) -> p a b", a=3)
                            ).then_inc(pcol_done, 1)

        @block.vector
        def _(dve):
            dve.wait_ge(bias_done, 1)
            dve.tensor_scalar(bias_row[:, :], bank[1][0:16, 0:384], 8.0, None, ALU.mult).then_inc(bias_done, 1)

        @block.scalar
        def _(act):
            act.wait_ge(bias_done, 2)
            act.dma_start(bass.AP(scratch, 0, [[P * 512, 16], [513, P], [1, 384]]),
                          bias_row[:, :].unsqueeze(1).to_broadcast((16, P, 384))).then_inc(bias_stored, 16)

        x_loaded = sem("x_loaded")

        @block.sync
        def _(sp):
            sp.dma_start(x[:, :, :], a["x"][0].rearrange("(t p) d -> p t d", p=P)).then_inc(x_loaded, 16)

        @block.scalar
        def _(act):
            act.wait_ge(pcol_done, 1)
            act.wait_ge(x_loaded, 16)

        @block.gpsimd
        def _(pool):
            pool.wait_ge(x_loaded, 16)

        end_phase()

        def cols_unit(w, c0, width=P):
            return w[:, c0:c0 + width].rearrange("(k p) n -> p k n", p=P)

        def a_load(sp, n, slot, sources):
            sp.wait_ge(a_lo_done, n + 1)
            for dst, src in sources:
                sp.dma_start(dst, src).then_inc(a_loaded[slot], 16)

        def hi_pair(act, i, s, AW, A0):
            slot = (A0 + s) % 2
            act.wait_ge(a_loaded[slot], i * 32 + (AW[slot] + 32 * (s // 2 + 1)))
            act.wait_ge(a_used, i * 2 + (A0 + s + 1))
            act.activation(hi_a[:, slot, :, :], raw_a[:, slot, :, :], ACT.Copy).then_inc(a_hi_done, 1)

        def lo_pair(dve, i, s, A0):
            slot = (A0 + s) % 2
            dve.wait_ge(a_hi_done, i * 2 + (A0 + s + 1))
            dve.tensor_tensor(lo_a[:, slot, :, :], raw_a[:, slot, :, :], hi_a[:, slot, :, :].bitcast(F32),
                              ALU.subtract).then_inc(a_lo_done, 1)

        PASSES = ((0, 0), (0, 1), (1, 0))

        def open_pairs(n):
            A0, AW = na[0], list(a_words)
            na[0] += n
            for s in range(n):
                a_words[(A0 + s) % 2] += 32
            return A0, AW

        @block.scalar
        def _(act):
            hi_pair(act, 0, 0, (0, 0), 0)

        @block.vector
        def _(dve):
            lo_pair(dve, 0, 0, 0)

        def proj_T(source, npairs, dest, evac=None):
            evac = evac or (lambda act, i, s, src: act.activation(dest(i, s), src, ACT.Copy))
            A0, AW = open_pairs(npairs)
            R0 = npt[0]
            npt[0] += npairs
            loops = npairs // 2 if npairs % 2 == 0 and npairs >= 4 else 0

            @block.sync
            def _(sp):
                def load(i, s):
                    slot = (A0 + s) % 2
                    for u in range(2):
                        if u == 0:
                            sp.wait_ge(a_lo_done, i * 2 + (A0 + s + 1))
                        src = source(i, s, u)
                        sp.dma_start(raw_a[:, slot, u, :].rearrange("p (k n) -> p k n", k=KC)[:, :, 0:src.shape[2]],
                                     src).then_inc(a_loaded[slot], 16)
                if loops:
                    with sp.Fori(0, loops) as i:
                        load(i, 0)
                        load(i, 1)
                else:
                    for s in range(npairs):
                        load(0, s)

            @block.scalar
            def _(act):
                def move(i, s):
                    act.wait_ge(a_used, i * 2 + (A0 + s + 3))
                    evac(act, i, s, bank[4 + s % 2][:, :].rearrange("p (u t) -> p u t", u=2)).then_inc(pt_read, 1)
                if loops:
                    with act.Fori(0, loops) as i:
                        for s in range(2):
                            hi_pair(act, i, s + 1, AW, A0)
                            move(i, s)
                else:
                    for s in range(npairs):
                        hi_pair(act, 0, s + 1, AW, A0)
                        move(0, s)

            @block.vector
            def _(dve):
                if loops:
                    with dve.Fori(0, loops) as i:
                        lo_pair(dve, i, 1, A0)
                        lo_pair(dve, i, 2, A0)
                else:
                    for s in range(npairs):
                        lo_pair(dve, 0, s + 1, A0)

            @block.tensor
            def _(pe):
                def products(i, s):
                    slot = (A0 + s) % 2
                    pe.wait_ge(a_lo_done, i * 2 + (A0 + s + 3))
                    pe.wait_ge(pt_read, i * 2 + (R0 + s + 1))
                    for u in range(2):
                        for k in range(KC):
                            w = slice(k * P, k * P + P)
                            for m, (wp, xp) in enumerate(PASSES):
                                ins = pe.matmul(bank[4 + s % 2][:, u * T:u * T + T], (hi_a, lo_a)[wp][:, slot, u, w],
                                                (act_hi, act_lo)[xp][:, k, :], start=(k == 0 and m == 0),
                                                stop=(k == KC - 1 and m == 2))
                    ins.then_inc(a_used, 1)
                if loops:
                    with pe.Fori(0, loops) as i:
                        products(i, 0)
                        products(i, 1)
                else:
                    for s in range(npairs):
                        products(0, s)

        def proj_rows(w, nk, width, k0=0, parts=None):
            npairs = (nk + 1) // 2
            A0, AW = open_pairs(npairs)
            parts = parts or [(c, min(width, c + HALF)) for c in range(0, width, HALF)]

            @block.sync
            def _(sp):
                for s in range(npairs):
                    slot = (A0 + s) % 2
                    sp.wait_ge(a_lo_done, A0 + s + 1)
                    units = min(2, nk - 2 * s)
                    for u in range(units):
                        r = (2 * s + u) * P
                        sp.dma_start(raw_a[:, slot, u, 0:width], w[r:r + P, :]).then_inc(a_loaded[slot], 32 // units)

            @block.scalar
            def _(act):
                for s in range(npairs):
                    hi_pair(act, 0, s + 1, AW, A0)

            @block.vector
            def _(dve):
                for s in range(npairs):
                    lo_pair(dve, 0, s + 1, A0)

            box = []

            @block.tensor
            def _(pe):
                for s in range(npairs):
                    slot = (A0 + s) % 2
                    pe.wait_ge(a_lo_done, A0 + s + 3)
                    for u in range(min(2, nk - 2 * s)):
                        k = 2 * s + u
                        for t in range(NT):
                            for h, (c, e) in enumerate(parts):
                                for m, (wp, xp) in enumerate(PASSES):
                                    ins = pe.matmul(bank[2 * t + h][:, 0:e - c],
                                                    (act_hi, act_lo)[xp][:, k0 + k, t * P:t * P + P],
                                                    (hi_a, lo_a)[wp][:, slot, u, c:e],
                                                    start=(k == 0 and m == 0), stop=(k == nk - 1 and m == 2))
                    ins.then_inc(a_used, 1)
            return A0 + npairs + 2

        def split_act(src, k0, n, ready_dve):
            box = []

            @block.scalar
            def _(act):
                act.wait_ge(dve_done, ready_dve)
                box.append(done("act", act.activation(act_hi[:, k0:k0 + n, :], src, ACT.Copy)))

            @block.vector
            def _(dve):
                dve.wait_ge(act_done, box[0])
                dve.tensor_tensor(act_lo[:, k0:k0 + n, :], src, act_hi[:, k0:k0 + n, :].bitcast(F32), ALU.subtract)

        def out_proj(w, scale):
            update_x(a_used, proj_rows(w, KC, D), scale)

        def update_x(used, ready, scale):
            @block.vector
            def _(dve):
                dve.wait_ge(used, ready)
                if x_free[0]:
                    dve.wait_ge(pool_done, x_free[0])
                for t in range(NT):
                    for h in range(2):
                        cols = slice(h * HALF, h * HALF + HALF)
                        ins = dve.scalar_tensor_tensor(x[:, t, cols], bank[2 * t + h][:, :], scale, x[:, t, cols],
                                                       ALU.mult, ALU.add)
                    x_ready[t] = done("dve", ins)

        x_free = [0]
        x_ready = [0] * NT

        xpose_done = sem("xpose_done")
        xhi_done = sem("xhi_done")
        xlo_done = sem("xlo_done")
        counts = {"xp": 0, "ln": 0}

        def view(k):
            return bank[4 + k // 2][:, (k % 2) * T:(k % 2) * T + T]

        def pe_transposes(src, nk, waits=()):
            base = counts["xp"]
            counts["xp"] += nk

            @block.tensor
            def _(pe):
                for t, ws in enumerate(waits):
                    for which, n in ws:
                        pe.wait_ge(which, n)
                    if t < NT - 1:
                        for k in range(nk):
                            pe.transpose(view(k)[:, t * P:t * P + P], src(t, k), ident[:, :])
                for k in range(nk):
                    for t in (range(NT) if not waits else (NT - 1,)):
                        ins = pe.transpose(view(k)[:, t * P:t * P + P], src(t, k), ident[:, :])
                    ins.then_inc(xpose_done, 1)
            return base

        def act_split_ready():
            n = counts["xp"]

            @block.tensor
            def _(pe):
                pe.wait_ge(xlo_done, n)

        def transpose_split(src, gain, nk=KC, dst0=0, waits=(), barrier=True):
            base = pe_transposes(src, nk, waits)

            @block.scalar
            def _(act):
                for k in range(nk):
                    act.wait_ge(xpose_done, base + min(nk, 2 * (k // 2) + 2))
                    act.activation(act_hi[:, dst0 + k, :], view(k), ACT.Copy,
                                   scale=gain(k) if gain else 1.0).then_inc(xhi_done, 1)

            @block.vector
            def _(dve):
                for k in range(nk):
                    dve.wait_ge(xhi_done, base + min(nk, 2 * (k // 2) + 2))
                    dve.scalar_tensor_tensor(act_lo[:, dst0 + k, :], view(k), gain(k) if gain else 1.0,
                                             act_hi[:, dst0 + k, :].bitcast(F32), ALU.mult, ALU.subtract
                                             ).then_inc(xlo_done, 1)
            if barrier:
                end_phase()
            else:
                act_split_ready()

        def rms_norm_to_act(layer, which, barrier=False):
            sq, ms, rs, xs = [0, 0], [0, 0], [0, 0], [0, 0]

            @block.scalar
            def _(act):
                for t in range(NT):
                    if x_ready[t]:
                        act.wait_ge(dve_done, x_ready[t])
                    sq[t] = done("act", act.activation(xn[:, t, :], x[:, t, :], ACT.Square,
                                                       accum_out=ssq[:, t:t + 1]))

            @block.vector
            def _(dve):
                for t in range(NT):
                    dve.wait_ge(act_done, sq[t])
                    ms[t] = done("dve", dve.tensor_scalar(ssq[:, t:t + 1], ssq[:, t:t + 1], 1.0 / D, RMS_EPS,
                                                          ALU.mult, ALU.add))

            inverse_root(ms, rs)

            @block.vector
            def _(dve):
                dve.wait_ge(pool_done, rs[0])
                xs[0] = done("dve", dve.tensor_scalar(xn[:, 0, :], x[:, 0, :], rstd[:, 0:1], None, ALU.mult))

            @block.scalar
            def _(act):
                act.wait_ge(pool_done, rs[1])
                xs[1] = done("act", act.activation(xn[:, 1, :], x[:, 1, :], ACT.Copy, scale=rstd[:, 1:2]))
            transpose_split(lambda t, k: xn[:, t, k * P:k * P + P],
                            lambda k: pc("norm", (layer * 3 + which) * KC + k),
                            waits=([(dve_done, xs[0])], [(act_done, xs[1])]), barrier=barrier)

        def inverse_root(ms, rs):
            @block.gpsimd
            def _(pool):
                for t in range(NT):
                    pool.wait_ge(dve_done, ms[t])
                    rs[t] = done("pool", pool.tensor_tensor(out=rstd[:, t:t + 1], in0=ssq[:, t:t + 1],
                                                            in1=neg_half[:, 0:1], op=ALU.pow))

        def layer_norm(layer, which, last=False):
            counts["ln"] += 1
            n = counts["ln"]
            ms, rs, xs = [0, 0], [0, 0], [0, 0]
            free = x_free[0]

            @block.gpsimd
            def _(pool):
                if n > 1:
                    pool.wait_ge(pool_done, free)
                for dst, src in ((ln_g, a["ln_gain_2"]), (ln_b, a["ln_bias_2"])):
                    pool.dma_start(dst[:, :], src[layer, which:which + 1, :].to_broadcast((P, D))
                                   ).then_inc(ln_loaded, 16)

            @block.vector
            def _(dve):
                agg = [0, 0]
                for t in range(NT):
                    dve.wait_ge(dve_done, x_ready[t])
                    for h in range(2):
                        last_stat = done("dve", dve.bn_stats(stat[:, t, h, :], x[:, t, h * HALF:h * HALF + HALF]))
                    dve.wait_ge(dve_done, last_stat)
                    V(dve, dve.bn_aggr(mv[:, t, :], stat[:, t, :, :]))
                    ms[t] = done("dve", dve.tensor_scalar(ssq[:, t:t + 1], mv[:, t, 1:2], LN_EPS / ALPHA ** 2, None,
                                                          ALU.add))

            inverse_root(ms, rs)

            @block.vector
            def _(dve):
                for t in range(NT):
                    dve.wait_ge(pool_done, rs[t])
                    xs[t] = done("dve", dve.tensor_scalar(xn[:, t, :], x[:, t, :], mv[:, t, 0:1], rstd[:, t:t + 1],
                                                          ALU.subtract, ALU.mult))

            @block.gpsimd
            def _(pool):
                pool.wait_ge(ln_loaded, 32 * n)
                for t in range(NT):
                    pool.wait_ge(dve_done, xs[t])
                    G(pool, pool.tensor_tensor(out=x[:, t, :], in0=xn[:, t, :], in1=ln_g[:, :], op=ALU.mult))
                    if not last:
                        G(pool, pool.tensor_tensor(out=x[:, t, :], in0=x[:, t, :], in1=ln_b[:, :], op=ALU.add))
                x_free[0] = chain["pool"]
            if last:
                @block.vector
                def _(dve):
                    dve.wait_ge(pool_done, x_free[0])
                    dve.tensor_tensor(x[:, :, :], x[:, :, :], ln_b[:, :].unsqueeze(1).to_broadcast((P, NT, D)), ALU.add)
                end_phase()
                return
            base = pe_transposes(lambda t, k: xn[:, t, k * P:k * P + P], KC,
                                 waits=([(dve_done, xs[0])], [(dve_done, xs[1])]))
            scaled, hi = [], []

            @block.scalar
            def _(act):
                for k in range(KC):
                    act.wait_ge(xpose_done, base + 2 * (k // 2) + 2)
                    c = (layer * 3 + which) * KC + k
                    scaled.append(done("act", act.activation(ln_t[:, k, :], view(k), ACT.Identity,
                                                             scale=pc("ln_gain", c), bias=pc("ln_bias", c))))

            @block.vector
            def _(dve):
                for k in range(0, KC, 2):
                    two = slice(k, k + 2)
                    dve.wait_ge(act_done, scaled[k + 1])
                    hi = done("dve", dve.tensor_copy(act_hi[:, two, :], ln_t[:, two, :]))
                    dve.wait_ge(dve_done, hi)
                    dve.tensor_tensor(act_lo[:, two, :], ln_t[:, two, :], act_hi[:, two, :].bitcast(F32),
                                      ALU.subtract).then_inc(xlo_done, 2)
            act_split_ready()

        ln_t = arena[:, 0:KC * T].rearrange("p (k t) -> p k t", k=KC)

        def ffn(w_gate, w_up, w_down, scale, last_ffn=False):
            A0, B0, T0 = na[0], nb[0], nffn[0] * FT
            na[0] += FT
            nb[0] += FT
            nffn[0] += 1
            AW, BW = list(a_words), list(b_words)
            for s in range(2):
                a_words[(A0 + s) % 2] += 32 * (FT // 2)
                b_words[(B0 + s) % 2] += 16 * (FT // 2)

            @block.sync
            def _(sp):
                with sp.Fori(0, FT // 2) as i:
                    for s in range(2):
                        sa, sbb = (A0 + s) % 2, (B0 + s) % 2
                        c = (i * 2 + s) * P
                        for u, w in enumerate((w_gate, w_up)):
                            if u == 0:
                                sp.wait_ge(a_lo_done, i * 2 + (A0 + s + 1))
                            sp.dma_start(raw_a[:, sa, u, :].rearrange("p (k n) -> p k n", k=KC),
                                         w[:, bass.ds(c, P)].rearrange("(k p) n -> p k n", p=P)
                                         ).then_inc(a_loaded[sa], 16)
                        sp.wait_ge(b_lo_done, i * 2 + (B0 + s + 1))
                        sp.dma_start(raw_b[:, sbb, :], w_down[bass.ds(c, P), :]).then_inc(b_loaded[sbb], 16)

            def act_tile(act, i, s):
                slot = (B0 + s) % 2
                act.wait_ge(b_loaded[slot], i * 16 + (BW[slot] + 16 * (s // 2 + 1)))
                act.wait_ge(b_used, i * 2 + (B0 + s + 1))
                act.activation(hi_b[:, slot, :], raw_b[:, slot, :], ACT.Copy).then_inc(b_hi_done, 1)
                act.wait_ge(a_used, i * 2 + (A0 + s + 3))
                act.wait_ge(h_done, i * 2 + (T0 + s + 1))
                act.activation(sg[:, s % 2, :], bank[4 + s % 2][:, 0:T], ACT.Silu).then_inc(silu_done, 1)

            @block.scalar
            def _(act):
                with act.Fori(0, FT // 2 - 1) as i:
                    for s in range(2):
                        hi_pair(act, i, s + 1, AW, A0)
                        act_tile(act, i, s)
                hi_pair(act, FT // 2 - 1, 1, AW, A0)
                act_tile(act, FT // 2 - 1, 0)
                if not last_ffn:
                    hi_pair(act, FT // 2 - 1, 2, AW, A0)
                act_tile(act, FT // 2 - 1, 1)

            def dve_tile(dve, i, s):
                slot = (B0 + s) % 2
                dve.wait_ge(b_hi_done, i * 2 + (B0 + s + 1))
                dve.tensor_tensor(lo_b[:, slot, :], raw_b[:, slot, :], hi_b[:, slot, :].bitcast(F32),
                                  ALU.subtract).then_inc(b_lo_done, 1)
                dve.wait_ge(silu_done, i * 2 + (T0 + s + 1))
                dve.tensor_tensor(hf[:, s, :], sg[:, s, :], bank[4 + s][:, T:2 * T], ALU.mult
                                  ).then_inc(h_done, 1)
                dve.wait_ge(h_done, i * 2 + (T0 + s + 3))
                dve.wait_ge(b_used, i * 2 + (B0 + s + 1))
                dve.tensor_copy(h_hi[:, s, :], hf[:, s, :]).then_inc(hs_hi, 1)
                dve.wait_ge(hs_hi, i * 2 + (T0 + s + 1))
                dve.tensor_tensor(h_lo[:, s, :], hf[:, s, :], h_hi[:, s, :].bitcast(F32), ALU.subtract
                                  ).then_inc(hs_done, 1)

            @block.vector
            def _(dve):
                with dve.Fori(0, FT // 2 - 1) as i:
                    for s in range(2):
                        lo_pair(dve, i, s + 1, A0)
                        dve_tile(dve, i, s)
                lo_pair(dve, FT // 2 - 1, 1, A0)
                dve_tile(dve, FT // 2 - 1, 0)
                if not last_ffn:
                    lo_pair(dve, FT // 2 - 1, 2, A0)
                dve_tile(dve, FT // 2 - 1, 1)

            def gate_up(pe, i, s):
                slot = (A0 + s) % 2
                pe.wait_ge(a_lo_done, i * 2 + (A0 + s + 3))
                pe.wait_ge(h_done, i * 2 + (T0 + s + 1))
                for u in range(2):
                    for k in range(KC):
                        w = slice(k * P, k * P + P)
                        for m, (wt, xt) in enumerate(((hi_a, act_hi), (hi_a, act_lo), (lo_a, act_hi))):
                            ins = pe.matmul(bank[4 + s % 2][:, u * T:u * T + T], wt[:, slot, u, w], xt[:, k, :],
                                            start=(k == 0 and m == 0), stop=(k == KC - 1 and m == 2))
                ins.then_inc(a_used, 1)

            def down(pe, i, s, first=False, last=False):
                slot = (B0 + s) % 2
                pe.wait_ge(b_lo_done, i * 2 + (B0 + s + 3))
                pe.wait_ge(hs_done, i * 2 + (T0 + s + 1))
                for t in range(NT):
                    tok = slice(t * P, t * P + P)
                    for h in range(2):
                        cols = slice(h * HALF, h * HALF + HALF)
                        for m, (ht, wt) in enumerate(((h_hi, hi_b), (h_hi, lo_b), (h_lo, hi_b))):
                            ins = pe.matmul(bank[2 * t + h][:, :], ht[:, s % 2, tok], wt[:, slot, cols],
                                            start=(first and m == 0), stop=(last and m == 2))
                ins.then_inc(b_used, 1)

            @block.tensor
            def _(pe):
                gate_up(pe, 0, 0)
                gate_up(pe, 0, 1)
                down(pe, 0, 0, first=True)
                with pe.Fori(0, FT // 2 - 1) as i:
                    gate_up(pe, i, 2)
                    down(pe, i, 1)
                    gate_up(pe, i, 3)
                    down(pe, i, 2)
                down(pe, FT // 2 - 1, 1, last=True)
            update_x(b_used, B0 + FT + 2, scale)


        def piece(start, *shape):
            n = int(np.prod(shape))
            assert start + n <= ARENA, (start, shape)
            v = arena[:, start:start + n]
            if len(shape) == 1:
                return v
            names = " ".join("abcd"[:len(shape)])
            return v.rearrange(f"p ({names}) -> p {names}", **dict(zip("abcd", shape)))

        def cols_dyn(w, i, s, u, c0=0):
            return w[:, bass.ds(i * 4 * P + (c0 + (2 * s + u) * P), P)].rearrange("(k p) n -> p k n", p=P)

        def pcs(name, n):
            tile, row = col_of[name]
            return pcol[:, tile, row:row + n]

        def flat(ap):
            return ap.rearrange("p a b -> p (a b)")

        def conv_rwkv():
            NTILE = 26
            PITCH = T + 2
            pT = piece(0, NTILE, PITCH)
            mx = piece(NTILE * PITCH, 14, T)
            live = NTILE * PITCH + 14 * T
            ar = piece(live, 4, 2, 2 * P)
            bt = piece(live + 2048, 4, T)
            kt = piece(live + 3072, 4, T)
            gate = piece(live + 4096, 4, T)
            vtok = piece(live + 5120, 2, HALF)
            bonus = piece(live + 6144, 4, T)
            bktok = piece(live + 7168, 2, HALF)
            mixed, conv_ready, m = [], [], {}
            tmp = [piece(i * 1024, 4, T) for i in range(3)]

            w_in = a["even_w_in"][0]

            w_small = piece(live + 7168, 1024)
            small_loaded = sem("small_loaded")

            @block.gpsimd
            def _(pool):
                pool.dma_start(w_small[0:32, 0:512], a["rwkv_w_up"][0]).then_inc(small_loaded, 16)
                pool.dma_start(w_small[32:64, 0:512], a["rwkv_a_up"][0]).then_inc(small_loaded, 16)
                pool.dma_start(w_small[0:96, 512:1024], a["rwkv_g_up"][0]).then_inc(small_loaded, 16)
                G(pool, pool.memset(pT[:, :, 0:2], 0.0))

            proj_T(lambda i, s, u: cols_dyn(w_in, i, s, u), 12, lambda i, s: pT[:, bass.ds(i * 4 + 2 * s, 2), 2:PITCH])
            proj_T(lambda i, s, u: w_in[:, 3072 + 64 * u:3072 + (64, 160)[u]].rearrange("(k p) n -> p k n", p=P), 1,
                   lambda i, s: pT[:, 24:26, 2:PITCH])
            end_phase()

            @block.vector
            def _(dve):
                cur = pT[:, 12:26, 2:PITCH]
                V(dve, dve.tensor_tensor(mx[:, :, :], pT[:, 12:26, 1:PITCH - 1], cur, ALU.subtract))
                for i in range(14):
                    mu = pc("mu", i) if i < 12 else pc(("mu_wa", "mu_g")[i - 12])
                    last = done("dve", dve.scalar_tensor_tensor(mx[:, i, :], mx[:, i, :], mu, pT[:, 12 + i, 2:PITCH],
                                                                ALU.mult, ALU.add))
                mixed.append(last)
                V(dve, dve.tensor_tensor(pT[:, 8:12, :], pT[:, 8:12, :], pT[:, 4:8, :], ALU.mult))
                for i in range(4):
                    u = pT[:, 8 + i, :]
                    y = pT[:, 4 + i, 0:T]
                    V(dve, dve.tensor_scalar(y, u[:, 0:T], pc("conv", i), None, ALU.mult))
                    V(dve, dve.scalar_tensor_tensor(y, u[:, 1:T + 1], pc("conv", 4 + i), y, ALU.mult, ALU.add))
                    V(dve, dve.scalar_tensor_tensor(y, u[:, 2:T + 2], pc("conv", 8 + i), y, ALU.mult, ALU.add))
                y = pT[:, 4:8, 0:T]
                conv_ready.append(done("dve", dve.tensor_tensor(y, y, pT[:, 0:4, 2:PITCH], ALU.mult)))
            split_act(pT[:, 4:8, 0:T], 0, 4, conv_ready[0])

            dwa = mx[:, 12, :]
            dg = mx[:, 13, :]

            @block.scalar
            def _(act):
                act.wait_ge(dve_done, mixed[0])
                act.activation(dwa[0:32, :], dwa[0:32, :], ACT.Tanh)
                m["tanh"] = done("act", act.activation(dg[0:96, :], dg[0:96, :], ACT.Tanh, scale=0.5))

            @block.vector
            def _(dve):
                dve.wait_ge(act_done, m["tanh"])
                m["dg"] = done("dve", dve.tensor_scalar(dg[0:96, :], dg[0:96, :], 0.5, 0.5, ALU.mult, ALU.add))

            @block.tensor
            def _(pe):
                pe.wait_ge(small_loaded, 48)
                pe.wait_ge(dve_done, m["dg"])
                for i in range(4):
                    o = slice((i % 2) * T, (i % 2) * T + T)
                    c = slice(i * P, i * P + P)
                    pe.matmul(bank[i // 2][:, o], w_small[0:32, c], dwa[0:32, :], start=True, stop=True)
                    pe.matmul(bank[2 + i // 2][:, o], w_small[32:64, c], dwa[32:64, :], start=True, stop=True)
                    ins = pe.matmul(bank[6 + i // 2][:, o], w_small[0:96, 512 + i * P:512 + i * P + P], dg[0:96, :],
                                    start=True, stop=True)
                m["lora"] = done("pe", ins)
                for c in range(2):
                    for i in range(4):
                        ins = pe.transpose(bank[4 + c][:, i * P:i * P + P], mx[:, 8 + i, c * P:c * P + P], ident[:, :])
                m["vtok"] = done("pe", ins)

            @block.vector
            def _(dve):
                half = small[:, 0:8]
                dve.tensor_scalar(half[:, 0:4], pcs("rwkv_w0", 4), 0.5, None, ALU.mult)
                m["half"] = done("dve", dve.tensor_scalar(half[:, 4:8], pcs("rwkv_a0", 4), 0.5, None, ALU.mult))
            ld, aa = tmp[0], tmp[1]

            @block.scalar
            def _(act):
                act.wait_ge(dve_done, m["half"])
                act.wait_ge(pe_done, m["lora"])
                for j, dst in ((0, ld), (1, aa)):
                    for i in range(4):
                        ins = act.activation(dst[:, i, :], bank[2 * j + i // 2][:, (i % 2) * T:(i % 2) * T + T], ACT.Tanh,
                                             bias=small[:, 4 * j + i:4 * j + i + 1], scale=0.5)
                act.activation(gate[:, 0:2, :], bank[6][:, :].rearrange("p (a t) -> p a t", a=2), ACT.Copy)
                act.activation(gate[:, 2:4, :], bank[7][:, :].rearrange("p (a t) -> p a t", a=2), ACT.Copy)
                act.wait_ge(pe_done, m["vtok"])
                act.activation(vtok[:, 0, :], bank[4][:, :], ACT.Copy)
                act.activation(vtok[:, 1, :], bank[5][:, :], ACT.Copy)
            end_phase()

            E05 = math.exp(-0.5)
            r, k, v = mx[:, 0:4, :], mx[:, 4:8, :], mx[:, 8:12, :]
            sumA, sumB, kk, kh = tmp[2], piece(3072, 4, T), piece(4096, 4, T), piece(5120, 4, T)
            t5 = xn[:, 1, :].rearrange("p (a t) -> p a t", a=4)
            t6 = xn[:, 0, :].rearrange("p (a t) -> p a t", a=4)

            def chunks(z):
                return z.rearrange("p a (c t) -> p (a c) t", c=2)

            @block.vector
            def _(dve):
                V(dve, dve.tensor_scalar(aa[:, :, :], aa[:, :, :], 0.5, 0.5, ALU.mult, ALU.add))
                V(dve, dve.tensor_scalar(ld[:, :, :], ld[:, :, :], 1.0, -0.5 * E05, ALU.add, ALU.mult))
                for i in range(4):
                    V(dve, dve.tensor_scalar(kk[:, i, :], k[:, i, :], pc("rwkv_k_k", i), None, ALU.mult))
                m["kk2"] = done("dve", dve.tensor_tensor(t5, kk[:, :, :], kk[:, :, :], ALU.mult))
                src = ld
                for n in range(7):
                    dst = (sumA, sumB)[n % 2]
                    w = 1 << n
                    V(dve, dve.tensor_tensor(chunks(dst)[:, :, w:P], chunks(src)[:, :, w:P], chunks(src)[:, :, 0:P - w], ALU.add))
                    V(dve, dve.tensor_copy(chunks(dst)[:, :, 0:w], chunks(src)[:, :, 0:w]))
                    src = dst
                V(dve, dve.tensor_scalar(kh[:, :, :], aa[:, :, :], -1.0, None, ALU.add))
                for i in range(4):
                    V(dve, dve.tensor_scalar(kh[:, i, :], kh[:, i, :], pc("rwkv_k_a", i), 1.0, ALU.mult, ALU.add))
                V(dve, dve.tensor_tensor(kh[:, :, :], kh[:, :, :], k, ALU.mult))
                for i in range(4):
                    V(dve, dve.scalar_tensor_tensor(bonus[:, i, :], kh[:, i, :], pc("rwkv_r_k", i), r[:, i, :], ALU.mult, ALU.mult))
                m["rkr"] = chain["dve"]

            @block.tensor
            def _(pe):
                def head_sums(src, b):
                    for i in range(2):
                        ins = pe.matmul(bank[b + i][:, :], block_ones[:, :], flat(src[:, 2 * i:2 * i + 2, :]), start=True, stop=True)
                    return done("pe", ins)
                pe.wait_ge(dve_done, m["kk2"])
                m["kksum"] = head_sums(t5, 0)
                pe.wait_ge(dve_done, m["rkr"])
                m["rkrsum"] = head_sums(bonus, 2)

            def from_banks(b):
                return [(bank[b + i][:, :].rearrange("p (a t) -> p a t", a=2), slice(2 * i, 2 * i + 2)) for i in range(2)]

            @block.vector
            def _(dve):
                dve.wait_ge(pe_done, m["kksum"])
                for src, at in from_banks(0):
                    last = done("dve", dve.tensor_scalar(t5[:, at, :], src, 1e-24, None, ALU.max))
                m["kkmax"] = last

            @block.scalar
            def _(act):
                act.wait_ge(dve_done, m["kkmax"])
                m["kknorm"] = done("act", act.activation(t5, t5, ACT.Sqrt))

            L = sumA
            cmid = chunks(L)[:, :, P // 2 - 1]
            cend = chunks(L)[:, :, P - 1]
            lab = t6

            @block.vector
            def _(dve):
                V(dve, dve.tensor_copy(small[:, 8:16], cmid))
                V(dve, dve.tensor_tensor(small[:, 16:24], cend, small[:, 8:16], ALU.subtract))
                V(dve, dve.tensor_tensor(sumB.rearrange("p a (c t) -> p (a c) t", c=2), chunks(L),
                                         small[:, 8:16].unsqueeze(2).to_broadcast((P, 8, P)), ALU.subtract))
                s2 = small[:, 16:24].rearrange("p (a c) -> p a c", c=2)[:, :, 0]
                s1 = small[:, 8:16].rearrange("p (a c) -> p a c", c=2)[:, :, 1]
                V(dve, dve.tensor_tensor(small[:, 24:28], s2, s1, ALU.add))
                m["logs"] = done("dve", dve.tensor_tensor(lab, sumB[:, :, :], ld[:, :, :], ALU.subtract))
                dve.wait_ge(act_done, m["kknorm"])
                V(dve, dve.reciprocal(t5, t5))
                V(dve, dve.tensor_tensor(kk[:, :, :], kk[:, :, :], t5, ALU.mult))
                dve.wait_ge(pe_done, m["rkrsum"])
                for src, at in from_banks(2):
                    V(dve, dve.tensor_tensor(bonus[:, at, :], src, v[:, at, :], ALU.mult))

            @block.scalar
            def _(act):
                act.wait_ge(dve_done, m["logs"])
                act.activation(small[:, 28:32], small[:, 24:28], ACT.Exp)
                for c in range(2):
                    tok = slice(c * P, c * P + P)
                    act.activation(ar[:, :, c, 0:P], lab[:, :, tok], ACT.Exp)
                    act.activation(ar[:, :, c, P:2 * P], sumB[:, :, tok], ACT.Exp)
                m["exps"] = done("act", act.activation(bt[:, :, :], sumB[:, :, :], ACT.Exp, scale=-1.0))

            @block.vector
            def _(dve):
                dve.wait_ge(act_done, m["exps"])
                V(dve, dve.tensor_tensor(kt[:, :, :], bt[:, :, :], kh[:, :, :], ALU.mult))
                V(dve, dve.tensor_tensor(bt[:, :, :], bt[:, :, :], kk[:, :, :], ALU.mult))
                V(dve, dve.tensor_tensor(bt[:, :, :], bt[:, :, :], aa[:, :, :], ALU.mult))
                for c in range(2):
                    tok = slice(c * P, c * P + P)
                    V(dve, dve.scalar_tensor_tensor(ar[:, :, c, 0:P], ar[:, :, c, 0:P], -1.0, kk[:, :, tok], ALU.mult, ALU.mult))
                    V(dve, dve.tensor_tensor(ar[:, :, c, P:2 * P], ar[:, :, c, P:2 * P], r[:, :, tok], ALU.mult))
            end_phase()

            mm = piece(0, 8, 4, P)
            X = piece(4096, 8, P)
            XT = piece(5120, 8, P)
            ct = piece(6144, 8, P)
            ysb = piece(7168, 8, P)
            zs = piece(8192, HALF)
            us = piece(8704, HALF)
            s0 = piece(9216, 4, 64)
            yT = t5

            @block.gpsimd
            def _(pool):
                m["zero"] = done("pool", pool.memset(piece(0, 4096), 0.0))

            @block.tensor
            def _(pe):
                for j, src in ((0, bt), (1, kt)):
                    for i in range(4):
                        ins = pe.transpose(bank[6 + j][:, i * P:i * P + P], src[:, i, 0:P], ident[:, :])
                m["bkt"] = done("pe", ins)

            @block.scalar
            def _(act):
                act.wait_ge(pe_done, m["bkt"])
                act.activation(bktok[:, 0, :], bank[6][:, :], ACT.Copy)
                m["bktok"] = done("act", act.activation(bktok[:, 1, :], bank[7][:, :], ACT.Copy))

            heads = [(slice(64 * e, 64 * e + 64), i, slice((2 * i + e) * 64, (2 * i + e) * 64 + 64))
                     for e in range(2) for i in range(4)]
            for c in range(2):
                tok = slice(c * P, c * P + P)
                start = chain["dve"]

                @block.tensor
                def _(pe):
                    for e, (q, i, hv) in enumerate(heads):
                        if e >= 4:
                            pe.wait_ge(dve_done, start + e - 3)
                        pe.matmul(bank[e % 4][:, 0:2 * P], bt[q, i, tok], ar[q, i, c, :], start=True, stop=True)
                        done("pe", pe.matmul(bank[e % 4][:, 2 * P:4 * P], kt[q, i, tok], ar[q, i, c, :], start=True, stop=True))
                    for e, (q, i, hv) in enumerate(heads):
                        ins = pe.matmul(bank[4 + e // 4][:, i * P:i * P + P], ar[q, i, c, 0:P], bt[q, i, tok],
                                        start=True, stop=True)
                    done("pe", ins)

                pe0 = chain["pe"] - 9

                @block.gpsimd
                def _(pool):
                    for h in range(8):
                        pool.tensor_copy(X[:, h, :], ident[:, :])
                        ins = pool.tensor_copy(XT[:, h, :], ident[:, :])
                    m["eye"] = done("pool", ins)

                @block.vector
                def _(dve):
                    dve.wait_ge(pool_done, m["zero"])
                    mask = upper[:, :, :].bitcast(U32)
                    for h in range(8):
                        dve.wait_ge(pe_done, pe0 + h + 1)
                        for f in range(2):
                            ins = dve.copy_predicated(mm[:, h, 2 * f:2 * f + 2, :], mask, bank[h % 4][:, 2 * f * P:2 * f * P + 2 * P]
                                                      .rearrange("p (a b) -> p a b", a=2))
                        done("dve", ins)
                    m["mm"] = chain["dve"]
                    dve.wait_ge(pool_done, m["eye"])
                    dve.wait_ge(pe_done, pe0 + 9)
                    dve.wait_ge(dve_done, m["mm"])
                    for q in range(2):
                        g = slice(4 * q, 4 * q + 4)
                        done("dve", dve.copy_predicated(X[:, g, :], level0_t[:, :].bitcast(U32).unsqueeze(1).to_broadcast((P, 4, P)),
                                            bank[4 + q][:, :].rearrange("p (a b) -> p a b", a=4)))
                        m["x", q] = done("dve", dve.copy_predicated(XT[:, g, :], level[:, 0, :].bitcast(U32).unsqueeze(1).to_broadcast((P, 4, P)),
                                            mm[:, g, 0, :]))

                for l in range(1, 7):
                    @block.gpsimd
                    def _(pool):
                        for q in range(2):
                            g = slice(4 * q, 4 * q + 4)
                            if l == 1:
                                pool.wait_ge(dve_done, m["mm"])
                            else:
                                pool.wait_ge(pe_done, m["y", q])
                            m["c", q] = done("pool", pool.tensor_tensor(
                                out=ct[:, g, :], in0=mm[:, g, 0, :],
                                in1=level[:, l, :].unsqueeze(1).to_broadcast((P, 4, P)), op=ALU.mult))

                    @block.tensor
                    def _(pe):
                        for q in range(2):
                            pe.wait_ge(pool_done, m["c", q])
                            pe.wait_ge(dve_done, m["x", q])
                            for h in range(4):
                                ins = pe.matmul(bank[q][:, h * P:h * P + P], ct[:, 4 * q + h, :], X[:, 4 * q + h, :],
                                                start=True, stop=True)
                            m["y", q] = done("pe", ins)

                    @block.scalar
                    def _(act):
                        for q in range(2):
                            act.wait_ge(pe_done, m["y", q])
                            m["ys", q] = done("act", act.activation(
                                ysb[:, 4 * q:4 * q + 4, :], bank[q][:, :].rearrange("p (a b) -> p a b", a=4), ACT.Copy))

                    @block.tensor
                    def _(pe):
                        for q in range(2):
                            pe.wait_ge(act_done, m["ys", q])
                            for h in range(4):
                                e = 4 * q + h
                                if l < 6:
                                    pe.matmul(bank[2 + q][:, h * P:h * P + P], XT[:, e, :], ysb[:, e, :], start=True, stop=True)
                                ins = pe.matmul(bank[4 + q][:, h * P:h * P + P], ysb[:, e, :], XT[:, e, :], start=True, stop=True)
                            m["dx", q] = done("pe", ins)

                    @block.vector
                    def _(dve):
                        for q in range(2):
                            g = slice(4 * q, 4 * q + 4)
                            dve.wait_ge(pe_done, m["dx", q])
                            if l < 6:
                                done("dve", dve.tensor_tensor(X[:, g, :], bank[2 + q][:, :].rearrange("p (a b) -> p a b", a=4),
                                                              X[:, g, :], ALU.add))
                            m["x", q] = done("dve", dve.tensor_tensor(
                                XT[:, g, :], bank[4 + q][:, :].rearrange("p (a b) -> p a b", a=4), XT[:, g, :], ALU.add))

                @block.tensor
                def _(pe):
                    for e, (q, i, hv) in enumerate(heads):
                        o = bank[6 * (e // 4)][:, i * 64:i * 64 + 64]
                        ins = pe.matmul(o, mm[:, e, 2, :], vtok[:, c, hv], start=True, stop=(c == 0))
                        if c == 1:
                            ins = pe.matmul(o, ar[q, i, c, 0:P], s0[q, i, :], start=False, stop=True)
                    m["z"] = done("pe", ins)

                @block.scalar
                def _(act):
                    act.wait_ge(pe_done, m["z"])
                    act.activation(zs[:, 0:256], bank[0][:, 0:256], ACT.Copy)
                    m["zs"] = done("act", act.activation(zs[:, 256:512], bank[6][:, 0:256], ACT.Copy))

                @block.tensor
                def _(pe):
                    pe.wait_ge(act_done, m["zs"])
                    pe.wait_ge(dve_done, m["x", 1])
                    for e in range(8):
                        ins = pe.matmul(bank[1][:, e * 64:e * 64 + 64], XT[:, e, :], zs[:, e * 64:e * 64 + 64], start=True, stop=True)
                    m["u"] = done("pe", ins)

                @block.scalar
                def _(act):
                    act.wait_ge(pe_done, m["u"])
                    m["us"] = done("act", act.activation(us[:, :], bank[1][:, :], ACT.Copy))

                @block.tensor
                def _(pe):
                    pe.wait_ge(act_done, m["us"])
                    for e, (q, i, hv) in enumerate(heads):
                        o = bank[2 + e // 4][q, i * P:i * P + P]
                        ue = us[:, e * 64:e * 64 + 64]
                        pe.matmul(o, ue, mm[:, e, 1, :], start=True, stop=False)
                        ins = pe.matmul(o, vtok[:, c, hv], mm[:, e, 3, :], start=False, stop=(c == 0))
                        if c == 1:
                            ins = pe.matmul(o, s0[q, i, :], ar[q, i, c, P:2 * P], start=False, stop=True)
                    m["y"] = done("pe", ins)
                    if c == 0:
                        for e, (q, i, hv) in enumerate(heads):
                            o = bank[4 + e // 4][q, i * 64:i * 64 + 64]
                            pe.matmul(o, bktok[:, 0, hv], us[:, e * 64:e * 64 + 64], start=True, stop=False)
                            ins = pe.matmul(o, bktok[:, 1, hv], vtok[:, c, hv], start=False, stop=True)
                        m["s"] = done("pe", ins)

                @block.vector
                def _(dve):
                    dve.wait_ge(pe_done, m["y"])
                    for e in range(2):
                        q = slice(64 * e, 64 * e + 64)
                        dve.tensor_copy(yT[q, :, tok], bank[2 + e][q, :].rearrange("p (a b) -> p a b", a=4))
                    if c == 0:
                        dve.wait_ge(pe_done, m["s"])
                        for i in range(4):
                            for e in range(2):
                                q = slice(64 * e, 64 * e + 64)
                                dve.tensor_scalar(s0[q, i, :], bank[4 + e][q, i * 64:i * 64 + 64], small[q, 28 + i:29 + i], None, ALU.mult)
                end_phase()

            sq = piece(0, 4, T)
            rs = piece(1024, 4, T)

            @block.tensor
            def _(pe):
                for i in range(2):
                    ins = pe.matmul(bank[i][:, :], block_ones[:, :], flat(yT[:, 2 * i:2 * i + 2, :]), start=True, stop=True)
                m["mu"] = done("pe", ins)

            @block.vector
            def _(dve):
                dve.wait_ge(pe_done, m["mu"])
                for src, at in from_banks(0):
                    V(dve, dve.scalar_tensor_tensor(yT[:, at, :], src, -1.0 / 64, yT[:, at, :], ALU.mult, ALU.add))
                m["sq"] = done("dve", dve.tensor_tensor(sq[:, :, :], yT, yT, ALU.mult))

            @block.tensor
            def _(pe):
                pe.wait_ge(dve_done, m["sq"])
                for i in range(2):
                    ins = pe.matmul(bank[2 + i][:, :], block_ones[:, :], flat(sq[:, 2 * i:2 * i + 2, :]), start=True, stop=True)
                m["var"] = done("pe", ins)

            @block.vector
            def _(dve):
                dve.wait_ge(pe_done, m["var"])
                for src, at in from_banks(2):
                    m["ve"] = done("dve", dve.tensor_scalar(rs[:, at, :], src, 1.0 / 64, 64e-5, ALU.mult, ALU.add))

            @block.scalar
            def _(act):
                act.wait_ge(dve_done, m["ve"])
                m["sd"] = done("act", act.activation(rs[:, :, :], rs[:, :, :], ACT.Sqrt))

            @block.vector
            def _(dve):
                dve.wait_ge(act_done, m["sd"])
                V(dve, dve.reciprocal(rs[:, :, :], rs[:, :, :]))
                V(dve, dve.tensor_tensor(yT, yT, rs[:, :, :], ALU.mult))
                for i in range(4):
                    V(dve, dve.tensor_scalar(yT[:, i, :], yT[:, i, :], pc("rwkv_ln_w", i), pc("rwkv_ln_b", i), ALU.mult, ALU.add))
                V(dve, dve.tensor_tensor(yT, yT, bonus[:, :, :], ALU.add))
                m["yg"] = done("dve", dve.tensor_tensor(yT, yT, gate[:, :, :], ALU.mult))
            split_act(yT, 4, 4, m["yg"])
            end_phase()
            out_proj(a["even_w_out"][0], 1.0)

        def mla():
            H, NOPE, ROPE, QR, KVR = 8, 128, 64, 384, 256
            QK = NOPE + ROPE
            m = {}
            qn = piece(0, NT, H, NOPE)
            qr = piece(2048, NT, H, ROPE)
            kn = piece(3072, NT, H, NOPE)
            kr = piece(5120, NT, H, ROPE)
            vv = piece(6144, NT, H, NOPE)
            cp = piece(8192, NT, 704)
            qnT = piece(9600, H, T)
            knT = piece(11648, H, T)
            qrT = piece(13696, H // 2, T)
            krT = piece(14720, H // 2, T)
            pr = piece(15744, 2, 3 * P)
            prT = piece(16512, 2, 3 * P)
            mask = piece(17280, 3 * P)
            rope_g = piece(17664, 2, ROPE)
            cs = piece(17792, 2, NT, ROPE // 2)
            stats = piece(17920, 2, NT, H)
            work = xn[:, :, :]
            misc_loaded = sem("mla_loaded")

            @block.gpsimd
            def _(pool):
                G(pool, pool.memset(mask, 0.0))
                for c in (0, 2):
                    v = mask[:, c * P:c * P + P]
                    ins = pool.affine_select(out=v, in_=v, compare_op=ALU.is_ge, fill=-1e30, base=0,
                                             pattern=[[-1, P]], channel_multiplier=1)
                m["mask"] = done("pool", ins)

            pos_i = small[:, 0:2].bitcast(I32)
            ang = work[:, 0, 0:64]
            turns = work[:, 0, 64:128]
            freq = work[:, 0, 128:160]
            arg = work[:, 0, 192:320]

            @block.gpsimd
            def _(pool):
                for i, n in enumerate(("mla_q_norm", "mla_k_norm")):
                    pool.dma_start(rope_g[:, i, :], a[n][0:1, NOPE:QK].to_broadcast((P, ROPE))).then_inc(misc_loaded, 16)
                pool.dma_start(freq, a["c_inv_freq"].to_broadcast((P, 32))).then_inc(misc_loaded, 16)
                pool.dma_start(pos_i, a["positions"][0].rearrange("(t p) -> p t", p=P),
                             allow_slow_non_contiguous=True).then_inc(misc_loaded, 16)

            @block.vector
            def _(dve):
                dve.wait_ge(misc_loaded, 64)
                V(dve, dve.tensor_copy(small[:, 2:4], pos_i))
                for t in range(NT):
                    V(dve, dve.tensor_scalar(ang[:, t * 32:t * 32 + 32], freq, small[:, 2 + t:3 + t], None, ALU.mult))
                V(dve, dve.tensor_scalar(turns, ang, 1.0 / (2 * math.pi), None, ALU.mult))
                V(dve, dve.tensor_scalar(turns, turns, 12582912.0, None, ALU.add))
                V(dve, dve.tensor_scalar(turns, turns, -12582912.0, None, ALU.add))
                c1 = 6.28125
                c2 = round((2 * math.pi - c1) * 2 ** 21) / 2 ** 21
                c3 = 2 * math.pi - c1 - c2
                for c in (c1, c2, c3):
                    V(dve, dve.scalar_tensor_tensor(ang, turns, -c, ang, ALU.mult, ALU.add))
                V(dve, dve.tensor_scalar(ang, ang, 3.1415925, -3.1415925, ALU.min, ALU.max))
                V(dve, dve.tensor_copy(arg[:, 64:128], ang))
                V(dve, dve.scalar_tensor_tensor(ang, ang, -1.0, ang, ALU.mult, ALU.min))
                m["arg"] = done("dve", dve.tensor_scalar(arg[:, 0:64], ang, math.pi / 2, None, ALU.add))

            @block.scalar
            def _(act):
                act.wait_ge(dve_done, m["arg"])
                act.activation(cs[:, :, :, :], arg.rearrange("p (a b c) -> p a b c", a=2, b=2), ACT.Sin)

            ready = proj_rows(a["odd_w_in"][0], KC, 704)

            @block.scalar
            def _(act):
                act.wait_ge(a_used, ready)
                for t in range(NT):
                    act.activation(cp[:, t, 0:HALF], bank[2 * t][:, :], ACT.Copy)
                    m["cp"] = done("act", act.activation(cp[:, t, HALF:704], bank[2 * t + 1][:, 0:192], ACT.Copy))
                act.wait_ge(act_done, m["cp"])
                for t in range(NT):
                    act.activation(work[:, 0, 0:QR], cp[:, t, 0:QR], ACT.Square, accum_out=small[:, t:t + 1])
                    A(act, act.activation(work[:, 1, 0:KVR], cp[:, t, QR:QR + KVR], ACT.Square, accum_out=small[:, 2 + t:3 + t]))
                m["ss"] = chain["act"]

            @block.vector
            def _(dve):
                dve.wait_ge(act_done, m["ss"])
                dve.tensor_scalar(small[:, 0:2], small[:, 0:2], 1.0 / QR, RMS_EPS, ALU.mult, ALU.add)
                m["ms"] = done("dve", dve.tensor_scalar(small[:, 2:4], small[:, 2:4], 1.0 / KVR, RMS_EPS, ALU.mult, ALU.add))

            @block.gpsimd
            def _(pool):
                pool.wait_ge(dve_done, m["ms"])
                m["rs"] = done("pool", pool.tensor_tensor(out=small[:, 4:8], in0=small[:, 0:4], in1=neg_half[:, 0:4], op=ALU.pow))

            @block.vector
            def _(dve):
                dve.wait_ge(pool_done, m["rs"])
                for t in range(NT):
                    dve.tensor_scalar(work[:, t, 0:QR], cp[:, t, 0:QR], small[:, 4 + t:5 + t], None, ALU.mult)
                    dve.tensor_scalar(work[:, t, QR:QR + KVR], cp[:, t, QR:QR + KVR], small[:, 6 + t:7 + t], None, ALU.mult)
            end_phase()
            transpose_split(lambda t, k: work[:, t, k * P:k * P + P],
                            lambda k: pc("q_a", k) if k < 3 else pc("kv_a", k - 3), nk=5)

            wq, wkv = a["mla_w_q_up"][0], a["mla_w_kv_up"][0]
            for g in range(2):
                heads4 = slice(4 * g, 4 * g + 4)
                ready_q = proj_rows(wq[:, g * 768:g * 768 + 768], 3, 768)

                @block.scalar
                def _(act):
                    act.wait_ge(a_used, ready_q)
                    for t in range(NT):
                        act.activation(work[:, t, 0:HALF], bank[2 * t][:, :], ACT.Copy)
                        m["qs"] = done("act", act.activation(work[:, t, HALF:768], bank[2 * t + 1][:, 0:256], ACT.Copy))

                @block.vector
                def _(dve):
                    dve.wait_ge(act_done, m["qs"])
                    for t in range(NT):
                        src = work[:, t, 0:768].rearrange("p (h c) -> p h c", h=4)
                        dve.tensor_copy(qn[:, t, heads4, :], src[:, :, 0:NOPE])
                        dve.tensor_copy(qr[:, t, heads4, :], src[:, :, NOPE:QK])
                end_phase()
                ready_kv = proj_rows(wkv[:, g * D:g * D + D], 2, D, k0=3)

                @block.scalar
                def _(act):
                    act.wait_ge(a_used, ready_kv)
                    for t in range(NT):
                        for h in range(2):
                            src = bank[2 * t + h][:, :].rearrange("p (h c) -> p h c", h=2)
                            two = slice(4 * g + 2 * h, 4 * g + 2 * h + 2)
                            act.activation(kn[:, t, two, :], src[:, :, 0:NOPE], ACT.Copy)
                            act.activation(vv[:, t, two, :], src[:, :, NOPE:2 * NOPE], ACT.Copy)
                end_phase()

            sqr = work

            @block.vector
            def _(dve):
                pe_sq = sqr[:, 0, 0:ROPE]
                for t in range(NT):
                    s8 = sqr[:, 0, :].rearrange("p (h c) -> p h c", h=H)
                    r8 = sqr[:, 1, 0:H * ROPE].rearrange("p (h c) -> p h c", h=H)
                    V(dve, dve.tensor_tensor(s8, qn[:, t, :, :], qn[:, t, :, :], ALU.mult))
                    V(dve, dve.tensor_tensor(r8, qr[:, t, :, :], qr[:, t, :, :], ALU.mult))
                    V(dve, dve.tensor_reduce(stats[:, 0, t, :], s8, AX.X, ALU.add))
                    V(dve, dve.tensor_reduce(small[:, 8:16], r8, AX.X, ALU.add))
                    V(dve, dve.tensor_tensor(stats[:, 0, t, :], stats[:, 0, t, :], small[:, 8:16], ALU.add))
                    V(dve, dve.tensor_tensor(s8, kn[:, t, :, :], kn[:, t, :, :], ALU.mult))
                    V(dve, dve.tensor_tensor(r8[:, 0, :], cp[:, t, 640:704], cp[:, t, 640:704], ALU.mult))
                    V(dve, dve.tensor_reduce(stats[:, 1, t, :], s8, AX.X, ALU.add))
                    V(dve, dve.tensor_reduce(small[:, 16:17], r8[:, 0, :], AX.X, ALU.add))
                    V(dve, dve.tensor_scalar(stats[:, 1, t, :], stats[:, 1, t, :], small[:, 16:17], None, ALU.add))
                m["hs"] = done("dve", dve.tensor_scalar(stats[:, :, :, :], stats[:, :, :, :], 1.0 / QK, RMS_EPS, ALU.mult, ALU.add))

            @block.gpsimd
            def _(pool):
                pool.wait_ge(dve_done, m["hs"])
                m["hr"] = done("pool", pool.tensor_tensor(
                    out=stats.rearrange("p a b c -> p (a b c)"), in0=stats.rearrange("p a b c -> p (a b c)"),
                    in1=neg_half[:, 0:2 * NT * H], op=ALU.pow))

            @block.vector
            def _(dve):
                dve.wait_ge(pool_done, m["hr"])
                hr = ROPE // 2
                for t in range(NT):
                    rq = stats[:, 0, t, :].unsqueeze(2)
                    rk = stats[:, 1, t, :].unsqueeze(2)
                    dve.tensor_tensor(qn[:, t, :, :], qn[:, t, :, :], rq.to_broadcast((P, H, NOPE)), ALU.mult)
                    dve.tensor_tensor(kn[:, t, :, :], kn[:, t, :, :], rk.to_broadcast((P, H, NOPE)), ALU.mult)
                    V(dve, dve.tensor_tensor(qr[:, t, :, :], qr[:, t, :, :], rq.to_broadcast((P, H, ROPE)), ALU.mult))
                    V(dve, dve.tensor_tensor(qr[:, t, :, :], qr[:, t, :, :],
                                             rope_g[:, 0, :].unsqueeze(1).to_broadcast((P, H, ROPE)), ALU.mult))
                    V(dve, dve.tensor_tensor(cp[:, t, 640:704], cp[:, t, 640:704], rope_g[:, 1, :], ALU.mult))
                    V(dve, dve.tensor_tensor(kr[:, t, :, :], cp[:, t, 640:704].unsqueeze(1).to_broadcast((P, H, ROPE)),
                                             rk.to_broadcast((P, H, ROPE)), ALU.mult))
                    for z in (qr, kr):
                        t1, t2 = z[:, t, :, 0:hr], z[:, t, :, hr:ROPE]
                        cos = cs[:, 0, t, :].unsqueeze(1).to_broadcast((P, H, hr))
                        sin = cs[:, 1, t, :].unsqueeze(1).to_broadcast((P, H, hr))
                        w = sqr[:, 0, :].rearrange("p (a h c) -> p a h c", a=4, h=H)
                        dve.tensor_tensor(w[:, 0, :, :], t1, cos, ALU.mult)
                        dve.tensor_tensor(w[:, 1, :, :], t2, sin, ALU.mult)
                        dve.tensor_tensor(w[:, 2, :, :], t2, cos, ALU.mult)
                        V(dve, dve.tensor_tensor(w[:, 3, :, :], t1, sin, ALU.mult))
                        dve.tensor_tensor(t1, w[:, 0, :, :], w[:, 1, :, :], ALU.subtract)
                        V(dve, dve.tensor_tensor(t2, w[:, 2, :, :], w[:, 3, :, :], ALU.add))
            end_phase()

            jobs = []
            for z, zT, gain in ((qn, qnT, "qn"), (kn, knT, "kn")):
                for h in range(0, H, 2):
                    jobs.append((lambda t, e, z=z, h=h: z[:, t, h + e, :], zT[:, h:h + 2, :], gain))
            for z, zT in ((qr, qrT), (kr, krT)):
                for h in range(0, H // 2, 2):
                    jobs.append((lambda t, e, z=z, h=h: z[:, t, 2 * (h + e):2 * (h + e) + 2, :].rearrange("p a b -> p (a b)"),
                                 zT[:, h:h + 2, :], None))
            pe0, act0 = chain["pe"], chain["act"]

            @block.tensor
            def _(pe):
                for n, (src, dst, gain) in enumerate(jobs):
                    if n >= 4:
                        pe.wait_ge(act_done, act0 + n - 3)
                    for e in range(2):
                        for t in range(NT):
                            ins = pe.transpose(bank[n % 4][:, e * T + t * P:e * T + t * P + P], src(t, e), ident[:, :])
                    done("pe", ins)

            @block.scalar
            def _(act):
                for n, (src, dst, gain) in enumerate(jobs):
                    act.wait_ge(pe_done, pe0 + n + 1)
                    done("act", act.activation(dst, bank[n % 4][:, :].rearrange("p (a t) -> p a t", a=2), ACT.Copy,
                                               scale=pc(gain) if gain else 1.0))
            end_phase()

            scale = QK ** -0.5
            parts = ((slice(0, P), 0, 1), (slice(P, 3 * P), 1, 2))

            def scores(h):
                @block.tensor
                def _(pe):
                    if h >= 2:
                        pe.wait_ge(dve_done, m["max", h - 2])
                    b, q = bank[h % 2], slice(64 * (h % 2), 64 * (h % 2) + 64)
                    for cols, t, n in parts:
                        tok = slice(t * P, t * P + P)
                        pe.matmul(b[:, cols], qnT[:, h, tok], knT[:, h, 0:n * P], start=True, stop=False)
                        ins = pe.matmul(b[:, cols], qrT[q, h // 2, tok], krT[q, h // 2, 0:n * P], start=False, stop=True)
                    m["s", h] = done("pe", ins)

                @block.vector
                def _(dve):
                    if h == 0:
                        dve.wait_ge(pool_done, m["mask"])
                    dve.wait_ge(pe_done, m["s", h])
                    if h >= 2:
                        dve.wait_ge(pe_done, m["t", h - 2])
                    c = 32 + 8 * (h % 2)
                    for cols, t, n in parts:
                        m["max", h] = done("dve", dve.tensor_tensor_reduce(
                            out=pr[:, h % 2, cols], in0=bank[h % 2][:, cols], in1=mask[:, cols], scale=1.0, scalar=-3e38,
                            op0=ALU.add, op1=ALU.max, accum_out=small[:, c + t:c + t + 1]))
                    dve.wait_ge(dve_done, m["max", h])
                    m["nb", h] = done("dve", dve.tensor_scalar(small[:, c + 2:c + 4], small[:, c:c + 2], -scale, None, ALU.mult))

                @block.scalar
                def _(act):
                    act.wait_ge(dve_done, m["nb", h])
                    c = 32 + 8 * (h % 2)
                    for cols, t, n in parts:
                        m["e", h] = done("act", act.activation(pr[:, h % 2, cols], pr[:, h % 2, cols], ACT.Exp, scale=scale,
                                                               bias=small[:, c + 2 + t:c + 3 + t],
                                                               accum_out=small[:, c + 4 + t:c + 5 + t]))

                @block.vector
                def _(dve):
                    dve.wait_ge(act_done, m["e", h])
                    c = 32 + 8 * (h % 2)
                    V(dve, dve.reciprocal(small[:, c + 6:c + 8], small[:, c + 4:c + 6]))
                    for cols, t, n in parts:
                        m["p", h] = done("dve", dve.tensor_scalar(pr[:, h % 2, cols], pr[:, h % 2, cols],
                                                                  small[:, c + 6 + t:c + 7 + t], None, ALU.mult))

            def turn(h):
                @block.tensor
                def _(pe):
                    pe.wait_ge(dve_done, m["p", h])
                    if h >= 2:
                        pe.wait_ge(act_done, m["pt", h - 2])
                    for j in range(3):
                        ins = pe.transpose(bank[2 + h % 2][:, j * P:j * P + P], pr[:, h % 2, j * P:j * P + P], ident[:, :])
                    m["t", h] = done("pe", ins)

                @block.scalar
                def _(act):
                    act.wait_ge(pe_done, m["t", h])
                    if h >= 2:
                        act.wait_ge(pe_done, m["o", h - 2])
                    m["pt", h] = done("act", act.activation(prT[:, h % 2, :], bank[2 + h % 2][:, 0:3 * P], ACT.Copy))

            def values(h):
                @block.tensor
                def _(pe):
                    pe.wait_ge(act_done, m["pt", h])
                    if h >= 2:
                        pe.wait_ge(dve_done, m["lo", h - 2])
                    b = bank[4 + h % 2]
                    pe.matmul(b[:, 0:T], vv[:, 0, h, :], prT[:, h % 2, 0:T], start=True, stop=False)
                    m["o", h] = done("pe", pe.matmul(b[:, P:T], vv[:, 1, h, :], prT[:, h % 2, T:3 * P], start=False, stop=True))

                @block.scalar
                def _(act):
                    act.wait_ge(pe_done, m["o", h])
                    m["hi", h] = done("act", act.activation(act_hi[:, h, :], bank[4 + h % 2][:, 0:T], ACT.Copy))

                @block.vector
                def _(dve):
                    dve.wait_ge(act_done, m["hi", h])
                    m["lo", h] = done("dve", dve.tensor_tensor(act_lo[:, h, :], bank[4 + h % 2][:, 0:T],
                                                               act_hi[:, h, :].bitcast(F32), ALU.subtract))

            for i in range(H + 2):
                if i < H:
                    scores(i)
                if 1 <= i <= H:
                    turn(i - 1)
                if i >= 2:
                    values(i - 2)
            end_phase()
            out_proj(a["odd_w_out"][0], 1.0)

        nsa_loaded = sem("nsa_loaded")

        def nsa_weights():
            w1, bias8, w2 = piece(8192, 2, 16, P), piece(13408, 16, T), piece(17942, 2, 64)

            @block.gpsimd
            def _(pool):
                pool.wait_ge(bias_stored, 16)
                for i in range(2):
                    pool.dma_start(w1[:, i, :, :], a["nsa_cmp_w1_2"][0, i].rearrange("(j l) d e -> (l d) j e", l=2)
                                   ).then_inc(nsa_loaded, 16)
                    pool.dma_start(w2[:, i, :], a["nsa_cmp_w2_2"][0, i]).then_inc(nsa_loaded, 16)
                pool.dma_start(bias8[:, :, :], bass.AP(scratch, P - 1, [[512, P], [P * 512, 16], [1, T]])
                               ).then_inc(nsa_loaded, 16)

        def nsa():
            G4, HD, NQ, NCMP = 4, 64, 16, T // 16 - 1
            m = {}
            pT = piece(0, 16, T)
            kd = piece(4096, 2, G4, T)
            z = piece(6144, 2, G4, T)
            w1 = piece(8192, 2, 16, P)
            vt = piece(12288, 2, NT, T)
            gates = piece(13312, NT, 48)
            bias8 = piece(13408, NQ, T)
            hid = piece(17504, 2, G4 * NCMP)
            kcd = piece(17624, G4 * NCMP)
            vc = piece(17684, T)
            hb = piece(17940, 2)
            w2 = piece(17942, 2, HD)
            pr = piece(8192, 2, 2, 512)
            prT = piece(10240, 2, 2, 512)
            w = a["nsa_w_in_2"][0]

            proj_T(lambda i, s, u: cols_dyn(w, i, s, u), 6, lambda i, s: pT[:, bass.ds(i * 4 + 2 * s, 2), :])
            c_ks, c_kw = 1536, 2048
            proj_T(lambda i, s, u: w[:, (c_ks, c_kw)[s] + u * P:(c_ks, c_kw)[s] + u * P + P].rearrange("(k p) n -> p k n", p=P),
                   2, lambda i, s: pT[:, 12 + 2 * s:14 + 2 * s, :])
            ready = proj_rows(w[:, 1792:2608], KC, 816, parts=((0, 256), (512, 816)))

            @block.scalar
            def _(act):
                act.wait_ge(a_used, ready)
                for t in range(NT):
                    act.activation(vt[:, 0, t, :], bank[2 * t][:, 0:T], ACT.Copy)
                    act.activation(vt[:, 1, t, :], bank[2 * t + 1][:, 0:T], ACT.Copy)
                    m["g"] = done("act", act.activation(gates[:, t, :], bank[2 * t + 1][:, T:T + 48], ACT.Tanh, scale=0.5))

            @block.vector
            def _(dve):
                dve.wait_ge(act_done, m["g"])
                dve.tensor_scalar(gates[:, :, :], gates[:, :, :], 0.5, 0.5, ALU.mult, ALU.add)
            end_phase()

            @block.scalar
            def _(act):
                for b in range(2):
                    for e in range(2):
                        src = pT[64 * e:64 * e + 64, 12 + 2 * b:14 + 2 * b, :]
                        for f in range(2):
                            act.activation(kd[64 * f:64 * f + 64, b, e:G4:2, :], src, ACT.Copy)

            @block.vector
            def _(dve):
                for b in range(2):
                    for e in range(2):
                        src = pT[64 * e:64 * e + 64, 8 + 2 * b:10 + 2 * b, :]
                        dve.tensor_copy(z[0:64, b, e:G4:2, :], src)
                        m["z"] = done("dve", dve.tensor_copy(z[64:P, b, e:G4:2, 0:T - 1], src[:, :, 1:T]))

            @block.tensor
            def _(pe):
                pe.wait_ge(nsa_loaded, 80)
                pe.wait_ge(dve_done, m["z"])
                for b in range(2):
                    for j in range(16):
                        pe.matmul(bank[b][:, 0:G4 * NCMP].rearrange("p (g n) -> p g n", g=G4), w1[:, b, j, :],
                                  z[:, b, :, 2 * j:2 * j + 16 * (NCMP - 1) + 1:16], start=(j == 0), stop=(j == 15))
                for b in range(2):
                    for j in range(16):
                        ins = pe.matmul(bank[2][:, b:b + 1], w1[:, b, j, :], pc("cmp_pos", 16 * b + j),
                                        start=(j == 0), stop=(j == 15))
                m["hid"] = done("pe", ins)

            @block.scalar
            def _(act):
                act.wait_ge(pe_done, m["hid"])
                A(act, act.activation(hb[:, :], bank[2][:, 0:2], ACT.Copy))
                for b in range(2):
                    m["gelu"] = done("act", act.activation(hid[:, b, :], bank[b][:, 0:G4 * NCMP], ACT.Gelu_apprx_tanh,
                                                           bias=hb[:, b:b + 1]))

            @block.tensor
            def _(pe):
                pe.wait_ge(act_done, m["gelu"])
                for f in range(2):
                    pe.matmul(bank[3][64 * f:64 * f + 64, 0:G4 * NCMP], w2[:, 0, :], hid[:, 0, :], start=True, stop=True)
                for g in range(G4):
                    ins = pe.matmul(bank[4][0:NCMP, g * HD:g * HD + HD], hid[:, 1, g * NCMP:g * NCMP + NCMP], w2[:, 1, :],
                                    start=True, stop=True)
                m["kc"] = done("pe", ins)

            @block.scalar
            def _(act):
                act.wait_ge(pe_done, m["kc"])
                act.activation(kcd[:, :], bank[3][:, 0:G4 * NCMP], ACT.Copy)
                act.activation(vc[0:NCMP, :], bank[4][0:NCMP, 0:T], ACT.Copy)
            end_phase()

            scale = HD ** -0.5
            n0 = 7
            c0 = 3 * P
            full = ((slice(0, P), 0, slice(P, 2 * P)), (slice(P, 3 * P), 1, slice(0, 2 * P)))
            comp = ((slice(c0, c0 + n0), 0, slice(P + 31, T, 16), n0), (slice(c0 + n0, c0 + n0 + NCMP), 1, slice(31, T, 16), NCMP))

            def rows(h):
                for t in range(NT):
                    cols, _, bcols = full[t]
                    ccols, _, cb, n = comp[t]
                    yield 3 * t + 0, 0, ccols, bias8[:, h, cb]
                    yield 3 * t + 1, 0, cols, bias8[:, h, bcols]
                    yield 3 * t + 2, 1, cols, bias8[:, h, bcols]

            def scores(h):
                g, q = h // 4, slice(64 * (h % 2), 64 * (h % 2) + 64)
                c = 64 + 32 * (h % 2)
                mx, nb, sm, co = (small[:, c + 6 * i:c + 6 * i + 6] for i in range(4))

                @block.tensor
                def _(pe):
                    if h >= 2:
                        pe.wait_ge(dve_done, m["max", h - 2])
                    for b in range(2):
                        for cols, t, _ in full:
                            ins = pe.matmul(bank[2 * b + h % 2][:, cols], pT[q, h // 2, t * P:t * P + P],
                                            kd[q, b, g, 0:t * P + P], start=True, stop=True)
                    for cols, t, _, n in comp:
                        ins = pe.matmul(bank[h % 2][:, cols], pT[q, h // 2, t * P:t * P + P],
                                        kcd[q, g * NCMP:g * NCMP + n], start=True, stop=True)
                    m["s", h] = done("pe", ins)

                @block.vector
                def _(dve):
                    dve.wait_ge(pe_done, m["s", h])
                    if h >= 2:
                        dve.wait_ge(pe_done, m["t", h - 2])
                    for i, b, cols, bias in rows(h):
                        m["max", h] = done("dve", dve.tensor_tensor_reduce(
                            out=pr[:, h % 2, b, cols], in0=bank[2 * b + h % 2][:, cols], in1=bias, scale=1.0, scalar=-3e38,
                            op0=ALU.add, op1=ALU.max, accum_out=mx[:, i:i + 1]))
                    dve.wait_ge(dve_done, m["max", h])
                    m["nb", h] = done("dve", dve.tensor_scalar(nb, mx, -scale, None, ALU.mult))

                @block.scalar
                def _(act):
                    act.wait_ge(dve_done, m["nb", h])
                    for i, b, cols, bias in rows(h):
                        m["e", h] = done("act", act.activation(pr[:, h % 2, b, cols], pr[:, h % 2, b, cols], ACT.Exp, scale=scale,
                                                               bias=nb[:, i:i + 1], accum_out=sm[:, i:i + 1]))

                @block.vector
                def _(dve):
                    dve.wait_ge(act_done, m["e", h])
                    V(dve, dve.reciprocal(co, sm))
                    V(dve, dve.tensor_tensor(co.rearrange("p (t b) -> p t b", t=2), co.rearrange("p (t b) -> p t b", t=2),
                                             gates[:, :, 3 * h:3 * h + 3], ALU.mult))
                    V(dve, dve.tensor_scalar(co[:, 0:1], co[:, 0:1], seen[:, 0:1], None, ALU.mult))
                    for i, b, cols, bias in rows(h):
                        m["p", h] = done("dve", dve.tensor_scalar(pr[:, h % 2, b, cols], pr[:, h % 2, b, cols], co[:, i:i + 1], None, ALU.mult))

            def turn(h):
                @block.tensor
                def _(pe):
                    pe.wait_ge(dve_done, m["p", h])
                    if h >= 1:
                        pe.wait_ge(act_done, m["pt", h - 1])
                    for b in range(2):
                        for j in range(3):
                            pe.transpose(bank[4 + b][:, j * P:j * P + P], pr[:, h % 2, b, j * P:j * P + P], ident[:, :])
                    for cols, t, _, n in comp:
                        ins = pe.transpose(bank[4 + t][0:n, c0:c0 + P], pr[:, h % 2, 0, cols], ident[:, :])
                    m["t", h] = done("pe", ins)

                @block.scalar
                def _(act):
                    act.wait_ge(pe_done, m["t", h])
                    if h >= 2:
                        act.wait_ge(pe_done, m["o", h - 2])
                    for b, n in ((0, n0), (1, NCMP)):
                        act.activation(prT[:, h % 2, b, 0:c0], bank[4 + b][:, 0:c0], ACT.Copy)
                        m["pt", h] = done("act", act.activation(prT[0:n, h % 2, b, c0:c0 + P], bank[4 + b][0:n, c0:c0 + P], ACT.Copy))
                    act.wait_ge(act_done, m["pt", h])

            def values(h):
                g, q = h // 4, slice(64 * (h % 2), 64 * (h % 2) + 64)
                gv = slice(g * HD, g * HD + HD)

                @block.tensor
                def _(pe):
                    pe.wait_ge(act_done, m["pt", h])
                    if h >= 2:
                        pe.wait_ge(dve_done, m["lo", h - 2])
                    o = bank[6 + h % 2]
                    for b in range(2):
                        pe.matmul(o[q, 0:T], vt[:, b, 0, gv], prT[:, h % 2, b, 0:T], start=(b == 0), stop=False)
                        pe.matmul(o[q, P:T], vt[:, b, 1, gv], prT[:, h % 2, b, T:3 * P], start=False, stop=False)
                    for t, n in ((0, n0), (1, NCMP)):
                        ins = pe.matmul(o[q, t * P:t * P + P], vc[0:n, gv], prT[0:n, h % 2, t, c0:c0 + P], start=False, stop=(t == 1))
                    m["o", h] = done("pe", ins)

                @block.scalar
                def _(act):
                    act.wait_ge(pe_done, m["o", h])
                    m["hi", h] = done("act", act.activation(act_hi[q, h // 2, :], bank[6 + h % 2][q, 0:T], ACT.Copy))

                @block.vector
                def _(dve):
                    dve.wait_ge(act_done, m["hi", h])
                    m["lo", h] = done("dve", dve.tensor_tensor(act_lo[q, h // 2, :], bank[6 + h % 2][q, 0:T],
                                                               act_hi[q, h // 2, :].bitcast(F32), ALU.subtract))

            for i in range(NQ + 2):
                if i < NQ:
                    scores(i)
                if 1 <= i <= NQ:
                    turn(i - 1)
                if i >= 2:
                    values(i - 2)
            end_phase()
            out_proj(a["nsa_w_out_2"][0], 1.0 / ALPHA)
            layer_norm(0, 1)

        def hgrn():
            H = 8
            m = {}
            q = piece(0, H, T)
            k = piece(2048, H, T)
            f = piece(4096, H, T)
            gz = piece(6144, H, T)
            v = piece(8192, NT, D)
            at = piece(10240, H, 3, P)
            tot = [f.rearrange("p h t -> p (h t)"), piece(13312, 1024), piece(14336, 512), piece(14848, 256),
                   piece(15104, 128), piece(15232, 64), piece(15296, 32), piece(15328, 16)]
            ones = piece(15344, P)
            lbc = small[:, 0:8]
            lbn = small[:, 8:16]
            w = a["hgrn_w_in_2"][0]

            @block.gpsimd
            def _(pool):
                pool.memset(ones, 1.0)
                m["zero"] = done("pool", pool.memset(at[:, :, :, :], 0.0))

            @block.vector
            def _(dve):
                t0, r0 = col_of["lb"]
                m["d"] = done("dve", dve.tensor_tensor(small[:, 16:24], pcol[:, t0, r0 + 8:r0 + 16], pcol[:, t0, r0:r0 + 8], ALU.subtract))

            @block.scalar
            def _(act):
                act.wait_ge(dve_done, m["d"])
                act.activation(lbc, small[:, 16:24], ACT.Sigmoid)
                act.activation(lbn, small[:, 16:24], ACT.Sigmoid, scale=-1.0)

            def gate_evac(act, i, s, src):
                two = bass.ds(i * 4 + 2 * s, 2)
                act.activation(f[:, two, :], src, ACT.Sigmoid)
                return act.activation(k[:, two, :], src, ACT.Sigmoid, scale=-1.0)

            proj_T(lambda i, s, u: cols_dyn(w, i, s, u, D), 4, None, evac=gate_evac)
            proj_T(lambda i, s, u: cols_dyn(w, i, s, u), 4, None,
                   evac=lambda act, i, s, src: act.activation(q[:, bass.ds(i * 4 + 2 * s, 2), :], src, ACT.Silu))
            proj_T(lambda i, s, u: cols_dyn(w, i, s, u, 3 * D), 4, None,
                   evac=lambda act, i, s, src: act.activation(gz[:, bass.ds(i * 4 + 2 * s, 2), :], src, ACT.Silu))
            ready = proj_rows(w[:, 2 * D:3 * D], KC, D)

            @block.scalar
            def _(act):
                act.wait_ge(a_used, ready)
                for t in range(NT):
                    for h in range(2):
                        act.activation(v[:, t, h * HALF:h * HALF + HALF], bank[2 * t + h][:, :], ACT.Copy)
            end_phase()

            @block.vector
            def _(dve):
                for h in range(H):
                    dve.tensor_scalar(f[:, h, :], f[:, h, :], lbn[:, h:h + 1], lbc[:, h:h + 1], ALU.mult, ALU.add)
                    done("dve", dve.tensor_scalar(k[:, h, :], k[:, h, :], lbn[:, h:h + 1], None, ALU.mult))
                m["fk"] = chain["dve"]

            hs = (slice(0, 4), slice(4, 8))
            for l in range(9):
                seg = 1 << max(l - 1, 0)

                @block.tensor
                def _(pe):
                    for g in range(2):
                        pe.wait_ge(dve_done, m["fk"] if l == 0 else m["up", l - 1, g])
                        if l >= 2:
                            pe.wait_ge(dve_done, m["cp", l - 2, g])
                        b0 = 4 * (l % 2) + 2 * g
                        for j in range(4):
                            h = 4 * g + j
                            if l < 8:
                                for t in range(NT):
                                    tok = slice(t * P, t * P + P)
                                    ins = pe.matmul(bank[b0 + t][:, j * P:j * P + P], k[:, h, tok], q[:, h, tok], start=True, stop=True)
                            else:
                                ins = pe.matmul(bank[b0][:, j * P:j * P + P], k[:, h, 0:P], q[:, h, P:T], start=True, stop=True)
                        m["a", l, g] = done("pe", ins)

                @block.vector
                def _(dve):
                    if l == 0:
                        dve.wait_ge(dve_done, m["fk"])
                        dve.wait_ge(pool_done, m["zero"])
                    for g in range(2):
                        dve.wait_ge(pe_done, m["a", l, g])
                        if l == 0:
                            m["up", l, g] = done("dve", dve.tensor_tensor(q[:, hs[g], :], q[:, hs[g], :], f[:, hs[g], :], ALU.mult))
                        elif l < 8:
                            nb = 4 * T // (2 * seg)
                            qv = q[:, hs[g], :].rearrange("p h t -> p (h t)").rearrange("p (b e s) -> p b e s", e=2, s=seg)
                            kv = k[:, hs[g], :].rearrange("p h t -> p (h t)").rearrange("p (b e s) -> p b e s", e=2, s=seg)
                            tv = tot[l - 1][:, g * 2 * nb:(g + 1) * 2 * nb].rearrange("p (b e) -> p b e", e=2)
                            left = tv[:, :, 0:1].to_broadcast((P, nb, seg))
                            right = tv[:, :, 1:2].to_broadcast((P, nb, seg))
                            done("dve", dve.tensor_tensor(qv[:, :, 1, :], qv[:, :, 1, :], left, ALU.mult))
                            m["up", l, g] = done("dve", dve.tensor_tensor(kv[:, :, 0, :], kv[:, :, 0, :], right, ALU.mult))
                            if l < 8:
                                m["tot", l, g] = done("dve", dve.tensor_tensor(tot[l][:, g * nb:(g + 1) * nb], tv[:, :, 0], tv[:, :, 1], ALU.mult))
                        b0 = 4 * (l % 2) + 2 * g
                        mask = ident[:, :] if l == 0 else level[:, min(l - 1, 6), :]
                        if l < 8:
                            for t in range(NT):
                                m["cp", l, g] = done("dve", dve.copy_predicated(
                                    at[:, hs[g], 2 * t, :], mask.bitcast(U32).unsqueeze(1).to_broadcast((P, 4, P)),
                                    bank[b0 + t][:, :].rearrange("p (a b) -> p a b", a=4)))
                        else:
                            m["cp", l, g] = done("dve", dve.tensor_copy(at[:, hs[g], 1, :], bank[b0][:, :].rearrange("p (a b) -> p a b", a=4)))
                    dve.wait_ge(dve_done, m["cp", l, 1])
            end_phase()

            o, sq, rs = q, k, f

            @block.tensor
            def _(pe):
                for h in range(H):
                    b = bank[h // 2][:, (h % 2) * T:(h % 2) * T + T]
                    pe.matmul(b, v[:, 0, h * P:h * P + P], at[:, h, 0:2, :].rearrange("p a b -> p (a b)"), start=True, stop=False)
                    ins = pe.matmul(b[:, P:T], v[:, 1, h * P:h * P + P], at[:, h, 2, :], start=False, stop=True)
                    if h % 2:
                        m["o", h // 2] = done("pe", ins)

            @block.scalar
            def _(act):
                for i in range(4):
                    act.wait_ge(pe_done, m["o", i])
                    src = bank[i][:, :].rearrange("p (a t) -> p a t", a=2)
                    act.activation(o[:, 2 * i:2 * i + 2, :], src, ACT.Copy)
                    m["sq", i] = done("act", act.activation(sq[:, 2 * i:2 * i + 2, :], src, ACT.Square))

            @block.tensor
            def _(pe):
                for i in range(4):
                    pe.wait_ge(act_done, m["sq", i])
                    m["ms", i] = done("pe", pe.matmul(bank[4 + i][:, :], ones, sq[:, 2 * i:2 * i + 2, :].rearrange("p a t -> p (a t)"),
                                                      start=True, stop=True))

            @block.vector
            def _(dve):
                for i in range(4):
                    dve.wait_ge(pe_done, m["ms", i])
                    m["ve"] = done("dve", dve.tensor_scalar(rs[:, 2 * i:2 * i + 2, :], bank[4 + i][:, :].rearrange("p (a t) -> p a t", a=2),
                                                            1.0 / P, RMS_EPS, ALU.mult, ALU.add))

            @block.scalar
            def _(act):
                act.wait_ge(dve_done, m["ve"])
                m["sd"] = done("act", act.activation(rs[:, :, :], rs[:, :, :], ACT.Sqrt))

            @block.vector
            def _(dve):
                dve.wait_ge(act_done, m["sd"])
                V(dve, dve.reciprocal(rs[:, :, :], rs[:, :, :]))
                V(dve, dve.tensor_tensor(o[:, :, :], o[:, :, :], rs[:, :, :], ALU.mult))
                m["og"] = done("dve", dve.scalar_tensor_tensor(o[:, :, :].rearrange("p a t -> p (a t)"), o[:, :, :].rearrange("p a t -> p (a t)"),
                                                               pc("hg"), gz[:, :, :].rearrange("p a t -> p (a t)"), ALU.mult, ALU.mult))
            split_act(o, 0, 8, m["og"])
            end_phase()
            out_proj(a["hgrn_w_out_2"][0], 1.0 / ALPHA)
            layer_norm(1, 1)
        def half_block(layer, which):
            w = (layer, which)
            rms_norm_to_act(layer, 2 * which)
            ffn(a["ffn_w_gate"][w], a["ffn_w_up"][w], a["ffn_w_down"][w], 0.5)

        def second_ffn(n, layer, norm, last=False):
            ffn(a[f"ffn{n}_w_gate_2"][layer], a[f"ffn{n}_w_up_2"][layer], a[f"ffn{n}_w_down_2"][layer],
                0.5 / ALPHA, last_ffn=last)
            layer_norm(layer, norm, last)

        def steps():
            plan = [("ffn0", lambda: half_block(0, 0)),
                    ("rwkv", lambda: (rms_norm_to_act(0, 1, barrier=True), conv_rwkv())),
                    ("ffn1", lambda: half_block(0, 1)),
                    ("ffn2", lambda: half_block(1, 0)),
                    ("mla", lambda: (rms_norm_to_act(1, 1, barrier=True), mla())),
                    ("ffn3", lambda: (nsa_weights(), half_block(1, 1))),
                    ("f4", lambda: second_ffn(1, 0, 0)),
                    ("nsa", nsa),
                    ("f5", lambda: second_ffn(2, 0, 2)),
                    ("f6", lambda: second_ffn(1, 1, 0)),
                    ("hgrn", hgrn),
                    ("f7", lambda: second_ffn(2, 1, 2, last=True))]
            names = [name for name, _ in plan]
            first = names.index(start) + 1 if start else 0
            if first > names.index("ffn3"):
                nsa_weights()
                transpose_split(lambda t, k: x[:, t, k * P:k * P + P], None)
            for name, run in plan[first:]:
                run()
                if name == "ffn3":
                    transpose_split(lambda t, k: x[:, t, k * P:k * P + P], None, barrier=False,
                                    waits=[[(dve_done, n)] for n in x_ready])
                yield name

        for name in steps():
            if name == stop:
                break

        if stop and stop != "f7":
            @block.sync
            def _(sp):
                for u in range(2):
                    if u == 0:
                        sp.wait_ge(a_lo_done, na[0] + 1)
                    sp.dma_start(raw_a[:, na[0] % 2, u, :], a["x"][0, 0:P, :]).then_inc(a_loaded[na[0] % 2], 16)
            end_phase()

        @block.sync
        def _(sp):
            sp.wait_ge(phase_done, 4 * nphase[0])
            sp.dma_start(out[0].rearrange("(t p) d -> p t d", p=P), x[:, :, :]).then_inc(out_stored, 16)
            sp.wait_ge(out_stored, 16)
            sp.wait_ge(bias_stored, 16)


def constants():
    c = {"c_ident": np.eye(P, dtype=np.float32)}
    c["c_inv_freq"] = (10000.0 ** (-np.arange(0, 64, 2) / 64.0)).astype(np.float32)[None, :]
    i = np.arange(P)
    f = np.float32
    c["c_block_ones"] = (i[:, None] // 64 == i[None, :] // 64).astype(f)
    level = np.stack([(i[:, None] >> (l + 1) == i[None, :] >> (l + 1)) & ((i[:, None] >> l) % 2 == 0)
                      & ((i[None, :] >> l) % 2 == 1) for l in range(7)], 1)
    c["c_level"] = level.astype(f)
    c["c_level0_t"] = np.ascontiguousarray(level[:, 0].T).astype(f)
    c["c_upper"] = np.stack([i[:, None] < i[None, :], i[:, None] <= i[None, :]], 1).astype(f)
    c["c_seen"] = (i >= 31).astype(f)[:, None]
    dist = 255 - np.arange(384)
    n = np.maximum(dist, 1)
    large = 16 + np.floor(np.log(n / 16.0) / math.log(8.0) * 16 + 1e-9).astype(int)
    bucket = np.where(dist < 16, dist, np.minimum(large, 31))
    bucket = np.where(dist < 0, 32, bucket)
    c["c_onehot"] = (np.arange(33)[:, None] == bucket[None, :]).astype(f)
    return c


def kernel(**inputs):
    import concourse.bacc as bacc
    from concourse.bass_utils import run_bass_kernel_spmd

    nc = bacc.Bacc("TRN2", target_bir_lowering=False, num_devices=1)
    arrays, args = {}, {}
    for name, value in list(inputs.items()) + list(constants().items()):
        if name in UNUSED:
            continue
        arrays[f"in_{name}"] = v = np.ascontiguousarray(value)
        args[name] = nc.dram_tensor(f"in_{name}", v.shape, mybir.dt.from_np(v.dtype), kind="ExternalInput").ap()
    out = nc.dram_tensor("out_x", (1, T, D), F32, kind="ExternalOutput").ap()
    build_program(nc, args, out)
    r = run_bass_kernel_spmd(nc, [arrays], core_ids=[0])
    return r.results[0]["out_x"]
```

```python
from contextlib import ExitStack
import math

import numpy as np
import concourse.bass as bass
from concourse import mybir

ALU = mybir.AluOpType
ACT = mybir.ActivationFunctionType
AX = mybir.AxisListType
F32 = mybir.dt.float32
F32R = mybir.dt.float32r
I32 = mybir.dt.int32
U32 = mybir.dt.uint32

P = 128
T = 256
NT = T // P
D = 1024
KC = D // P
FF = 2816
FT = FF // P
HALF = 512
RMS_EPS = 1e-6
LN_EPS = 1e-5
DEPTH = 2
ALPHA = (2.0 * DEPTH) ** 0.25
UNUSED = ("swa_w_in_2", "swa_w_out_2", "swa_sinks_2")
ARENA = 18484


def build_program(nc, a, out, stop=None, start=None):
    ctx = ExitStack()
    with ctx:
        def sb(name, shape, dt=F32):
            return ctx.enter_context(nc.sbuf_tensor(name, shape, dt))

        def sem(name):
            return ctx.enter_context(nc.semaphore(name))

        raw_a = sb("raw_a", [P, 2, 2, D])
        hi_a = sb("hi_a", [P, 2, 2, D], F32R)
        lo_a = sb("lo_a", [P, 2, 2, D], F32R)
        raw_b = sb("raw_b", [P, 2, D])
        hi_b = sb("hi_b", [P, 2, D], F32R)
        lo_b = sb("lo_b", [P, 2, D], F32R)
        x = sb("x_res", [P, NT, D])
        xn = sb("xn", [P, NT, D])
        act_hi = sb("act_hi", [P, KC, T], F32R)
        act_lo = sb("act_lo", [P, KC, T], F32R)
        sg = sb("sg", [P, 2, T])
        hf = sb("hf", [P, 2, T])
        h_hi = sb("h_hi", [P, 2, T], F32R)
        h_lo = sb("h_lo", [P, 2, T], F32R)
        ln_g = sb("ln_g", [P, D])
        ln_b = sb("ln_b", [P, D])
        ident = sb("ident", [P, P])
        prow = sb("prow", [P, 3, P])
        pcol = sb("pcol", [P, 3, P])
        stat = sb("stat", [P, NT, 2, 6])
        mv = sb("mv", [P, NT, 2])
        ssq = sb("ssq", [P, NT])
        rstd = sb("rstd", [P, NT])
        neg_half = sb("neg_half", [P, T])
        arena = sb("arena", [P, ARENA])
        block_ones = sb("block_ones", [P, P])
        level = sb("level", [P, 7, P])
        level0_t = sb("level0_t", [P, P])
        upper = sb("upper", [P, 2, P])
        small = sb("small", [P, 256])
        bank = [ctx.enter_context(nc.psum_tensor(f"bank{i}", [P, HALF], F32)) for i in range(8)]

        a_loaded = [sem("a_loaded0"), sem("a_loaded1")]
        b_loaded = [sem("b_loaded0"), sem("b_loaded1")]
        a_hi_done = sem("a_hi_done")
        b_hi_done = sem("b_hi_done")
        a_lo_done = sem("a_lo_done")
        b_lo_done = sem("b_lo_done")
        a_used = sem("a_used")
        b_used = sem("b_used")
        silu_done = sem("silu_done")
        h_done = sem("h_done")
        hs_hi = sem("hs_hi")
        hs_done = sem("hs_done")
        pe_done = sem("pe_done")
        act_done = sem("act_done")
        dve_done = sem("dve_done")
        pool_done = sem("pool_done")
        done_of = {"pe": pe_done, "act": act_done, "dve": dve_done, "pool": pool_done}
        pt_read = sem("pt_read")
        phase_done = sem("phase_done")
        p_loaded = sem("p_loaded")
        p_loaded_pool = sem("p_loaded_pool")
        consts_loaded = sem("consts_loaded")
        ln_loaded = sem("ln_loaded")
        out_stored = sem("out_stored")

        block = ctx.enter_context(nc.Block())

        na = [0]
        nb = [0]
        a_words = [0, 0]
        b_words = [0, 0]
        nffn = [0]
        nphase = [0]
        chain = {"pe": 0, "act": 0, "dve": 0, "pool": 0}
        npt = [0]

        def done(kind, ins):
            chain[kind] += 1
            ins.then_inc(done_of[kind], 1)
            return chain[kind]

        def V(dve, ins):
            dve.wait_ge(dve_done, done("dve", ins))

        def A(act, ins):
            act.wait_ge(act_done, done("act", ins))

        def G(pool, ins):
            pool.wait_ge(pool_done, done("pool", ins))

        def end_phase():
            nphase[0] += 1
            n = 4 * nphase[0]

            @block.tensor
            def _(pe):
                pe.drain().then_inc(phase_done, 1)
                pe.wait_ge(phase_done, n)

            @block.scalar
            def _(act):
                act.drain().then_inc(phase_done, 1)
                act.wait_ge(phase_done, n)

            @block.vector
            def _(dve):
                dve.drain().then_inc(phase_done, 1)
                dve.wait_ge(phase_done, n)

            @block.gpsimd
            def _(pool):
                pool.drain().then_inc(phase_done, 1)
                pool.wait_ge(phase_done, n)

        prime = sb("prime", [P, 1])

        @block.vector
        def _(dve):
            dve.memset(prime[:, :], 0.0).then_inc(a_lo_done, 2)
            dve.memset(neg_half[:, :], -0.5).then_inc(b_lo_done, 2)

        @block.gpsimd
        def _(pool):
            pool.nop().then_inc(a_used, 2)
            pool.nop().then_inc(b_used, 2)
            pool.nop().then_inc(h_done, 2)
            pool.nop().then_inc(pt_read, 2)

        rows = []
        col_of = {}
        fill = [0, 0, 0]

        def param(name, src, n, width=P, tile=0):
            rows.append((tile, fill[tile], n, src, width))
            col_of[name] = (tile, fill[tile])
            fill[tile] += n

        def as_rows(ap):
            return ap.rearrange("(r c) -> r c", c=P)

        param("norm", a["norm_gains"].rearrange("l s (r c) -> (l s r) c", c=P), 48)
        param("conv", a["even_conv_w"][0].rearrange("j (r c) -> (j r) c", c=P), 12)
        param("mu", as_rows(a["even_mu_shift"][0][0:1536]), 12)
        param("mu_wa", a["even_mu_shift"][0:1, 1536:1600], 1, 64)
        param("mu_g", a["even_mu_shift"][0:1, 1600:1696], 1, 96)
        for name in ("rwkv_w0", "rwkv_a0", "rwkv_k_k", "rwkv_k_a", "rwkv_ln_w", "rwkv_ln_b"):
            param(name, as_rows(a[name][0]), 4)
        param("rwkv_r_k", a["rwkv_r_k"][0].rearrange("(r q) c -> r (q c)", q=2), 4)
        param("q_a", as_rows(a["mla_q_a_norm"][0]), 3)
        param("kv_a", as_rows(a["mla_kv_a_norm"][0]), 2)
        param("qn", a["mla_q_norm"][0:1, 0:128], 1)
        param("kn", a["mla_k_norm"][0:1, 0:128], 1)
        param("cmp_pos", a["nsa_cmp_pos_2"][0].rearrange("a (r l) d -> (a r) (l d)", l=2), 32, tile=1)
        param("lb", a["hgrn_lb_2"].rearrange("l (r c) -> (l r) c", c=P), 16, tile=1)
        param("hg", a["hgrn_norm_gain_2"], 1, tile=1)
        param("ln_gain", a["ln_gain_2"].rearrange("l s (r c) -> (l s r) c", c=P), 48, tile=1)
        param("ln_bias", a["ln_bias_2"].rearrange("l s (r c) -> (l s r) c", c=P), 48, tile=2)
        assert max(fill) <= P

        def pc(name, i=0):
            tile, row = col_of[name]
            return pcol[:, tile, row + i:row + i + 1]

        tab = sb("tab", [33, 16])
        onehot = sb("onehot", [33, 384])
        bias_row = sb("bias_row", [16, 384])
        seen = sb("seen", [P, 1])
        scratch = nc.dram_tensor("bias_scratch", (16, P, 512), F32)
        bias_in = sem("bias_in")
        bias_done = sem("bias_done")
        bias_stored = sem("bias_stored")

        @block.vector
        def _(dve):
            dve.memset(tab[32:33, :], -1e30).then_inc(bias_in, 1)

        @block.scalar
        def _(act):
            act.dma_start(tab[0:32, :], a["rel_bias_2"]).then_inc(p_loaded, 16)
            act.dma_start(onehot[:, :], a["c_onehot"]).then_inc(p_loaded, 16)

        consts = ((block_ones, "c_block_ones"), (level, "c_level"), (level0_t, "c_level0_t"), (upper, "c_upper"),
                  (seen, "c_seen"))
        prow_zero = sem("prow_zero")
        pcol_in = sem("pcol_in")
        pcol_done = sem("pcol_done")

        @block.gpsimd
        def _(pool):
            pool.memset(prow[:, :, :], 0.0).then_inc(prow_zero, 1)

        @block.scalar
        def _(act):
            act.dma_start(ident[:, :], a["c_ident"]).then_inc(p_loaded, 16)
            act.wait_ge(prow_zero, 1)
            for tile, row, n, src, width in rows[0::2]:
                act.dma_start(prow[row:row + n, tile, 0:width], src).then_inc(p_loaded, 16)

        @block.gpsimd
        def _(pool):
            pool.wait_ge(prow_zero, 1)
            for tile, row, n, src, width in rows[1::2]:
                pool.dma_start(prow[row:row + n, tile, 0:width], src).then_inc(p_loaded_pool, 16)
            for dst, name in consts:
                pool.dma_start(dst[:], a[name]).then_inc(consts_loaded, 16)

        def parameter_columns():
            @block.tensor
            def _(pe):
                pe.wait_ge(p_loaded, 16 * (len(rows[0::2]) + 3))
                pe.wait_ge(p_loaded_pool, 16 * len(rows[1::2]))
                for tile in range(3):
                    ins = pe.transpose(bank[0][:, tile * P:tile * P + P], prow[:, tile, :], ident[:, :])
                ins.then_inc(pcol_in, 1)
                pe.wait_ge(bias_in, 1)
                pe.matmul(bank[1][0:16, 0:384], tab[:, :], onehot[:, :], start=True, stop=True).then_inc(bias_done, 1)

            @block.vector
            def _(dve):
                dve.wait_ge(pcol_in, 1)
                dve.tensor_copy(pcol[:, :, :], bank[0][:, 0:3 * P].rearrange("p (a b) -> p a b", a=3)
                                ).then_inc(pcol_done, 1)

            @block.vector
            def _(dve):
                dve.wait_ge(bias_done, 1)
                dve.tensor_scalar(bias_row[:, :], bank[1][0:16, 0:384], 8.0, None, ALU.mult).then_inc(bias_done, 1)

            @block.gpsimd
            def _(pool):
                pool.wait_ge(bias_done, 2)
                pool.dma_start(bass.AP(scratch, 0, [[P * 512, 16], [513, P], [1, 384]]),
                              bias_row[:, :].unsqueeze(1).to_broadcast((16, P, 384))).then_inc(bias_stored, 16)

        x_loaded = sem("x_loaded")

        @block.sync
        def _(sp):
            sp.dma_start(x[:, :, :], a["x"][0].rearrange("(t p) d -> p t d", p=P)).then_inc(x_loaded, 16)

        @block.scalar
        def _(act):
            act.wait_ge(x_loaded, 16)

        @block.vector
        def _(dve):
            dve.wait_ge(x_loaded, 16)

        def hi_pair(act, i, s, AW, A0):
            slot = (A0 + s) % 2
            act.wait_ge(a_loaded[slot], i * 32 + (AW[slot] + 32 * (s // 2 + 1)))
            act.wait_ge(a_used, i * 2 + (A0 + s + 1))
            act.activation(hi_a[:, slot, :, :], raw_a[:, slot, :, :], ACT.Copy).then_inc(a_hi_done, 1)

        def lo_pair(dve, i, s, A0):
            slot = (A0 + s) % 2
            dve.wait_ge(a_hi_done, i * 2 + (A0 + s + 1))
            dve.tensor_tensor(lo_a[:, slot, :, :], raw_a[:, slot, :, :], hi_a[:, slot, :, :].bitcast(F32),
                              ALU.subtract).then_inc(a_lo_done, 1)

        PASSES = ((0, 0), (0, 1), (1, 0))

        def open_pairs(n):
            A0, AW = na[0], list(a_words)
            na[0] += n
            for s in range(n):
                a_words[(A0 + s) % 2] += 32
            return A0, AW

        @block.scalar
        def _(act):
            hi_pair(act, 0, 0, (0, 0), 0)

        @block.vector
        def _(dve):
            lo_pair(dve, 0, 0, 0)

        def proj_T(source, npairs, dest, evac=None):
            evac = evac or (lambda act, i, s, src: act.activation(dest(i, s), src, ACT.Copy))
            A0, AW = open_pairs(npairs)
            R0 = npt[0]
            npt[0] += npairs
            loops = npairs // 2 if npairs % 2 == 0 and npairs >= 4 else 0

            @block.sync
            def _(sp):
                def load(i, s):
                    slot = (A0 + s) % 2
                    for u in range(2):
                        if u == 0:
                            sp.wait_ge(a_lo_done, i * 2 + (A0 + s + 1))
                        src = source(i, s, u)
                        sp.dma_start(raw_a[:, slot, u, :].rearrange("p (k n) -> p k n", k=KC)[:, :, 0:src.shape[2]],
                                     src).then_inc(a_loaded[slot], 16)
                if loops:
                    with sp.Fori(0, loops) as i:
                        load(i, 0)
                        load(i, 1)
                else:
                    for s in range(npairs):
                        load(0, s)

            @block.scalar
            def _(act):
                def move(i, s):
                    act.wait_ge(a_used, i * 2 + (A0 + s + 3))
                    evac(act, i, s, bank[4 + s % 2][:, :].rearrange("p (u t) -> p u t", u=2)).then_inc(pt_read, 1)
                if loops:
                    with act.Fori(0, loops) as i:
                        for s in range(2):
                            hi_pair(act, i, s + 1, AW, A0)
                            move(i, s)
                else:
                    for s in range(npairs):
                        hi_pair(act, 0, s + 1, AW, A0)
                        move(0, s)

            @block.vector
            def _(dve):
                if loops:
                    with dve.Fori(0, loops) as i:
                        lo_pair(dve, i, 1, A0)
                        lo_pair(dve, i, 2, A0)
                else:
                    for s in range(npairs):
                        lo_pair(dve, 0, s + 1, A0)

            @block.tensor
            def _(pe):
                def products(i, s):
                    slot = (A0 + s) % 2
                    pe.wait_ge(a_lo_done, i * 2 + (A0 + s + 3))
                    pe.wait_ge(pt_read, i * 2 + (R0 + s + 1))
                    for u in range(2):
                        for k in range(KC):
                            w = slice(k * P, k * P + P)
                            for m, (wp, xp) in enumerate(PASSES):
                                ins = pe.matmul(bank[4 + s % 2][:, u * T:u * T + T], (hi_a, lo_a)[wp][:, slot, u, w],
                                                (act_hi, act_lo)[xp][:, k, :], start=(k == 0 and m == 0),
                                                stop=(k == KC - 1 and m == 2))
                    ins.then_inc(a_used, 1)
                pe.wait_ge(xlo_done, counts["xp"])
                if loops:
                    with pe.Fori(0, loops) as i:
                        products(i, 0)
                        products(i, 1)
                else:
                    for s in range(npairs):
                        products(0, s)

        def proj_rows(w, nk, width, k0=0, parts=None, b0=0, free=None):
            npairs = (nk + 1) // 2
            A0, AW = open_pairs(npairs)
            parts = parts or [(c, min(width, c + HALF)) for c in range(0, width, HALF)]

            @block.sync
            def _(sp):
                for s in range(npairs):
                    slot = (A0 + s) % 2
                    sp.wait_ge(a_lo_done, A0 + s + 1)
                    units = min(2, nk - 2 * s)
                    for u in range(units):
                        r = (2 * s + u) * P
                        sp.dma_start(raw_a[:, slot, u, 0:width], w[r:r + P, :]).then_inc(a_loaded[slot], 32 // units)

            @block.scalar
            def _(act):
                for s in range(npairs):
                    hi_pair(act, 0, s + 1, AW, A0)

            @block.vector
            def _(dve):
                for s in range(npairs):
                    lo_pair(dve, 0, s + 1, A0)

            @block.tensor
            def _(pe):
                pe.wait_ge(xlo_done, counts["xp"])
                if free:
                    pe.wait_ge(act_done, free)
                for s in range(npairs):
                    slot = (A0 + s) % 2
                    pe.wait_ge(a_lo_done, A0 + s + 3)
                    for u in range(min(2, nk - 2 * s)):
                        k = 2 * s + u
                        for t in range(NT):
                            for h, (c, e) in enumerate(parts):
                                for m, (wp, xp) in enumerate(PASSES):
                                    ins = pe.matmul(bank[b0 + 2 * t + h][:, 0:e - c],
                                                    (act_hi, act_lo)[xp][:, k0 + k, t * P:t * P + P],
                                                    (hi_a, lo_a)[wp][:, slot, u, c:e],
                                                    start=(k == 0 and m == 0), stop=(k == nk - 1 and m == 2))
                    ins.then_inc(a_used, 1)
            return A0 + npairs + 2

        def split_act(src, k0, n, ready_dve):
            hi_written = []

            @block.scalar
            def _(act):
                act.wait_ge(dve_done, ready_dve)
                hi_written.append(done("act", act.activation(act_hi[:, k0:k0 + n, :], src, ACT.Copy)))

            @block.vector
            def _(dve):
                dve.wait_ge(act_done, hi_written[0])
                dve.tensor_tensor(act_lo[:, k0:k0 + n, :], src, act_hi[:, k0:k0 + n, :].bitcast(F32), ALU.subtract)

        def out_proj(w, scale):
            update_x(a_used, proj_rows(w, KC, D), scale)

        def update_x(used, ready, scale, ready0=None):
            @block.vector
            def _(dve):
                if ready0:
                    dve.wait_ge(pe_done, ready0)
                else:
                    dve.wait_ge(used, ready)
                if x_free[0]:
                    dve.wait_ge(pool_done, x_free[0])
                for t in range(NT):
                    if ready0 and t == 1:
                        dve.wait_ge(used, ready)
                    for h in range(2):
                        cols = slice(h * HALF, h * HALF + HALF)
                        ins = dve.scalar_tensor_tensor(x[:, t, cols], bank[2 * t + h][:, :], scale, x[:, t, cols],
                                                       ALU.mult, ALU.add)
                    x_ready[t] = done("dve", ins)

        x_free = [0]
        x_ready = [0] * NT

        xpose_done = sem("xpose_done")
        xhi_done = sem("xhi_done")
        xlo_done = sem("xlo_done")
        counts = {"xp": 0, "ln": 0}

        def view(k):
            return bank[4 + k // 2][:, (k % 2) * T:(k % 2) * T + T]

        def pe_transposes(src, nk, waits=()):
            base = counts["xp"]
            counts["xp"] += nk
            if base == 0:
                parameter_columns()

            @block.tensor
            def _(pe):
                for t, ws in enumerate(waits):
                    for which, n in ws:
                        pe.wait_ge(which, n)
                    if t < NT - 1:
                        for k in range(nk):
                            pe.transpose(view(k)[:, t * P:t * P + P], src(t, k), ident[:, :])
                for k in range(nk):
                    for t in (range(NT) if not waits else (NT - 1,)):
                        ins = pe.transpose(view(k)[:, t * P:t * P + P], src(t, k), ident[:, :])
                    ins.then_inc(xpose_done, 1)
            return base

        def transpose_split(src, gain, nk=KC, dst0=0, waits=(), barrier=True):
            base = pe_transposes(src, nk, waits)

            @block.scalar
            def _(act):
                if base == 0:
                    act.wait_ge(pcol_done, 1)
                for k in range(nk):
                    act.wait_ge(xpose_done, base + min(nk, 2 * (k // 2) + 2))
                    act.activation(act_hi[:, dst0 + k, :], view(k), ACT.Copy,
                                   scale=gain(k) if gain else 1.0).then_inc(xhi_done, 1)

            @block.vector
            def _(dve):
                for k in range(nk):
                    dve.wait_ge(xhi_done, base + min(nk, 2 * (k // 2) + 2))
                    dve.scalar_tensor_tensor(act_lo[:, dst0 + k, :], view(k), gain(k) if gain else 1.0,
                                             act_hi[:, dst0 + k, :].bitcast(F32), ALU.mult, ALU.subtract
                                             ).then_inc(xlo_done, 1)
            if barrier:
                @block.gpsimd
                def _(pool):
                    pool.wait_ge(consts_loaded, 16 * len(consts))
                end_phase()

        def rms_norm_to_act(layer, which, barrier=False):
            sq, ms, rs, xs = [0, 0], [0, 0], [0, 0], [0, 0]

            @block.scalar
            def _(act):
                for t in range(NT):
                    if x_ready[t]:
                        act.wait_ge(dve_done, x_ready[t])
                    sq[t] = done("act", act.activation(xn[:, t, :], x[:, t, :], ACT.Square,
                                                       accum_out=ssq[:, t:t + 1]))

            @block.vector
            def _(dve):
                for t in range(NT):
                    dve.wait_ge(act_done, sq[t])
                    ms[t] = done("dve", dve.tensor_scalar(ssq[:, t:t + 1], ssq[:, t:t + 1], 1.0 / D, RMS_EPS,
                                                          ALU.mult, ALU.add))

            inverse_root(ms, rs)

            @block.vector
            def _(dve):
                for t in range(NT):
                    dve.wait_ge(pool_done, rs[t])
                    xs[t] = done("dve", dve.tensor_scalar(xn[:, t, :], x[:, t, :], rstd[:, t:t + 1], None, ALU.mult))
            transpose_split(lambda t, k: xn[:, t, k * P:k * P + P],
                            lambda k: pc("norm", (layer * 3 + which) * KC + k),
                            waits=([(dve_done, xs[0])], [(dve_done, xs[1])]), barrier=barrier)

        def inverse_root(ms, rs):
            @block.gpsimd
            def _(pool):
                for t in range(NT):
                    pool.wait_ge(dve_done, ms[t])
                    rs[t] = done("pool", pool.tensor_tensor(out=rstd[:, t:t + 1], in0=ssq[:, t:t + 1],
                                                            in1=neg_half[:, 0:1], op=ALU.pow))

        def layer_norm(layer, which, last=False):
            counts["ln"] += 1
            n = counts["ln"]
            ms, rs, xs = [0, 0], [0, 0], [0, 0]
            free = x_free[0]

            @block.gpsimd
            def _(pool):
                if n > 1:
                    pool.wait_ge(pool_done, free)
                for dst, src in ((ln_g, a["ln_gain_2"]), (ln_b, a["ln_bias_2"])):
                    pool.dma_start(dst[:, :], src[layer, which:which + 1, :].to_broadcast((P, D))
                                   ).then_inc(ln_loaded, 16)

            @block.vector
            def _(dve):
                agg = [0, 0]
                for t in range(NT):
                    dve.wait_ge(dve_done, x_ready[t])
                    for h in range(2):
                        last_stat = done("dve", dve.bn_stats(stat[:, t, h, :], x[:, t, h * HALF:h * HALF + HALF]))
                    dve.wait_ge(dve_done, last_stat)
                    V(dve, dve.bn_aggr(mv[:, t, :], stat[:, t, :, :]))
                    ms[t] = done("dve", dve.tensor_scalar(ssq[:, t:t + 1], mv[:, t, 1:2], LN_EPS / ALPHA ** 2, None,
                                                          ALU.add))

            inverse_root(ms, rs)

            @block.vector
            def _(dve):
                for t in range(NT):
                    dve.wait_ge(pool_done, rs[t])
                    xs[t] = done("dve", dve.tensor_scalar(xn[:, t, :], x[:, t, :], mv[:, t, 0:1], rstd[:, t:t + 1],
                                                          ALU.subtract, ALU.mult))

            @block.gpsimd
            def _(pool):
                pool.wait_ge(ln_loaded, 32 * n)
                for t in range(NT):
                    pool.wait_ge(dve_done, xs[t])
                    G(pool, pool.tensor_tensor(out=x[:, t, :], in0=xn[:, t, :], in1=ln_g[:, :], op=ALU.mult))
                    if not last:
                        G(pool, pool.tensor_tensor(out=x[:, t, :], in0=x[:, t, :], in1=ln_b[:, :], op=ALU.add))
                x_free[0] = chain["pool"]
            if last:
                @block.vector
                def _(dve):
                    dve.wait_ge(pool_done, x_free[0])
                    dve.tensor_tensor(x[:, :, :], x[:, :, :], ln_b[:, :].unsqueeze(1).to_broadcast((P, NT, D)), ALU.add)
                end_phase()
                return
            base = pe_transposes(lambda t, k: xn[:, t, k * P:k * P + P], KC,
                                 waits=([(dve_done, xs[0])], [(dve_done, xs[1])]))
            scaled = []

            @block.scalar
            def _(act):
                for k in range(KC):
                    act.wait_ge(xpose_done, base + 2 * (k // 2) + 2)
                    c = (layer * 3 + which) * KC + k
                    scaled.append(done("act", act.activation(ln_t[:, k, :], view(k), ACT.Identity,
                                                             scale=pc("ln_gain", c), bias=pc("ln_bias", c))))

            @block.vector
            def _(dve):
                for k in range(0, KC, 2):
                    two = slice(k, k + 2)
                    dve.wait_ge(act_done, scaled[k + 1])
                    hi = done("dve", dve.tensor_copy(act_hi[:, two, :], ln_t[:, two, :]))
                    dve.wait_ge(dve_done, hi)
                    dve.tensor_tensor(act_lo[:, two, :], ln_t[:, two, :], act_hi[:, two, :].bitcast(F32),
                                      ALU.subtract).then_inc(xlo_done, 2)

        ln_t = arena[:, 0:KC * T].rearrange("p (k t) -> p k t", k=KC)

        def ffn(w_gate, w_up, w_down, scale, last_ffn=False):
            A0, B0, T0 = na[0], nb[0], nffn[0] * FT
            na[0] += FT
            nb[0] += FT
            nffn[0] += 1
            AW, BW = list(a_words), list(b_words)
            for s in range(2):
                a_words[(A0 + s) % 2] += 32 * (FT // 2)
                b_words[(B0 + s) % 2] += 16 * (FT // 2)

            @block.sync
            def _(sp):
                with sp.Fori(0, FT // 2) as i:
                    for s in range(2):
                        sa, sbb = (A0 + s) % 2, (B0 + s) % 2
                        c = (i * 2 + s) * P
                        for u, w in enumerate((w_gate, w_up)):
                            if u == 0:
                                sp.wait_ge(a_lo_done, i * 2 + (A0 + s + 1))
                            sp.dma_start(raw_a[:, sa, u, :].rearrange("p (k n) -> p k n", k=KC),
                                         w[:, bass.ds(c, P)].rearrange("(k p) n -> p k n", p=P)
                                         ).then_inc(a_loaded[sa], 16)
                        sp.wait_ge(b_lo_done, i * 2 + (B0 + s + 1))
                        sp.dma_start(raw_b[:, sbb, :], w_down[bass.ds(c, P), :]).then_inc(b_loaded[sbb], 16)

            def act_tile(act, i, s):
                slot = (B0 + s) % 2
                act.wait_ge(b_loaded[slot], i * 16 + (BW[slot] + 16 * (s // 2 + 1)))
                act.wait_ge(b_used, i * 2 + (B0 + s + 1))
                act.activation(hi_b[:, slot, :], raw_b[:, slot, :], ACT.Copy).then_inc(b_hi_done, 1)
                act.wait_ge(a_used, i * 2 + (A0 + s + 3))
                act.wait_ge(h_done, i * 2 + (T0 + s + 1))
                act.activation(sg[:, s % 2, :], bank[4 + s % 2][:, 0:T], ACT.Silu).then_inc(silu_done, 1)

            @block.scalar
            def _(act):
                with act.Fori(0, FT // 2 - 1) as i:
                    for s in range(2):
                        hi_pair(act, i, s + 1, AW, A0)
                        act_tile(act, i, s)
                hi_pair(act, FT // 2 - 1, 1, AW, A0)
                act_tile(act, FT // 2 - 1, 0)
                if not last_ffn:
                    hi_pair(act, FT // 2 - 1, 2, AW, A0)
                act_tile(act, FT // 2 - 1, 1)

            def dve_tile(dve, i, s):
                slot = (B0 + s) % 2
                dve.wait_ge(b_hi_done, i * 2 + (B0 + s + 1))
                dve.tensor_tensor(lo_b[:, slot, :], raw_b[:, slot, :], hi_b[:, slot, :].bitcast(F32),
                                  ALU.subtract).then_inc(b_lo_done, 1)
                dve.wait_ge(silu_done, i * 2 + (T0 + s + 1))
                dve.tensor_tensor(hf[:, s, :], sg[:, s, :], bank[4 + s][:, T:2 * T], ALU.mult
                                  ).then_inc(h_done, 1)
                dve.wait_ge(h_done, i * 2 + (T0 + s + 3))
                dve.wait_ge(b_used, i * 2 + (B0 + s + 1))
                dve.tensor_copy(h_hi[:, s, :], hf[:, s, :]).then_inc(hs_hi, 1)
                dve.wait_ge(hs_hi, i * 2 + (T0 + s + 1))
                dve.tensor_tensor(h_lo[:, s, :], hf[:, s, :], h_hi[:, s, :].bitcast(F32), ALU.subtract
                                  ).then_inc(hs_done, 1)

            @block.vector
            def _(dve):
                with dve.Fori(0, FT // 2 - 1) as i:
                    for s in range(2):
                        lo_pair(dve, i, s + 1, A0)
                        dve_tile(dve, i, s)
                lo_pair(dve, FT // 2 - 1, 1, A0)
                dve_tile(dve, FT // 2 - 1, 0)
                if not last_ffn:
                    lo_pair(dve, FT // 2 - 1, 2, A0)
                dve_tile(dve, FT // 2 - 1, 1)

            first_tile = []
            split = counts["xp"] - KC

            def gate_up(pe, i, s, first=False):
                slot = (A0 + s) % 2
                pe.wait_ge(a_lo_done, i * 2 + (A0 + s + 3))
                pe.wait_ge(h_done, i * 2 + (T0 + s + 1))
                for u in range(2):
                    for k in range(KC):
                        w = slice(k * P, k * P + P)
                        if first and u == 0:
                            pe.wait_ge(xlo_done, split + max(k + 1, 2))
                        for m, (wt, xt) in enumerate(((hi_a, act_hi), (hi_a, act_lo), (lo_a, act_hi))):
                            ins = pe.matmul(bank[4 + s % 2][:, u * T:u * T + T], wt[:, slot, u, w], xt[:, k, :],
                                            start=(k == 0 and m == 0), stop=(k == KC - 1 and m == 2))
                ins.then_inc(a_used, 1)

            def down(pe, i, s, first=False, last=False):
                slot = (B0 + s) % 2
                pe.wait_ge(b_lo_done, i * 2 + (B0 + s + 3))
                pe.wait_ge(hs_done, i * 2 + (T0 + s + 1))
                for t in range(NT):
                    tok = slice(t * P, t * P + P)
                    for h in range(2):
                        cols = slice(h * HALF, h * HALF + HALF)
                        for m, (ht, wt) in enumerate(((h_hi, hi_b), (h_hi, lo_b), (h_lo, hi_b))):
                            ins = pe.matmul(bank[2 * t + h][:, :], ht[:, s % 2, tok], wt[:, slot, cols],
                                            start=(first and m == 0), stop=(last and m == 2))
                    if last and t == 0:
                        first_tile.append(done("pe", ins))
                ins.then_inc(b_used, 1)

            @block.tensor
            def _(pe):
                gate_up(pe, 0, 0, first=True)
                gate_up(pe, 0, 1)
                down(pe, 0, 0, first=True)
                with pe.Fori(0, FT // 2 - 1) as i:
                    gate_up(pe, i, 2)
                    down(pe, i, 1)
                    gate_up(pe, i, 3)
                    down(pe, i, 2)
                down(pe, FT // 2 - 1, 1, last=True)
            update_x(b_used, B0 + FT + 2, scale, first_tile[0])

        def piece(start, *shape):
            n = int(np.prod(shape))
            assert start + n <= ARENA, (start, shape)
            v = arena[:, start:start + n]
            if len(shape) == 1:
                return v
            names = " ".join("abcd"[:len(shape)])
            return v.rearrange(f"p ({names}) -> p {names}", **dict(zip("abcd", shape)))

        def cols_dyn(w, i, s, u, c0=0):
            return w[:, bass.ds(i * 4 * P + (c0 + (2 * s + u) * P), P)].rearrange("(k p) n -> p k n", p=P)

        def pcs(name, n):
            tile, row = col_of[name]
            return pcol[:, tile, row:row + n]

        def flat(ap):
            return ap.rearrange("p a b -> p (a b)")

        def conv_rwkv():
            NTILE = 26
            PITCH = T + 2
            pT = piece(0, NTILE, PITCH)
            mx = piece(NTILE * PITCH, 14, T)
            live = NTILE * PITCH + 14 * T
            ar = piece(live, 4, 2, 2 * P)
            bt = piece(live + 2048, 4, T)
            kt = piece(live + 3072, 4, T)
            gate = piece(live + 4096, 4, T)
            vtok = piece(live + 5120, 2, HALF)
            bonus = piece(live + 6144, 4, T)
            bktok = piece(live + 7168, 2, HALF)
            m = {}
            ld, aa, L = [piece(12 * PITCH + i * 1024, 4, T) for i in range(3)]
            kk = bktok.rearrange("p a b -> p (a b)").rearrange("p (a t) -> p a t", a=4)
            keep = ar[:, 0:2, :, :].rearrange("p a c n -> p (a c n)")

            w_in = a["even_w_in"][0]
            dwa, dg = mx[:, 12, :], mx[:, 13, :]

            w_small = xn[:, 0, :]
            small_loaded = sem("small_loaded")

            @block.gpsimd
            def _(pool):
                pool.dma_start(w_small[0:32, 0:512], a["rwkv_w_up"][0]).then_inc(small_loaded, 16)
                pool.dma_start(w_small[32:64, 0:512], a["rwkv_a_up"][0]).then_inc(small_loaded, 16)
                pool.dma_start(w_small[0:96, 512:1024], a["rwkv_g_up"][0]).then_inc(small_loaded, 16)
                G(pool, pool.memset(pT[:, :, 0:2], 0.0))

            proj_T(lambda i, s, u: cols_dyn(w_in, i, s, u), 12, lambda i, s: pT[:, bass.ds(i * 4 + 2 * s, 2), 2:PITCH])
            proj_T(lambda i, s, u: w_in[:, 3072 + 64 * u:3072 + (64, 160)[u]].rearrange("(k p) n -> p k n", p=P), 1,
                   lambda i, s: pT[:, 24:26, 2:PITCH])
            end_phase()

            def mix(dve, lo, hi):
                V(dve, dve.tensor_tensor(mx[:, lo:hi, :], pT[:, 12 + lo:12 + hi, 1:PITCH - 1],
                                         pT[:, 12 + lo:12 + hi, 2:PITCH], ALU.subtract))
                for i in range(lo, hi):
                    mu = pc("mu", i) if i < 12 else pc(("mu_wa", "mu_g")[i - 12])
                    m["mix", lo] = done("dve", dve.scalar_tensor_tensor(mx[:, i, :], mx[:, i, :], mu, pT[:, 12 + i, 2:PITCH],
                                                                        ALU.mult, ALU.add))

            @block.vector
            def _(dve):
                half = small[:, 0:8]
                dve.tensor_scalar(half[:, 0:4], pcs("rwkv_w0", 4), 0.5, None, ALU.mult)
                m["half"] = done("dve", dve.tensor_scalar(half[:, 4:8], pcs("rwkv_a0", 4), 0.5, None, ALU.mult))
                mix(dve, 12, 14)

            @block.scalar
            def _(act):
                act.wait_ge(dve_done, m["mix", 12])
                act.activation(dwa[0:32, :], dwa[0:32, :], ACT.Tanh)
                m["tanh"] = done("act", act.activation(dg[0:96, :], dg[0:96, :], ACT.Tanh, scale=0.5))

            @block.vector
            def _(dve):
                mix(dve, 4, 8)
                dve.wait_ge(act_done, m["tanh"])
                m["dg"] = done("dve", dve.tensor_scalar(dg[0:96, :], dg[0:96, :], 0.5, 0.5, ALU.mult, ALU.add))
                mix(dve, 0, 4)
                mix(dve, 8, 12)

            @block.gpsimd
            def _(pool):
                tap = hf[:, 0, :]
                G(pool, pool.memset(keep, 1.0))
                m["keep"] = done("pool", pool.memset(keep.rearrange("p (c t) -> p c t", t=P)[:, :, 0:1], 0.0))
                G(pool, pool.tensor_tensor(out=pT[:, 8:12, :], in0=pT[:, 8:12, :], in1=pT[:, 4:8, :], op=ALU.mult))
                for i in range(4):
                    u = pT[:, 8 + i, :]
                    y = pT[:, 4 + i, 0:T]
                    G(pool, pool.tensor_scalar(y, u[:, 0:T], pc("conv", i), None, ALU.mult))
                    for n in (1, 2):
                        G(pool, pool.tensor_scalar(tap, u[:, n:T + n], pc("conv", 4 * n + i), None, ALU.mult))
                        G(pool, pool.tensor_tensor(out=y, in0=y, in1=tap, op=ALU.add))
                y = pT[:, 4:8, 0:T]
                m["conv"] = done("pool", pool.tensor_tensor(out=y, in0=y, in1=pT[:, 0:4, 2:PITCH], op=ALU.mult))

            @block.tensor
            def _(pe):
                pe.wait_ge(small_loaded, 48)
                pe.wait_ge(dve_done, m["dg"])
                for i in range(4):
                    o = slice((i % 2) * T, (i % 2) * T + T)
                    c = slice(i * P, i * P + P)
                    pe.matmul(bank[i // 2][:, o], w_small[0:32, c], dwa[0:32, :], start=True, stop=True)
                    pe.matmul(bank[2 + i // 2][:, o], w_small[32:64, c], dwa[32:64, :], start=True, stop=True)
                    ins = pe.matmul(bank[6 + i // 2][:, o], w_small[0:96, 512 + i * P:512 + i * P + P], dg[0:96, :],
                                    start=True, stop=True)
                m["lora"] = done("pe", ins)
                pe.wait_ge(dve_done, m["mix", 8])
                for c in range(2):
                    for i in range(4):
                        ins = pe.transpose(bank[4 + c][:, i * P:i * P + P], mx[:, 8 + i, c * P:c * P + P], ident[:, :])
                m["vtok"] = done("pe", ins)

            @block.scalar
            def _(act):
                act.wait_ge(dve_done, m["mix", 8])
                act.wait_ge(pe_done, m["lora"])
                for j, dst in ((0, ld), (1, aa)):
                    for i in range(4):
                        ins = act.activation(dst[:, i, :], bank[2 * j + i // 2][:, (i % 2) * T:(i % 2) * T + T], ACT.Tanh,
                                             bias=small[:, 4 * j + i:4 * j + i + 1], scale=0.5)
                    m["tanh", j] = done("act", ins)
                act.activation(gate[:, 0:2, :], bank[6][:, :].rearrange("p (a t) -> p a t", a=2), ACT.Copy)
                act.activation(gate[:, 2:4, :], bank[7][:, :].rearrange("p (a t) -> p a t", a=2), ACT.Copy)
                act.wait_ge(pe_done, m["vtok"])
                act.activation(vtok[:, 0, :], bank[4][:, :], ACT.Copy)
                m["gate"] = done("act", act.activation(vtok[:, 1, :], bank[5][:, :], ACT.Copy))
                act.wait_ge(pool_done, m["conv"])
                m["conv_hi"] = done("act", act.activation(act_hi[:, 0:4, :], pT[:, 4:8, 0:T], ACT.Copy))

            E05 = math.exp(-0.5)
            r, k, v = mx[:, 0:4, :], mx[:, 4:8, :], mx[:, 8:12, :]
            kh = kt
            norm_buf = xn[:, 1, :].rearrange("p (a t) -> p a t", a=4)

            def chunks(z):
                return z.rearrange("p a (c t) -> p (a c) t", c=2)

            cmid = chunks(L)[:, :, P // 2 - 1]
            cend = chunks(L)[:, :, P - 1]
            lab = xn[:, 0, :].rearrange("p (a t) -> p a t", a=4)

            @block.vector
            def _(dve):
                for i in range(4):
                    V(dve, dve.tensor_scalar(kk[:, i, :], k[:, i, :], pc("rwkv_k_k", i), None, ALU.mult))
                m["kk2"] = done("dve", dve.tensor_tensor(norm_buf, kk[:, :, :], kk[:, :, :], ALU.mult))
                dve.wait_ge(act_done, m["tanh", 0])
                V(dve, dve.tensor_scalar(ld[:, :, :], ld[:, :, :], 1.0, -0.5 * E05, ALU.add, ALU.mult))
                dve.wait_ge(pool_done, m["keep"])
                V(dve, dve.tensor_tensor_scan(flat(L), keep, flat(ld), 0.0, ALU.mult, ALU.add))
                V(dve, dve.tensor_copy(small[:, 8:16], cmid))
                V(dve, dve.tensor_tensor(small[:, 16:24], cend, small[:, 8:16], ALU.subtract))
                V(dve, dve.tensor_tensor(chunks(L), chunks(L), small[:, 8:16].unsqueeze(2).to_broadcast((P, 8, P)), ALU.subtract))
                s2 = small[:, 16:24].rearrange("p (a c) -> p a c", c=2)[:, :, 0]
                s1 = small[:, 8:16].rearrange("p (a c) -> p a c", c=2)[:, :, 1]
                V(dve, dve.tensor_tensor(small[:, 24:28], s2, s1, ALU.add))
                m["logs"] = done("dve", dve.tensor_tensor(lab, L[:, :, :], ld[:, :, :], ALU.subtract))
                dve.wait_ge(act_done, m["tanh", 1])
                V(dve, dve.tensor_scalar(aa[:, :, :], aa[:, :, :], 0.5, 0.5, ALU.mult, ALU.add))
                V(dve, dve.tensor_scalar(kh[:, :, :], aa[:, :, :], -1.0, None, ALU.add))
                for i in range(4):
                    V(dve, dve.tensor_scalar(kh[:, i, :], kh[:, i, :], pc("rwkv_k_a", i), 1.0, ALU.mult, ALU.add))
                V(dve, dve.tensor_tensor(kh[:, :, :], kh[:, :, :], k, ALU.mult))
                for i in range(4):
                    V(dve, dve.scalar_tensor_tensor(bonus[:, i, :], kh[:, i, :], pc("rwkv_r_k", i), r[:, i, :], ALU.mult, ALU.mult))
                m["rkr"] = chain["dve"]

            @block.tensor
            def _(pe):
                def head_sums(src, b):
                    for i in range(2):
                        ins = pe.matmul(bank[b + i][:, :], block_ones[:, :], flat(src[:, 2 * i:2 * i + 2, :]), start=True, stop=True)
                    return done("pe", ins)
                pe.wait_ge(dve_done, m["kk2"])
                pe.wait_ge(act_done, m["gate"])
                m["kksum"] = head_sums(norm_buf, 0)
                pe.wait_ge(dve_done, m["rkr"])
                m["rkrsum"] = head_sums(bonus, 2)

            def from_banks(b):
                return [(bank[b + i][:, :].rearrange("p (a t) -> p a t", a=2), slice(2 * i, 2 * i + 2)) for i in range(2)]

            @block.scalar
            def _(act):
                act.wait_ge(dve_done, m["logs"])
                act.activation(small[:, 28:32], small[:, 24:28], ACT.Exp)
                for c in range(2):
                    tok = slice(c * P, c * P + P)
                    act.activation(ar[:, :, c, 0:P], lab[:, :, tok], ACT.Exp)
                    act.activation(ar[:, :, c, P:2 * P], L[:, :, tok], ACT.Exp)
                m["exps"] = done("act", act.activation(bt[:, :, :], L[:, :, :], ACT.Exp, scale=-1.0))

            @block.vector
            def _(dve):
                dve.wait_ge(pe_done, m["kksum"])
                for src, at in from_banks(0):
                    last = done("dve", dve.tensor_scalar(norm_buf[:, at, :], src, 1e-24, None, ALU.max))
                m["kkmax"] = last

            @block.scalar
            def _(act):
                act.wait_ge(dve_done, m["kkmax"])
                m["kknorm"] = done("act", act.activation(norm_buf, norm_buf, ACT.Sqrt))

            @block.vector
            def _(dve):
                dve.wait_ge(act_done, m["kknorm"])
                V(dve, dve.reciprocal(norm_buf, norm_buf))
                V(dve, dve.tensor_tensor(kk[:, :, :], kk[:, :, :], norm_buf, ALU.mult))
                dve.wait_ge(pe_done, m["rkrsum"])
                for src, at in from_banks(2):
                    V(dve, dve.tensor_tensor(bonus[:, at, :], src, v[:, at, :], ALU.mult))
                dve.wait_ge(act_done, m["conv_hi"])
                dve.tensor_tensor(act_lo[:, 0:4, :], pT[:, 4:8, 0:T], act_hi[:, 0:4, :].bitcast(F32), ALU.subtract)

            @block.vector
            def _(dve):
                dve.wait_ge(act_done, m["exps"])
                V(dve, dve.tensor_tensor(kt[:, :, :], bt[:, :, :], kh[:, :, :], ALU.mult))
                V(dve, dve.tensor_tensor(bt[:, :, :], bt[:, :, :], kk[:, :, :], ALU.mult))
                V(dve, dve.tensor_tensor(bt[:, :, :], bt[:, :, :], aa[:, :, :], ALU.mult))
                for c in range(2):
                    tok = slice(c * P, c * P + P)
                    V(dve, dve.scalar_tensor_tensor(ar[:, :, c, 0:P], ar[:, :, c, 0:P], -1.0, kk[:, :, tok], ALU.mult, ALU.mult))
                    V(dve, dve.tensor_tensor(ar[:, :, c, P:2 * P], ar[:, :, c, P:2 * P], r[:, :, tok], ALU.mult))
            end_phase()

            XT = piece(0, 4, 4, P)
            abT = piece(2048, 4, 4, P)
            X = piece(4096, 4, 4, P)
            ct = piece(6144, 4, 4, P)
            ysb = piece(8192, 4, 4, P)
            mm = piece(2048, 2, 8, 3, P)
            zs = xn[:, 0, 0:HALF]
            us = xn[:, 0, HALF:D]
            s0 = sg[:, :, :].rearrange("p a b -> p (a b)")[:, 0:256].rearrange("p (i d) -> p i d", i=4)
            yT = norm_buf

            heads = [(slice(64 * e, 64 * e + 64), i, slice((2 * i + e) * 64, (2 * i + e) * 64 + 64))
                     for e in range(2) for i in range(4)]
            tiles = [slice(c * P, c * P + P) for c in range(2)]

            def four(b, n=4):
                return bank[b][:, 0:n * P].rearrange("p (a b) -> p a b", a=n)

            def over_heads(mask):
                return mask.bitcast(U32).unsqueeze(1).to_broadcast((P, 4, P))

            eye4 = ident[:, :].unsqueeze(1).to_broadcast((P, 4, P))

            @block.gpsimd
            def _(pool):
                m["zero"] = done("pool", pool.memset(abT[:, :, :, :], 0.0))
                for g in range(4):
                    m["eye", g] = done("pool", pool.tensor_copy(X[:, g, :, :], eye4))

            @block.scalar
            def _(act):
                for g in range(4):
                    m["eyeT", g] = done("act", act.activation(XT[:, g, :, :], eye4, ACT.Copy))

            @block.tensor
            def _(pe):
                for g in range(4):
                    c = g // 2
                    for e in range(4 * (g % 2), 4 * (g % 2) + 4):
                        q, i, hv = heads[e]
                        pe.matmul(bank[2 * g][:, i * P:i * P + P], bt[q, i, tiles[c]], ar[q, i, c, 0:P], start=True, stop=True)
                        ins = pe.matmul(bank[2 * g + 1][:, i * P:i * P + P], ar[q, i, c, 0:P], bt[q, i, tiles[c]],
                                        start=True, stop=True)
                    m["ab", g] = done("pe", ins)

            @block.vector
            def _(dve):
                dve.wait_ge(pool_done, m["zero"])
                for g in range(4):
                    dve.wait_ge(pe_done, m["ab", g])
                    m["abT", g] = done("dve", dve.copy_predicated(abT[:, g, :, :], over_heads(upper[:, 0, :]), four(2 * g)))
                    dve.wait_ge(pool_done, m["eye", g])
                    dve.copy_predicated(X[:, g, :, :], over_heads(level0_t[:, :]), four(2 * g + 1))
                    dve.wait_ge(act_done, m["eyeT", g])
                    m["x", g] = done("dve", dve.copy_predicated(XT[:, g, :, :], over_heads(level[:, 0, :]), four(2 * g)))

            for l in range(1, 7):
                @block.gpsimd
                def _(pool):
                    for g in range(4):
                        if l == 1:
                            pool.wait_ge(dve_done, m["abT", g])
                        else:
                            pool.wait_ge(pe_done, m["y", g])
                        m["c", g] = done("pool", pool.tensor_tensor(
                            out=ct[:, g, :, :], in0=abT[:, g, :, :],
                            in1=level[:, l, :].unsqueeze(1).to_broadcast((P, 4, P)), op=ALU.mult))

                @block.tensor
                def _(pe):
                    for g in range(4):
                        pe.wait_ge(pool_done, m["c", g])
                        pe.wait_ge(dve_done, m["x", g])
                        for h in range(4):
                            ins = pe.matmul(bank[2 * g][:, h * P:h * P + P], ct[:, g, h, :], X[:, g, h, :], start=True, stop=True)
                        m["y", g] = done("pe", ins)

                @block.scalar
                def _(act):
                    for g in range(4):
                        act.wait_ge(pe_done, m["y", g])
                        m["ys", g] = done("act", act.activation(ysb[:, g, :, :], four(2 * g), ACT.Copy))

                @block.tensor
                def _(pe):
                    for g in range(4):
                        pe.wait_ge(act_done, m["ys", g])
                        for h in range(4):
                            if l < 6:
                                pe.matmul(bank[2 * g][:, h * P:h * P + P], XT[:, g, h, :], ysb[:, g, h, :], start=True, stop=True)
                            ins = pe.matmul(bank[2 * g + 1][:, h * P:h * P + P], ysb[:, g, h, :], XT[:, g, h, :], start=True, stop=True)
                        m["dx", g] = done("pe", ins)

                @block.vector
                def _(dve):
                    for g in range(4):
                        dve.wait_ge(pe_done, m["dx", g])
                        if l < 6:
                            done("dve", dve.tensor_tensor(X[:, g, :, :], four(2 * g), X[:, g, :, :], ALU.add))
                        m["x", g] = done("dve", dve.tensor_tensor(XT[:, g, :, :], four(2 * g + 1), XT[:, g, :, :], ALU.add))

            @block.gpsimd
            def _(pool):
                for c in range(2):
                    pool.wait_ge(pe_done, m["y", 3])
                    m["zero", c] = done("pool", pool.memset(mm[:, c, :, :, :], 0.0))

            @block.gpsimd
            def _(pool):
                for i in range(4):
                    G(pool, pool.tensor_scalar(bonus[:, i, :], bonus[:, i, :], pc("rwkv_ln_b", i), None, ALU.add))
                G(pool, pool.tensor_tensor(out=bonus[:, :, :], in0=bonus[:, :, :], in1=gate[:, :, :], op=ALU.mult))
                for i in range(4):
                    G(pool, pool.tensor_scalar(gate[:, i, :], gate[:, i, :], pc("rwkv_ln_w", i), None, ALU.mult))
                m["gated"] = chain["pool"]

            def products(c):
                @block.tensor
                def _(pe):
                    for e, (q, i, hv) in enumerate(heads):
                        if c == 0 and e == 0:
                            pe.wait_ge(dve_done, m["x", 3])
                        if c or e >= 4:
                            pe.wait_ge(dve_done, m["mm", (8 * c + e - 4) // 8, (e + 4) % 8])
                        pe.matmul(bank[e % 4][:, 0:2 * P], kt[q, i, tiles[c]], ar[q, i, c, :], start=True, stop=True)
                        m["p", c, e] = done("pe", pe.matmul(bank[e % 4][:, 2 * P:3 * P], bt[q, i, tiles[c]], ar[q, i, c, P:2 * P],
                                                            start=True, stop=True))
                        m["mm", c, e] = chain["dve"] + e + 1

                @block.vector
                def _(dve):
                    dve.wait_ge(pool_done, m["zero", c])
                    for e in range(8):
                        dve.wait_ge(pe_done, m["p", c, e])
                        dve.copy_predicated(mm[:, c, e, 0:2, :], upper[:, :, :].bitcast(U32),
                                            bank[e % 4][:, 0:2 * P].rearrange("p (a b) -> p a b", a=2))
                        n = done("dve", dve.copy_predicated(mm[:, c, e, 2, :], upper[:, 1, :].bitcast(U32), bank[e % 4][:, 2 * P:3 * P]))
                        assert n == m["mm", c, e]

            def solve(c, zb):
                @block.tensor
                def _(pe):
                    pe.wait_ge(dve_done, m["mm", c, 7])
                    if c == 1:
                        pe.wait_ge(dve_done, m["s0"])
                    for e, (q, i, hv) in enumerate(heads):
                        o = bank[zb[e // 4]][:, i * 64:i * 64 + 64]
                        ins = pe.matmul(o, mm[:, c, e, 0, :], vtok[:, c, hv], start=True, stop=(c == 0))
                        if c == 1:
                            ins = pe.matmul(o, ar[q, i, c, 0:P], s0[q, i, :], start=False, stop=True)
                    m["z"] = done("pe", ins)

                @block.scalar
                def _(act):
                    act.wait_ge(pe_done, m["z"])
                    act.activation(zs[:, 0:256], bank[zb[0]][:, 0:256], ACT.Copy)
                    m["zs"] = done("act", act.activation(zs[:, 256:512], bank[zb[1]][:, 0:256], ACT.Copy))

            def apply(c, ub, yb, sb_):
                @block.tensor
                def _(pe):
                    pe.wait_ge(act_done, m["zs"])
                    for e in range(8):
                        ins = pe.matmul(bank[ub][:, e * 64:e * 64 + 64], XT[:, 2 * c + e // 4, e % 4, :], zs[:, e * 64:e * 64 + 64],
                                        start=True, stop=True)
                    m["u"] = done("pe", ins)

                @block.scalar
                def _(act):
                    act.wait_ge(pe_done, m["u"])
                    m["us"] = done("act", act.activation(us, bank[ub][:, :], ACT.Copy))

                @block.tensor
                def _(pe):
                    pe.wait_ge(act_done, m["us"])
                    if c == 0:
                        pe.wait_ge(act_done, m["bktok"])
                        for e, (q, i, hv) in enumerate(heads):
                            o = bank[sb_[e // 4]][q, i * 64:i * 64 + 64]
                            pe.matmul(o, bktok[:, 0, hv], us[:, e * 64:e * 64 + 64], start=True, stop=False)
                            ins = pe.matmul(o, bktok[:, 1, hv], vtok[:, c, hv], start=False, stop=True)
                        m["s"] = done("pe", ins)
                    for e, (q, i, hv) in enumerate(heads):
                        o = bank[yb[e // 4]][:, i * 64:i * 64 + 64]
                        pe.matmul(o, mm[:, c, e, 2, :], us[:, e * 64:e * 64 + 64], start=True, stop=False)
                        ins = pe.matmul(o, mm[:, c, e, 1, :], vtok[:, c, hv], start=False, stop=(c == 0))
                        if c == 1:
                            ins = pe.matmul(o, ar[q, i, c, P:2 * P], s0[q, i, :], start=False, stop=True)
                    m["y"] = done("pe", ins)

                @block.vector
                def _(dve):
                    if c == 0:
                        dve.wait_ge(pe_done, m["s"])
                        for i in range(4):
                            for e in range(2):
                                q = slice(64 * e, 64 * e + 64)
                                m["s0"] = done("dve", dve.tensor_scalar(s0[q, i, :], bank[sb_[e]][q, i * 64:i * 64 + 64],
                                                                        small[q, 28 + i:29 + i], None, ALU.mult))

            yc, ysq = piece(8192, 2, 4, 2, 64), piece(9216, 2, 4, 2, 64)

            def group_norm(c, yb):
                mu, var, rs = (small[:, 32 + 24 * c + 8 * n:40 + 24 * c + 8 * n] for n in range(3))

                def by_head(z):
                    return z.rearrange("p (e i) -> p i e", e=2).unsqueeze(3).to_broadcast((P, 4, 2, 64))

                @block.vector
                def _(dve):
                    dve.wait_ge(pe_done, m["y"])
                    for e in range(2):
                        src = bank[yb[e]][:, 0:256].rearrange("p (i d) -> p i d", i=4)
                        V(dve, dve.tensor_reduce(mu[:, 4 * e:4 * e + 4], src, AX.X, ALU.add))
                    V(dve, dve.tensor_scalar(mu, mu, 1.0 / 64, None, ALU.mult))
                    for e in range(2):
                        src = bank[yb[e]][:, 0:256].rearrange("p (i d) -> p i d", i=4)
                        m["yc", c] = done("dve", dve.tensor_tensor(yc[:, c, :, e, :], src, mu[:, 4 * e:4 * e + 4].unsqueeze(2)
                                                                   .to_broadcast((P, 4, 64)), ALU.subtract))

                @block.scalar
                def _(act):
                    act.wait_ge(dve_done, m["yc", c])
                    m["ysq", c] = done("act", act.activation(ysq[:, c, :, :, :], yc[:, c, :, :, :], ACT.Square))

                @block.vector
                def _(dve):
                    dve.wait_ge(act_done, m["ysq", c])
                    V(dve, dve.tensor_reduce(var.rearrange("p (e i) -> p i e", e=2), ysq[:, c, :, :, :], AX.X, ALU.add))
                    m["var", c] = done("dve", dve.tensor_scalar(var, var, 1.0 / 64, 64e-5, ALU.mult, ALU.add))

                @block.gpsimd
                def _(pool):
                    pool.wait_ge(dve_done, m["var", c])
                    m["rs", c] = done("pool", pool.tensor_tensor(out=rs, in0=var, in1=neg_half[:, 0:8], op=ALU.pow))

                @block.vector
                def _(dve):
                    dve.wait_ge(pool_done, m["rs", c])
                    m["yn", c] = done("dve", dve.tensor_tensor(yc[:, c, :, :, :], yc[:, c, :, :, :], by_head(rs), ALU.mult))

            def gated(c, b):
                @block.tensor
                def _(pe):
                    pe.wait_ge(dve_done, m["yn", c])
                    for i in range(4):
                        ins = pe.transpose(bank[b][:, i * P:i * P + P], yc[:, c, i, :, :].rearrange("p a b -> p (a b)"), ident[:, :])
                    m["yt", c] = done("pe", ins)

                @block.vector
                def _(dve):
                    y = yT[:, :, tiles[c]]
                    dve.wait_ge(pe_done, m["yt", c])
                    dve.wait_ge(pool_done, m["gated"])
                    V(dve, dve.tensor_tensor(y, four(b), gate[:, :, tiles[c]], ALU.mult))
                    m["yg", c] = done("dve", dve.tensor_tensor(y, y, bonus[:, :, tiles[c]], ALU.add))

                @block.scalar
                def _(act):
                    act.wait_ge(dve_done, m["yg", c])
                    m["yhi", c] = done("act", act.activation(act_hi[:, 4:8, tiles[c]], yT[:, :, tiles[c]], ACT.Copy))

                @block.vector
                def _(dve):
                    dve.wait_ge(act_done, m["yhi", c])
                    dve.tensor_tensor(act_lo[:, 4:8, tiles[c]], yT[:, :, tiles[c]], act_hi[:, 4:8, tiles[c]].bitcast(F32),
                                      ALU.subtract)

            products(0)

            @block.tensor
            def _(pe):
                for j, src in ((0, bt), (1, kt)):
                    for i in range(4):
                        ins = pe.transpose(bank[6 + j][:, i * P:i * P + P], src[:, i, 0:P], ident[:, :])
                m["bkt"] = done("pe", ins)

            @block.scalar
            def _(act):
                act.wait_ge(pe_done, m["bkt"])
                act.activation(bktok[:, 0, :], bank[6][:, :], ACT.Copy)
                m["bktok"] = done("act", act.activation(bktok[:, 1, :], bank[7][:, :], ACT.Copy))

            solve(0, (4, 5))
            products(1)
            apply(0, 6, (7, 4), (5, 6))
            group_norm(0, (7, 4))
            solve(1, (0, 1))
            apply(1, 2, (5, 6), None)
            group_norm(1, (5, 6))
            gated(0, 7)
            gated(1, 5)
            end_phase()
            out_proj(a["even_w_out"][0], 1.0)

        def mla():
            H, NOPE, ROPE, QR, KVR = 8, 128, 64, 384, 256
            QK = NOPE + ROPE
            m = {}
            qn = piece(0, NT, H, NOPE)
            qr = piece(2048, NT, H, ROPE)
            kn = piece(3072, NT, H, NOPE)
            kr = piece(5120, NT, H, ROPE)
            vv = piece(6144, NT, H, NOPE)
            cp = piece(8192, NT, 704)
            qnT = piece(9600, H, T)
            knT = piece(11648, H, T)
            qrT = piece(13696, H // 2, T)
            krT = piece(14720, H // 2, T)
            pr = piece(15744, 3, 3 * P)
            prT = piece(2048, 2, 3 * P)
            mask = piece(17280, 3 * P)
            rope_g = piece(17664, 2, ROPE)
            cs = piece(17792, 2, NT, ROPE // 2)
            stats = piece(17920, 2, 2, NT, 4)
            krot = piece(17952, NT, ROPE)
            sqq = piece(9600, NT, H, QK)
            sqk = piece(12672, NT, H, NOPE)
            rot = piece(14720, 4, NT, 4, ROPE // 2)
            exp_scale = small[:, 64:80].rearrange("p (g t h) -> p g t h", g=2, t=NT)
            neg_scale = small[:, 80:96].rearrange("p (g t h) -> p g t h", g=2, t=NT)
            work = xn[:, :, :]
            misc_loaded = sem("mla_loaded")

            @block.gpsimd
            def _(pool):
                G(pool, pool.memset(mask, 0.0))
                for c in (0, 2):
                    v = mask[:, c * P:c * P + P]
                    ins = pool.affine_select(out=v, in_=v, compare_op=ALU.is_ge, fill=-1e30, base=0,
                                             pattern=[[-1, P]], channel_multiplier=1)
                m["mask"] = done("pool", ins)

            pos_i = small[:, 20:22].bitcast(I32)
            angles = piece(14720, 320)
            ang = angles[:, 0:64]
            turns = angles[:, 64:128]
            freq = angles[:, 128:160]
            arg = angles[:, 192:320]

            @block.gpsimd
            def _(pool):
                for i, n in enumerate(("mla_q_norm", "mla_k_norm")):
                    pool.dma_start(rope_g[:, i, :], a[n][0:1, NOPE:QK].to_broadcast((P, ROPE))).then_inc(misc_loaded, 16)
                pool.dma_start(freq, a["c_inv_freq"].to_broadcast((P, 32))).then_inc(misc_loaded, 16)
                pool.dma_start(pos_i, a["positions"][0].rearrange("(t p) -> p t", p=P),
                             allow_slow_non_contiguous=True).then_inc(misc_loaded, 16)

            ready = proj_rows(a["odd_w_in"][0], KC, 704)

            @block.scalar
            def _(act):
                act.wait_ge(a_used, ready)
                for t in range(NT):
                    act.activation(cp[:, t, 0:HALF], bank[2 * t][:, :], ACT.Copy)
                    m["cp"] = done("act", act.activation(cp[:, t, HALF:704], bank[2 * t + 1][:, 0:192], ACT.Copy))

            @block.scalar
            def _(act):
                act.wait_ge(act_done, m["cp"])
                for t in range(NT):
                    act.activation(work[:, 0, 0:QR], cp[:, t, 0:QR], ACT.Square, accum_out=small[:, 2 * t:2 * t + 1])
                    ins = act.activation(work[:, 1, 0:KVR], cp[:, t, QR:QR + KVR], ACT.Square,
                                         accum_out=small[:, 2 * t + 1:2 * t + 2])
                    A(act, ins)
                    m["ss", t] = chain["act"]

            @block.vector
            def _(dve):
                for t in range(NT):
                    dve.wait_ge(act_done, m["ss", t])
                    dve.tensor_scalar(small[:, 2 * t:2 * t + 1], small[:, 2 * t:2 * t + 1], 1.0 / QR, RMS_EPS, ALU.mult, ALU.add)
                    m["ms", t] = done("dve", dve.tensor_scalar(small[:, 2 * t + 1:2 * t + 2], small[:, 2 * t + 1:2 * t + 2],
                                                               1.0 / KVR, RMS_EPS, ALU.mult, ALU.add))

            @block.gpsimd
            def _(pool):
                for t in range(NT):
                    pool.wait_ge(dve_done, m["ms", t])
                    m["rs", t] = done("pool", pool.tensor_tensor(out=small[:, 4 + 2 * t:6 + 2 * t], in0=small[:, 2 * t:2 * t + 2],
                                                                 in1=neg_half[:, 0:2], op=ALU.pow))

            @block.vector
            def _(dve):
                dve.wait_ge(act_done, m["ss", 1])
                for t in range(NT):
                    dve.wait_ge(pool_done, m["rs", t])
                    dve.tensor_scalar(work[:, t, 0:QR], cp[:, t, 0:QR], small[:, 4 + 2 * t:5 + 2 * t], None, ALU.mult)
                    m["ls", t] = done("dve", dve.tensor_scalar(work[:, t, QR:QR + KVR], cp[:, t, QR:QR + KVR],
                                                               small[:, 5 + 2 * t:6 + 2 * t], None, ALU.mult))
            transpose_split(lambda t, k: work[:, t, k * P:k * P + P],
                            lambda k: pc("q_a", k) if k < 3 else pc("kv_a", k - 3), nk=5,
                            waits=([(dve_done, m["ls", 0])], [(dve_done, m["ls", 1])]), barrier=False)

            @block.vector
            def _(dve):
                dve.wait_ge(misc_loaded, 64)
                V(dve, dve.tensor_copy(small[:, 22:24], pos_i))
                for t in range(NT):
                    V(dve, dve.tensor_scalar(ang[:, t * 32:t * 32 + 32], freq, small[:, 22 + t:23 + t], None, ALU.mult))
                V(dve, dve.tensor_scalar(turns, ang, 1.0 / (2 * math.pi), None, ALU.mult))
                V(dve, dve.tensor_scalar(turns, turns, 12582912.0, None, ALU.add))
                V(dve, dve.tensor_scalar(turns, turns, -12582912.0, None, ALU.add))
                c1 = 6.28125
                c2 = round((2 * math.pi - c1) * 2 ** 21) / 2 ** 21
                c3 = 2 * math.pi - c1 - c2
                for c in (c1, c2, c3):
                    V(dve, dve.scalar_tensor_tensor(ang, turns, -c, ang, ALU.mult, ALU.add))
                V(dve, dve.tensor_scalar(ang, ang, 3.1415925, -3.1415925, ALU.min, ALU.max))
                V(dve, dve.tensor_copy(arg[:, 64:128], ang))
                V(dve, dve.scalar_tensor_tensor(ang, ang, -1.0, ang, ALU.mult, ALU.min))
                m["arg"] = done("dve", dve.tensor_scalar(arg[:, 0:64], ang, math.pi / 2, None, ALU.add))

            @block.scalar
            def _(act):
                act.wait_ge(dve_done, m["arg"])
                m["cs"] = done("act", act.activation(cs[:, :, :, :], arg.rearrange("p (a b c) -> p a b c", a=2, b=2), ACT.Sin))

            wq, wkv = a["mla_w_q_up"][0], a["mla_w_kv_up"][0]

            def up(b0, w, nk, width, k0, parts, targets, sq, name, g):
                ready = proj_rows(w, nk, width, k0=k0, parts=parts, b0=b0, free=m.get((name, g - 1)))

                @block.scalar
                def _(act):
                    act.wait_ge(a_used, ready)
                    for t in range(NT):
                        for h in range(2):
                            n = parts[h][1] - parts[h][0]
                            src = bank[b0 + 2 * t + h][:, 0:n].rearrange("p (h c) -> p h c", h=2)
                            two = slice(4 * g + 2 * h, 4 * g + 2 * h + 2)
                            act.activation(sq[0][:, t, two, :], src[:, :, 0:sq[1]], ACT.Square)
                            for dst, lo, hi in targets:
                                m[name, g] = done("act", act.activation(dst[:, t, two, :], src[:, :, lo:hi], ACT.Copy))

            def q_up(g):
                up(0, wq[:, g * 768:g * 768 + 768], 3, 768, 0, ((0, 384), (384, 768)),
                   ((qn, 0, NOPE), (qr, NOPE, QK)), (sqq, QK), "q", g)

            def kv_up(g):
                up(4, wkv[:, g * D:g * D + D], 2, D, 3, ((0, HALF), (HALF, D)),
                   ((kn, 0, NOPE), (vv, NOPE, 2 * NOPE)), (sqk, NOPE), "kv", g)

            hr = ROPE // 2

            def rotate(eng, z, out, cos, sin, w, last):
                t1, t2 = z[..., 0:hr], z[..., hr:ROPE]
                eng.tensor_tensor(w[0], t1, cos, ALU.mult)
                eng.tensor_tensor(w[1], t2, sin, ALU.mult)
                eng.tensor_tensor(w[2], t2, cos, ALU.mult)
                V(eng, eng.tensor_tensor(w[3], t1, sin, ALU.mult))
                eng.tensor_tensor(out[..., 0:hr], w[0], w[1], ALU.subtract)
                last(eng.tensor_tensor(out[..., hr:ROPE], w[2], w[3], ALU.add))

            def key_rotary():
                @block.vector
                def _(dve):
                    z = cp[:, :, 640:704]
                    dve.wait_ge(act_done, m["cs"])
                    sq = rot[:, 0, :, 0:2, :].rearrange("p t a c -> p t (a c)")
                    V(dve, dve.tensor_tensor(sq, z, z, ALU.mult))
                    V(dve, dve.tensor_reduce(small[:, 16:18], sq, AX.X, ALU.add))
                    V(dve, dve.tensor_tensor(z, z, rope_g[:, 1, :].unsqueeze(1).to_broadcast((P, NT, ROPE)), ALU.mult))
                    rotate(dve, z, krot[:, :, :], cs[:, 0, :, :], cs[:, 1, :, :], [rot[:, i, :, 0, :] for i in range(4)],
                           lambda ins: V(dve, ins))

            def norms(g):
                four = slice(4 * g, 4 * g + 4)

                @block.vector
                def _(dve):
                    z = qr[:, :, four, :]
                    dve.wait_ge(act_done, m["q", g])
                    V(dve, dve.tensor_reduce(stats[:, g, 0, :, :], sqq[:, :, four, :], AX.X, ALU.add))
                    V(dve, dve.tensor_tensor(z, z, rope_g[:, 0, :].unsqueeze(1).unsqueeze(1).to_broadcast((P, NT, 4, ROPE)), ALU.mult))
                    cos, sin = [cs[:, i, :, :].unsqueeze(2).to_broadcast((P, NT, 4, hr)) for i in range(2)]
                    rotate(dve, z, z, cos, sin, [rot[:, i, :, :, :] for i in range(4)], lambda ins: V(dve, ins))
                    m["rot", g] = chain["dve"]
                    dve.wait_ge(act_done, m["kv", g])
                    V(dve, dve.tensor_reduce(stats[:, g, 1, :, :], sqk[:, :, four, :], AX.X, ALU.add))
                    V(dve, dve.tensor_tensor(stats[:, g, 1, :, :], stats[:, g, 1, :, :],
                                             small[:, 16:18].unsqueeze(2).to_broadcast((P, NT, 4)), ALU.add))
                    m["hs", g] = done("dve", dve.tensor_scalar(stats[:, g, :, :, :], stats[:, g, :, :, :], 1.0 / QK, RMS_EPS,
                                                               ALU.mult, ALU.add))

                @block.gpsimd
                def _(pool):
                    flat16 = stats[:, g, :, :, :].rearrange("p a b c -> p (a b c)")
                    pool.wait_ge(dve_done, m["hs", g])
                    m["hr", g] = done("pool", pool.tensor_tensor(out=flat16, in0=flat16, in1=neg_half[:, 0:16], op=ALU.pow))

                @block.vector
                def _(dve):
                    dve.wait_ge(pool_done, m["hr", g])
                    rk = stats[:, g, 1, :, :].unsqueeze(3)
                    dve.tensor_scalar(exp_scale[:, g, :, :], stats[:, g, 0, :, :], QK ** -0.5, None, ALU.mult)
                    dve.tensor_scalar(neg_scale[:, g, :, :], stats[:, g, 0, :, :], -QK ** -0.5, None, ALU.mult)
                    dve.tensor_tensor(kr[:, :, four, :], krot[:, :, :].unsqueeze(2).to_broadcast((P, NT, 4, ROPE)),
                                      rk.to_broadcast((P, NT, 4, ROPE)), ALU.mult)
                    m["kn", g] = done("dve", dve.tensor_tensor(kn[:, :, four, :], kn[:, :, four, :],
                                                               rk.to_broadcast((P, NT, 4, NOPE)), ALU.mult))

            q_up(0)
            key_rotary()
            kv_up(0)
            q_up(1)
            norms(0)
            kv_up(1)
            norms(1)

            jobs = []

            def job(z, zT, h, gain, ready):
                if gain:
                    jobs.append((lambda t, e: z[:, t, h + e, :], zT[:, h:h + 2, :], gain, ready))
                else:
                    jobs.append((lambda t, e: z[:, t, 2 * (h + e):2 * (h + e) + 2, :].rearrange("p a b -> p (a b)"),
                                 zT[:, h:h + 2, :], None, ready))
            for h in range(0, H, 2):
                job(qn, qnT, h, "qn", None)
            for g in range(2):
                job(qr, qrT, 2 * g, None, m["rot", g])
            for g in range(2):
                job(kn, knT, 4 * g, "kn", m["kn", g])
                job(kn, knT, 4 * g + 2, "kn", m["kn", g])
                job(kr, krT, 2 * g, None, m["kn", g])
            pe0, act0 = chain["pe"], chain["act"]

            @block.tensor
            def _(pe):
                for n, (src, dst, gain, ready) in enumerate(jobs):
                    if n == 0:
                        pe.wait_ge(act_done, m["q", 1])
                    if ready:
                        pe.wait_ge(dve_done, ready)
                    if n >= 4:
                        pe.wait_ge(act_done, act0 + n - 3)
                    for e in range(2):
                        for t in range(NT):
                            ins = pe.transpose(bank[n % 4][:, e * T + t * P:e * T + t * P + P], src(t, e), ident[:, :])
                    done("pe", ins)

            @block.scalar
            def _(act):
                act.wait_ge(dve_done, m["hs", 1])
                for n, (src, dst, gain, ready) in enumerate(jobs):
                    act.wait_ge(pe_done, pe0 + n + 1)
                    done("act", act.activation(dst, bank[n % 4][:, :].rearrange("p (a t) -> p a t", a=2), ACT.Copy,
                                               scale=pc(gain) if gain else 1.0))
            end_phase()

            parts = ((slice(0, P), 0, 1), (slice(P, 3 * P), 1, 2))

            def scores(h):
                @block.tensor
                def _(pe):
                    if h >= 2:
                        pe.wait_ge(dve_done, m["max", h - 2])
                    b, q = bank[h % 2], slice(64 * (h % 2), 64 * (h % 2) + 64)
                    for cols, t, n in parts:
                        tok = slice(t * P, t * P + P)
                        pe.matmul(b[:, cols], qnT[:, h, tok], knT[:, h, 0:n * P], start=True, stop=False)
                        ins = pe.matmul(b[:, cols], qrT[q, h // 2, tok], krT[q, h // 2, 0:n * P], start=False, stop=True)
                    m["s", h] = done("pe", ins)

                @block.vector
                def _(dve):
                    if h == 0:
                        dve.wait_ge(pool_done, m["mask"])
                    dve.wait_ge(pe_done, m["s", h])
                    if h >= 3:
                        dve.wait_ge(pe_done, m["t", h - 3])
                    c = 32 + 8 * (h % 3)
                    for cols, t, n in parts:
                        m["max", h] = done("dve", dve.tensor_tensor_reduce(
                            out=pr[:, h % 3, cols], in0=bank[h % 2][:, cols], in1=mask[:, cols], scale=1.0, scalar=-3e38,
                            op0=ALU.add, op1=ALU.max, accum_out=small[:, c + t:c + t + 1]))
                    dve.wait_ge(dve_done, m["max", h])
                    m["nb", h] = done("dve", dve.tensor_tensor(small[:, c + 2:c + 4], small[:, c:c + 2],
                                                             neg_scale[:, h // 4, :, h % 4], ALU.mult))

                @block.scalar
                def _(act):
                    act.wait_ge(dve_done, m["nb", h])
                    c = 32 + 8 * (h % 3)
                    for cols, t, n in parts:
                        m["e", h] = done("act", act.activation(pr[:, h % 3, cols], pr[:, h % 3, cols], ACT.Exp,
                                                               scale=exp_scale[:, h // 4, t, h % 4:h % 4 + 1],
                                                               bias=small[:, c + 2 + t:c + 3 + t],
                                                               accum_out=small[:, c + 4 + t:c + 5 + t]))

                @block.vector
                def _(dve):
                    dve.wait_ge(act_done, m["e", h])
                    c = 32 + 8 * (h % 3)
                    V(dve, dve.reciprocal(small[:, c + 6:c + 8], small[:, c + 4:c + 6]))
                    for cols, t, n in parts:
                        m["p", h] = done("dve", dve.tensor_scalar(pr[:, h % 3, cols], pr[:, h % 3, cols],
                                                                  small[:, c + 6 + t:c + 7 + t], None, ALU.mult))

            def turn(h):
                @block.tensor
                def _(pe):
                    pe.wait_ge(dve_done, m["p", h])
                    if h >= 2:
                        pe.wait_ge(act_done, m["pt", h - 2])
                    for j in range(3):
                        ins = pe.transpose(bank[2 + h % 2][:, j * P:j * P + P], pr[:, h % 3, j * P:j * P + P], ident[:, :])
                    m["t", h] = done("pe", ins)

                @block.scalar
                def _(act):
                    act.wait_ge(pe_done, m["t", h])
                    if h >= 2:
                        act.wait_ge(pe_done, m["o", h - 2])
                    m["pt", h] = done("act", act.activation(prT[:, h % 2, :], bank[2 + h % 2][:, 0:3 * P], ACT.Copy))

            def values(h):
                @block.tensor
                def _(pe):
                    pe.wait_ge(act_done, m["pt", h])
                    if h >= 2:
                        pe.wait_ge(dve_done, m["lo", h - 2])
                    b = bank[4 + h % 2]
                    pe.matmul(b[:, 0:T], vv[:, 0, h, :], prT[:, h % 2, 0:T], start=True, stop=False)
                    m["o", h] = done("pe", pe.matmul(b[:, P:T], vv[:, 1, h, :], prT[:, h % 2, T:3 * P], start=False, stop=True))

                @block.scalar
                def _(act):
                    act.wait_ge(pe_done, m["o", h])
                    m["hi", h] = done("act", act.activation(act_hi[:, h, :], bank[4 + h % 2][:, 0:T], ACT.Copy))

                @block.vector
                def _(dve):
                    dve.wait_ge(act_done, m["hi", h])
                    m["lo", h] = done("dve", dve.tensor_tensor(act_lo[:, h, :], bank[4 + h % 2][:, 0:T],
                                                               act_hi[:, h, :].bitcast(F32), ALU.subtract))

            for i in range(H + 3):
                if i < H:
                    scores(i)
                if 2 <= i < H + 2:
                    turn(i - 2)
                if i >= 3:
                    values(i - 3)
            end_phase()
            out_proj(a["odd_w_out"][0], 1.0)

        nsa_loaded = sem("nsa_loaded")

        def nsa_weights():
            w1, bias8, w2 = piece(8192, 2, 16, P), piece(13408, 16, T), piece(17942, 2, 64)

            @block.gpsimd
            def _(pool):
                pool.wait_ge(bias_stored, 16)
                for i in range(2):
                    pool.dma_start(w1[:, i, :, :], a["nsa_cmp_w1_2"][0, i].rearrange("(j l) d e -> (l d) j e", l=2)
                                   ).then_inc(nsa_loaded, 16)
                    pool.dma_start(w2[:, i, :], a["nsa_cmp_w2_2"][0, i]).then_inc(nsa_loaded, 16)
                pool.dma_start(bias8[:, :, :], bass.AP(scratch, P - 1, [[512, P], [P * 512, 16], [1, T]])
                               ).then_inc(nsa_loaded, 16)

        def nsa():
            G4, HD, NQ, NCMP = 4, 64, 16, T // 16 - 1
            m = {}
            pT = piece(0, 16, T)
            kw = piece(4096, G4, T)
            ks = piece(5120, G4, NCMP + T)
            zp = piece(6204, 2, 16, G4 * NCMP)
            z = xn[:, :, :].rearrange("p b (g t) -> p b g t", g=G4)
            w1 = piece(8192, 2, 16, P)
            vt = piece(12288, 2, NT, T)
            gates = piece(13312, NT, 48)
            bias8 = piece(13408, NQ, T)
            hid = piece(17504, 2, G4 * NCMP)
            vc = piece(17684, T)
            hid_t = piece(18070, 2, P)
            w2 = piece(17942, 2, HD)
            prT = piece(6204, 2, 2, 512)
            pr = piece(9216, 3, 2, 512)
            w = a["nsa_w_in_2"][0]

            proj_T(lambda i, s, u: cols_dyn(w, i, s, u), 6, lambda i, s: pT[:, bass.ds(i * 4 + 2 * s, 2), :])
            c_ks, c_kw = 1536, 2048
            proj_T(lambda i, s, u: w[:, (c_ks, c_kw)[s] + u * P:(c_ks, c_kw)[s] + u * P + P].rearrange("(k p) n -> p k n", p=P),
                   2, lambda i, s: pT[:, 12 + 2 * s:14 + 2 * s, :])
            moved = npt[0] + 2

            @block.vector
            def _(dve):
                dve.wait_ge(pt_read, moved)
                dve.wait_ge(pool_done, x_free[0])
                for b in range(2):
                    for e in range(2):
                        src = pT[64 * e:64 * e + 64, 8 + 2 * b:10 + 2 * b, :]
                        dve.tensor_copy(z[0:64, b, e:G4:2, :], src)
                        m["z"] = done("dve", dve.tensor_copy(z[64:P, b, e:G4:2, 0:T - 1], src[:, :, 1:T]))

            ready = proj_rows(w[:, 1792:2608], KC, 816, parts=((0, 256), (512, 816)))

            @block.scalar
            def _(act):
                act.wait_ge(a_used, ready)
                for t in range(NT):
                    act.activation(vt[:, 0, t, :], bank[2 * t][:, 0:T], ACT.Copy)
                    act.activation(vt[:, 1, t, :], bank[2 * t + 1][:, 0:T], ACT.Copy)
                    m["g"] = done("act", act.activation(gates[:, t, :], bank[2 * t + 1][:, T:T + 48], ACT.Tanh, scale=0.5))

            @block.vector
            def _(dve):
                dve.wait_ge(act_done, m["g"])
                dve.tensor_scalar(gates[:, :, :], gates[:, :, :], 0.5, 0.5, ALU.mult, ALU.add)

            @block.scalar
            def _(act):
                for b in range(2):
                    for e in range(2):
                        src = pT[64 * e:64 * e + 64, 12 + 2 * b:14 + 2 * b, :]
                        for f in range(2):
                            dst = (ks[64 * f:64 * f + 64, e:G4:2, NCMP:NCMP + T], kw[64 * f:64 * f + 64, e:G4:2, :])[b]
                            act.activation(dst, src, ACT.Copy)

            @block.vector
            def _(dve):
                dve.wait_ge(dve_done, m["z"])
                for b in range(2):
                    for j in range(16):
                        ins = dve.tensor_scalar(zp[:, b, j, :].rearrange("p (g n) -> p g n", g=G4),
                                                z[:, b, :, 2 * j:2 * j + 16 * (NCMP - 1) + 1:16],
                                                pc("cmp_pos", 16 * b + j), None, ALU.add)
                    m["zp", b] = done("dve", ins)

            @block.tensor
            def _(pe):
                pe.wait_ge(nsa_loaded, 80)
                pe.wait_ge(pt_read, moved)
                for b in range(2):
                    pe.wait_ge(dve_done, m["zp", b])
                    for j in range(16):
                        ins = pe.matmul(bank[4 + b][0:G4 * NCMP, 0:P], zp[:, b, j, :], w1[:, b, j, :], start=(j == 0), stop=(j == 15))
                    m["hid", b] = done("pe", ins)

            @block.scalar
            def _(act):
                for b in range(2):
                    act.wait_ge(pe_done, m["hid", b])
                    m["hid_t", b] = done("act", act.activation(hid_t[0:G4 * NCMP, b, :], bank[4 + b][0:G4 * NCMP, 0:P], ACT.Copy))

            @block.tensor
            def _(pe):
                n = G4 * NCMP
                for b in range(2):
                    pe.wait_ge(act_done, m["hid_t", b])
                    m["turn", b] = done("pe", pe.transpose(bank[6 + b][:, 0:n], hid_t[0:n, b, :], ident[0:n, 0:n]))

            @block.scalar
            def _(act):
                for b in range(2):
                    act.wait_ge(pe_done, m["turn", b])
                    m["gelu"] = done("act", act.activation(hid[:, b, :], bank[6 + b][:, 0:G4 * NCMP], ACT.Gelu_apprx_tanh))

            @block.tensor
            def _(pe):
                pe.wait_ge(act_done, m["gelu"])
                for f in range(2):
                    pe.matmul(bank[3][64 * f:64 * f + 64, 0:G4 * NCMP], w2[:, 0, :], hid[:, 0, :], start=True, stop=True)
                for g in range(G4):
                    ins = pe.matmul(bank[4][0:NCMP, g * HD:g * HD + HD], hid[:, 1, g * NCMP:g * NCMP + NCMP], w2[:, 1, :],
                                    start=True, stop=True)
                m["kc"] = done("pe", ins)

            @block.scalar
            def _(act):
                act.wait_ge(pe_done, m["kc"])
                act.activation(ks[:, :, 0:NCMP], bank[3][:, 0:G4 * NCMP].rearrange("p (g n) -> p g n", g=G4), ACT.Copy)
                act.activation(vc[0:NCMP, :], bank[4][0:NCMP, 0:T], ACT.Copy)
            end_phase()

            scale = HD ** -0.5
            n0 = 7
            c0 = 3 * P
            full = ((slice(0, P), 0, slice(P, 2 * P)), (slice(P, 3 * P), 1, slice(0, 2 * P)))
            comp = ((slice(c0, c0 + n0), 0, slice(P + 31, T, 16), n0), (slice(c0 + n0, c0 + n0 + NCMP), 1, slice(31, T, 16), NCMP))
            s1 = NCMP + P
            sel_at = (slice(NCMP, s1), slice(s1 + NCMP, s1 + NCMP + T))
            comp_at = (slice(0, n0), slice(s1, s1 + NCMP))

            def rows(h):
                for t in range(NT):
                    cols, _, bcols = full[t]
                    ccols, _, cb, n = comp[t]
                    yield 3 * t + 0, 0, ccols, bias8[:, h, cb], comp_at[t]
                    yield 3 * t + 1, 0, cols, bias8[:, h, bcols], sel_at[t]
                    yield 3 * t + 2, 1, cols, bias8[:, h, bcols], cols

            def scores(h):
                g, q = h // 4, slice(64 * (h % 2), 64 * (h % 2) + 64)
                c = 64 + 32 * (h % 3)
                mx, nb, sm, co = (small[:, c + 6 * i:c + 6 * i + 6] for i in range(4))

                @block.tensor
                def _(pe):
                    if h >= 2:
                        pe.wait_ge(dve_done, m["max", h - 2])
                    for cols, t, _ in full:
                        query = pT[q, h // 2, t * P:t * P + P]
                        pe.matmul(bank[h % 2][:, t * s1:t * s1 + NCMP + t * P + P], query, ks[q, g, 0:NCMP + t * P + P],
                                  start=True, stop=True)
                        ins = pe.matmul(bank[2 + h % 2][:, cols], query, kw[q, g, 0:t * P + P], start=True, stop=True)
                    m["s", h] = done("pe", ins)

                @block.vector
                def _(dve):
                    dve.wait_ge(pe_done, m["s", h])
                    if h >= 3:
                        dve.wait_ge(pe_done, m["t", h - 3])
                    for i, b, cols, bias, at in rows(h):
                        m["max", h] = done("dve", dve.tensor_tensor_reduce(
                            out=pr[:, h % 3, b, cols], in0=bank[2 * b + h % 2][:, at], in1=bias, scale=1.0, scalar=-3e38,
                            op0=ALU.add, op1=ALU.max, accum_out=mx[:, i:i + 1]))
                    dve.wait_ge(dve_done, m["max", h])
                    m["nb", h] = done("dve", dve.tensor_scalar(nb, mx, -scale, None, ALU.mult))

                @block.scalar
                def _(act):
                    act.wait_ge(dve_done, m["nb", h])
                    for i, b, cols, bias, at in rows(h):
                        m["e", h] = done("act", act.activation(pr[:, h % 3, b, cols], pr[:, h % 3, b, cols], ACT.Exp, scale=scale,
                                                               bias=nb[:, i:i + 1], accum_out=sm[:, i:i + 1]))

                @block.vector
                def _(dve):
                    dve.wait_ge(act_done, m["e", h])
                    V(dve, dve.reciprocal(co, sm))
                    V(dve, dve.tensor_tensor(co.rearrange("p (t b) -> p t b", t=2), co.rearrange("p (t b) -> p t b", t=2),
                                             gates[:, :, 3 * h:3 * h + 3], ALU.mult))
                    V(dve, dve.tensor_scalar(co[:, 0:1], co[:, 0:1], seen[:, 0:1], None, ALU.mult))
                    for i, b, cols, bias, at in rows(h):
                        m["p", h] = done("dve", dve.tensor_scalar(pr[:, h % 3, b, cols], pr[:, h % 3, b, cols], co[:, i:i + 1], None, ALU.mult))

            def turn(h):
                @block.tensor
                def _(pe):
                    pe.wait_ge(dve_done, m["p", h])
                    if h >= 1:
                        pe.wait_ge(act_done, m["pt", h - 1])
                    for b in range(2):
                        for j in range(3):
                            pe.transpose(bank[4 + b][:, j * P:j * P + P], pr[:, h % 3, b, j * P:j * P + P], ident[:, :])
                    for cols, t, _, n in comp:
                        ins = pe.transpose(bank[4 + t][0:n, c0:c0 + P], pr[:, h % 3, 0, cols], ident[:, :])
                    m["t", h] = done("pe", ins)

                @block.scalar
                def _(act):
                    act.wait_ge(pe_done, m["t", h])
                    if h >= 2:
                        act.wait_ge(pe_done, m["o", h - 2])
                    for b, n in ((0, n0), (1, NCMP)):
                        act.activation(prT[:, h % 2, b, 0:c0], bank[4 + b][:, 0:c0], ACT.Copy)
                        m["pt", h] = done("act", act.activation(prT[0:n, h % 2, b, c0:c0 + P], bank[4 + b][0:n, c0:c0 + P], ACT.Copy))
                    act.wait_ge(act_done, m["pt", h])

            def values(h):
                g, q = h // 4, slice(64 * (h % 2), 64 * (h % 2) + 64)
                gv = slice(g * HD, g * HD + HD)

                @block.tensor
                def _(pe):
                    pe.wait_ge(act_done, m["pt", h])
                    if h >= 2:
                        pe.wait_ge(dve_done, m["lo", h - 2])
                    o = bank[6 + h % 2]
                    for b in range(2):
                        pe.matmul(o[q, 0:T], vt[:, b, 0, gv], prT[:, h % 2, b, 0:T], start=(b == 0), stop=False)
                        pe.matmul(o[q, P:T], vt[:, b, 1, gv], prT[:, h % 2, b, T:3 * P], start=False, stop=False)
                    for t, n in ((0, n0), (1, NCMP)):
                        ins = pe.matmul(o[q, t * P:t * P + P], vc[0:n, gv], prT[0:n, h % 2, t, c0:c0 + P], start=False, stop=(t == 1))
                    m["o", h] = done("pe", ins)

                @block.scalar
                def _(act):
                    act.wait_ge(pe_done, m["o", h])
                    m["hi", h] = done("act", act.activation(act_hi[q, h // 2, :], bank[6 + h % 2][q, 0:T], ACT.Copy))

                @block.vector
                def _(dve):
                    dve.wait_ge(act_done, m["hi", h])
                    m["lo", h] = done("dve", dve.tensor_tensor(act_lo[q, h // 2, :], bank[6 + h % 2][q, 0:T],
                                                               act_hi[q, h // 2, :].bitcast(F32), ALU.subtract))

            for i in range(NQ + 3):
                if i < NQ:
                    scores(i)
                if 2 <= i < NQ + 2:
                    turn(i - 2)
                if i >= 3:
                    values(i - 3)
            end_phase()
            out_proj(a["nsa_w_out_2"][0], 1.0 / ALPHA)
            layer_norm(0, 1)

        def hgrn():
            H = 8
            m = {}
            q = piece(0, H, T)
            k = piece(2048, H, T)
            f = piece(4096, H, T)
            gz = piece(6144, H, T)
            v = piece(8192, NT, D)
            at = piece(10240, H, 3, P)
            tot = [f.rearrange("p h t -> p (h t)"), piece(13312, 1024), piece(14336, 512), piece(14848, 256),
                   piece(15104, 128), piece(15232, 64), piece(15296, 32), piece(15328, 16)]
            lbc = small[:, 0:8]
            lbn = small[:, 8:16]
            w = a["hgrn_w_in_2"][0]

            @block.gpsimd
            def _(pool):
                m["zero"] = done("pool", pool.memset(at[:, :, :, :], 0.0))

            @block.vector
            def _(dve):
                t0, r0 = col_of["lb"]
                m["d"] = done("dve", dve.tensor_tensor(small[:, 16:24], pcol[:, t0, r0 + 8:r0 + 16], pcol[:, t0, r0:r0 + 8], ALU.subtract))

            @block.scalar
            def _(act):
                act.wait_ge(dve_done, m["d"])
                act.activation(lbc, small[:, 16:24], ACT.Sigmoid)
                act.activation(lbn, small[:, 16:24], ACT.Sigmoid, scale=-1.0)

            def gate_evac(act, i, s, src):
                two = bass.ds(i * 4 + 2 * s, 2)
                act.activation(f[:, two, :], src, ACT.Sigmoid)
                return act.activation(k[:, two, :], src, ACT.Sigmoid, scale=-1.0)

            proj_T(lambda i, s, u: cols_dyn(w, i, s, u, D), 4, None, evac=gate_evac)
            proj_T(lambda i, s, u: cols_dyn(w, i, s, u), 4, None,
                   evac=lambda act, i, s, src: act.activation(q[:, bass.ds(i * 4 + 2 * s, 2), :], src, ACT.Silu))
            proj_T(lambda i, s, u: cols_dyn(w, i, s, u, 3 * D), 4, None,
                   evac=lambda act, i, s, src: act.activation(gz[:, bass.ds(i * 4 + 2 * s, 2), :], src, ACT.Silu))
            ready = proj_rows(w[:, 2 * D:3 * D], KC, D)

            @block.scalar
            def _(act):
                act.wait_ge(a_used, ready)
                for t in range(NT):
                    for h in range(2):
                        act.activation(v[:, t, h * HALF:h * HALF + HALF], bank[2 * t + h][:, :], ACT.Copy)
            end_phase()

            @block.vector
            def _(dve):
                for h in range(H):
                    dve.tensor_scalar(f[:, h, :], f[:, h, :], lbn[:, h:h + 1], lbc[:, h:h + 1], ALU.mult, ALU.add)
                    done("dve", dve.tensor_scalar(k[:, h, :], k[:, h, :], lbn[:, h:h + 1], None, ALU.mult))
                m["fk"] = chain["dve"]

            hs = (slice(0, 4), slice(4, 8))
            for l in range(9):
                seg = 1 << max(l - 1, 0)

                @block.tensor
                def _(pe):
                    for g in range(2):
                        pe.wait_ge(dve_done, m["fk"] if l == 0 else m["up", l - 1, g])
                        if l >= 2:
                            pe.wait_ge(pool_done, m["upk", l - 1, g])
                        if l >= 2:
                            pe.wait_ge(dve_done, m["cp", l - 2, g])
                        b0 = 4 * (l % 2) + 2 * g
                        for j in range(4):
                            h = 4 * g + j
                            if l < 8:
                                for t in range(NT):
                                    tok = slice(t * P, t * P + P)
                                    ins = pe.matmul(bank[b0 + t][:, j * P:j * P + P], k[:, h, tok], q[:, h, tok], start=True, stop=True)
                            else:
                                ins = pe.matmul(bank[b0][:, j * P:j * P + P], k[:, h, 0:P], q[:, h, P:T], start=True, stop=True)
                        m["a", l, g] = done("pe", ins)

                def blocks(z, g):
                    return z[:, hs[g], :].rearrange("p h t -> p (h t)").rearrange("p (b e s) -> p b e s", e=2, s=seg)

                nb = 4 * T // (2 * seg)

                if 1 <= l < 8:
                    @block.gpsimd
                    def _(pool):
                        for g in range(2):
                            pool.wait_ge(pe_done, m["a", l, g])
                            if l == 1:
                                pool.wait_ge(dve_done, m["fk"])
                            tv = tot[l - 1][:, g * 2 * nb:(g + 1) * 2 * nb].rearrange("p (b e) -> p b e", e=2)
                            kv = blocks(k, g)
                            if l > 1:
                                pool.wait_ge(pool_done, m["tot", l - 1, g])
                            m["upk", l, g] = done("pool", pool.tensor_tensor(
                                out=kv[:, :, 0, :], in0=kv[:, :, 0, :], in1=tv[:, :, 1:2].to_broadcast((P, nb, seg)), op=ALU.mult))
                            m["tot", l, g] = done("pool", pool.tensor_tensor(
                                out=tot[l][:, g * nb:(g + 1) * nb], in0=tv[:, :, 0], in1=tv[:, :, 1], op=ALU.mult))

                @block.vector
                def _(dve):
                    if l == 0:
                        dve.wait_ge(dve_done, m["fk"])
                        dve.wait_ge(pool_done, m["zero"])
                    for g in range(2):
                        dve.wait_ge(pe_done, m["a", l, g])
                        if l == 0:
                            m["up", l, g] = done("dve", dve.tensor_tensor(q[:, hs[g], :], q[:, hs[g], :], f[:, hs[g], :], ALU.mult))
                        elif l < 8:
                            qv = blocks(q, g)
                            if l > 1:
                                dve.wait_ge(pool_done, m["tot", l - 1, g])
                            tv = tot[l - 1][:, g * 2 * nb:(g + 1) * 2 * nb].rearrange("p (b e) -> p b e", e=2)
                            left = tv[:, :, 0:1].to_broadcast((P, nb, seg))
                            m["up", l, g] = done("dve", dve.tensor_tensor(qv[:, :, 1, :], qv[:, :, 1, :], left, ALU.mult))
                        b0 = 4 * (l % 2) + 2 * g
                        mask = ident[:, :] if l == 0 else level[:, min(l - 1, 6), :]
                        if l < 8:
                            for t in range(NT):
                                m["cp", l, g] = done("dve", dve.copy_predicated(
                                    at[:, hs[g], 2 * t, :], mask.bitcast(U32).unsqueeze(1).to_broadcast((P, 4, P)),
                                    bank[b0 + t][:, :].rearrange("p (a b) -> p a b", a=4)))
                        else:
                            m["cp", l, g] = done("dve", dve.tensor_copy(at[:, hs[g], 1, :], bank[b0][:, :].rearrange("p (a b) -> p a b", a=4)))
                    dve.wait_ge(dve_done, m["cp", l, 1])
            end_phase()

            on, sq, og = piece(0, NT, D), piece(2048, NT, D), f
            ms, rh = small[:, 32:48], small[:, 48:64]
            by_half = [(t, hh) for t in range(NT) for hh in range(2)]

            def heads4(z, t, hh):
                return z[:, t, hh * HALF:hh * HALF + HALF].rearrange("p (h c) -> p h c", h=4)

            @block.tensor
            def _(pe):
                for t, hh in by_half:
                    for j in range(4):
                        h = 4 * hh + j
                        b = bank[2 * t + hh][:, j * P:j * P + P]
                        vh = slice(h * P, h * P + P)
                        ins = pe.matmul(b, at[:, h, t, :], v[:, 0, vh], start=True, stop=(t == 0))
                        if t == 1:
                            ins = pe.matmul(b, at[:, h, 2, :], v[:, 1, vh], start=False, stop=True)
                    m["o", t, hh] = done("pe", ins)

            @block.scalar
            def _(act):
                for t, hh in by_half:
                    act.wait_ge(pe_done, m["o", t, hh])
                    m["sq", t, hh] = done("act", act.activation(sq[:, t, hh * HALF:hh * HALF + HALF], bank[2 * t + hh][:, :], ACT.Square))

            for t in range(NT):
                @block.vector
                def _(dve):
                    for hh in range(2):
                        c = 8 * t + 4 * hh
                        dve.wait_ge(act_done, m["sq", t, hh])
                        V(dve, dve.tensor_reduce(ms[:, c:c + 4], heads4(sq, t, hh), AX.X, ALU.add))
                    m["ve", t] = done("dve", dve.tensor_scalar(ms[:, 8 * t:8 * t + 8], ms[:, 8 * t:8 * t + 8], 1.0 / P, RMS_EPS,
                                                               ALU.mult, ALU.add))

                @block.gpsimd
                def _(pool):
                    pool.wait_ge(dve_done, m["ve", t])
                    m["rh", t] = done("pool", pool.tensor_tensor(out=rh[:, 8 * t:8 * t + 8], in0=ms[:, 8 * t:8 * t + 8],
                                                                 in1=neg_half[:, 0:8], op=ALU.pow))

            @block.vector
            def _(dve):
                for t, hh in by_half:
                    c = 8 * t + 4 * hh
                    dve.wait_ge(pool_done, m["rh", t])
                    m["on", t] = done("dve", dve.tensor_tensor(
                        heads4(on, t, hh), bank[2 * t + hh][:, :].rearrange("p (h c) -> p h c", h=4),
                        rh[:, c:c + 4].unsqueeze(2).to_broadcast((P, 4, P)), ALU.mult))

            base = pe_transposes(lambda t, k: on[:, t, k * P:k * P + P], KC,
                                 waits=[[(dve_done, m["on", t])] for t in range(NT)])

            for i in range(4):
                pair = slice(2 * i, 2 * i + 2)

                @block.vector
                def _(dve):
                    dve.wait_ge(xpose_done, base + 2 * i + 2)
                    m["og", i] = done("dve", dve.scalar_tensor_tensor(flat(og[:, pair, :]), bank[4 + i][:, :], pc("hg"),
                                                                      flat(gz[:, pair, :]), ALU.mult, ALU.mult))

                @block.scalar
                def _(act):
                    act.wait_ge(dve_done, m["og", i])
                    m["hi", i] = done("act", act.activation(act_hi[:, pair, :], og[:, pair, :], ACT.Copy))

            @block.vector
            def _(dve):
                for i in range(4):
                    pair = slice(2 * i, 2 * i + 2)
                    dve.wait_ge(act_done, m["hi", i])
                    dve.tensor_tensor(act_lo[:, pair, :], og[:, pair, :], act_hi[:, pair, :].bitcast(F32), ALU.subtract
                                      ).then_inc(xlo_done, 2)
            out_proj(a["hgrn_w_out_2"][0], 1.0 / ALPHA)
            layer_norm(1, 1)
        def half_block(layer, which):
            w = (layer, which)
            rms_norm_to_act(layer, 2 * which)
            ffn(a["ffn_w_gate"][w], a["ffn_w_up"][w], a["ffn_w_down"][w], 0.5)

        def second_ffn(n, layer, norm, last=False):
            ffn(a[f"ffn{n}_w_gate_2"][layer], a[f"ffn{n}_w_up_2"][layer], a[f"ffn{n}_w_down_2"][layer],
                0.5 / ALPHA, last_ffn=last)
            layer_norm(layer, norm, last)

        half_block(0, 0)
        rms_norm_to_act(0, 1, barrier=True)
        conv_rwkv()
        half_block(0, 1)
        half_block(1, 0)
        rms_norm_to_act(1, 1, barrier=True)
        mla()
        nsa_weights()
        half_block(1, 1)
        transpose_split(lambda t, k: x[:, t, k * P:k * P + P], None, barrier=False,
                        waits=[[(dve_done, n)] for n in x_ready])
        second_ffn(1, 0, 0)
        nsa()
        second_ffn(2, 0, 2)
        second_ffn(1, 1, 0)
        hgrn()
        second_ffn(2, 1, 2, last=True)

        @block.sync
        def _(sp):
            sp.wait_ge(phase_done, 4 * nphase[0])
            sp.dma_start(out[0].rearrange("(t p) d -> p t d", p=P), x[:, :, :]).then_inc(out_stored, 16)
            sp.wait_ge(out_stored, 16)
            sp.wait_ge(bias_stored, 16)


def constants():
    c = {"c_ident": np.eye(P, dtype=np.float32)}
    c["c_inv_freq"] = (10000.0 ** (-np.arange(0, 64, 2) / 64.0)).astype(np.float32)[None, :]
    i = np.arange(P)
    f = np.float32
    c["c_block_ones"] = (i[:, None] // 64 == i[None, :] // 64).astype(f)
    level = np.stack([(i[:, None] >> (l + 1) == i[None, :] >> (l + 1)) & ((i[:, None] >> l) % 2 == 0)
                      & ((i[None, :] >> l) % 2 == 1) for l in range(7)], 1)
    c["c_level"] = level.astype(f)
    c["c_level0_t"] = np.ascontiguousarray(level[:, 0].T).astype(f)
    c["c_upper"] = np.stack([i[:, None] < i[None, :], i[:, None] <= i[None, :]], 1).astype(f)
    c["c_seen"] = (i >= 31).astype(f)[:, None]
    dist = 255 - np.arange(384)
    n = np.maximum(dist, 1)
    large = 16 + np.floor(np.log(n / 16.0) / math.log(8.0) * 16 + 1e-9).astype(int)
    bucket = np.where(dist < 16, dist, np.minimum(large, 31))
    bucket = np.where(dist < 0, 32, bucket)
    c["c_onehot"] = (np.arange(33)[:, None] == bucket[None, :]).astype(f)
    return c


def kernel(**inputs):
    import concourse.bacc as bacc
    from concourse.bass_utils import run_bass_kernel_spmd

    nc = bacc.Bacc("TRN2", target_bir_lowering=False, num_devices=1)
    arrays, args = {}, {}
    for name, value in list(inputs.items()) + list(constants().items()):
        if name in UNUSED:
            continue
        arrays[f"in_{name}"] = v = np.ascontiguousarray(value)
        args[name] = nc.dram_tensor(f"in_{name}", v.shape, mybir.dt.from_np(v.dtype), kind="ExternalInput").ap()
    out = nc.dram_tensor("out_x", (1, T, D), F32, kind="ExternalOutput").ap()
    build_program(nc, args, out)
    r = run_bass_kernel_spmd(nc, [arrays], core_ids=[0])
    return r.results[0]["out_x"]
```
